# Optimizing a Trainium2 kernel written in Bass

```python
import jax, jax.numpy as jnp
from jax import lax
import numpy as np

D_MODEL = 1024
BATCH = 1
SEQ = 1024
DEPTH = 2

N_MIXERS = 2
N_SB = (DEPTH + 1) // 2
N_MLA = DEPTH // 2
HEAD_DIM = 64
N_SB_HEADS = 12
N_MLA_HEADS = 12
MLA_Q_RANK = 768
MLA_KV_RANK = 256
MLA_NOPE = 64
MLA_ROPE = 32
MLA_QK = MLA_NOPE + MLA_ROPE
MLA_V = 64
N_MEM = 256
N_MEM_HEADS = 4
MEM_HEAD_DIM = 64
MEM_Q = N_MEM_HEADS * MEM_HEAD_DIM
MIX_WIDTH = N_SB_HEADS * HEAD_DIM + MEM_Q
SB_IN = 3 * N_SB_HEADS * HEAD_DIM + MEM_Q
MLA_IN = MLA_Q_RANK + MLA_KV_RANK + MLA_ROPE + MEM_Q
D_FF = -(-8 * D_MODEL // (3 * 256)) * 256
Q_BLOCK = 128
ROPE_THETA = 10000.0
EPS = 1e-6

kernel_name = "hybrid_stickbreak_mla_memory_swiglu"

def _rms(x, g):
    x32 = x.astype(jnp.float32)
    y = x32 * lax.rsqrt(jnp.mean(x32 * x32, axis=-1, keepdims=True) + EPS)
    return (y * g.astype(jnp.float32)).astype(x.dtype)

def _rope(x, positions):
    half = x.shape[-1] // 2
    inv_freq = ROPE_THETA ** (-jnp.arange(half, dtype=jnp.float32) / half)
    ang = positions.astype(jnp.float32)[:, :, None, None] * inv_freq
    cos, sin = jnp.cos(ang), jnp.sin(ang)
    x32 = x.astype(jnp.float32)
    x1, x2 = x32[..., :half], x32[..., half:]
    return jnp.concatenate([x1 * cos - x2 * sin, x2 * cos + x1 * sin], axis=-1).astype(x.dtype)

def _sweep_query_blocks(block_fn, q):
    b, h, s, d = q.shape
    nb = s // Q_BLOCK
    qb = jnp.moveaxis(q.reshape(b, h, nb, Q_BLOCK, d), 2, 0)
    out = lax.map(lambda a: block_fn(a[0], a[1]), (qb, jnp.arange(nb)))
    return jnp.moveaxis(out, 0, 2).reshape(b, h, s, out.shape[-1])

def _stick_breaking(q, k, v):
    s_len = k.shape[2]
    scale = q.shape[-1] ** -0.5
    key_pos = jnp.arange(s_len)[None, :]

    def block(q_blk, blk):
        z = jnp.einsum('bhqd,bhkd->bhqk', q_blk, k).astype(jnp.float32) * scale
        q_pos = blk * Q_BLOCK + jnp.arange(Q_BLOCK)[:, None]
        strict = key_pos < q_pos
        log_fail = jnp.where(strict, jax.nn.log_sigmoid(-z), 0.0)
        after = lax.cumsum(log_fail, axis=3, reverse=True) - log_fail
        w = jnp.where(strict, jnp.exp(jax.nn.log_sigmoid(z) + after), 0.0)
        return jnp.einsum('bhqk,bhkd->bhqd', w.astype(v.dtype), v)

    return _sweep_query_blocks(block, q)

def _causal_softmax_attn(q, k, v):
    s_len = k.shape[2]
    scale = q.shape[-1] ** -0.5
    key_pos = jnp.arange(s_len)[None, :]

    def block(q_blk, blk):
        sc = jnp.einsum('bhqd,bhkd->bhqk', q_blk, k).astype(jnp.float32) * scale
        q_pos = blk * Q_BLOCK + jnp.arange(Q_BLOCK)[:, None]
        sc = jnp.where(key_pos <= q_pos, sc, -jnp.inf)
        p = jax.nn.softmax(sc, axis=-1)
        return jnp.einsum('bhqk,bhkd->bhqd', p.astype(v.dtype), v)

    return _sweep_query_blocks(block, q)

def _memory_heads(q_flat, mem, ln_g, w_kv, g_qn, g_kn):
    b, s, _ = q_flat.shape
    q = _rms(q_flat.reshape(b, s, N_MEM_HEADS, MEM_HEAD_DIM), g_qn)
    kv = (_rms(mem, ln_g) @ w_kv).reshape(b, mem.shape[1], N_MEM_HEADS, 2 * MEM_HEAD_DIM)
    k = _rms(kv[..., :MEM_HEAD_DIM], g_kn)
    v = kv[..., MEM_HEAD_DIM:]
    sc = jnp.einsum('bqhd,bkhd->bhqk', q, k).astype(jnp.float32) * (MEM_HEAD_DIM ** -0.5)
    p = jax.nn.softmax(sc, axis=-1)
    o = jnp.einsum('bhqk,bkhd->bqhd', p.astype(v.dtype), v)
    return o.reshape(b, s, MEM_Q)

def _heads_first(t, n_heads):
    b, s, _ = t.shape
    return t.reshape(b, s, n_heads, -1).transpose(0, 2, 1, 3)

def setup_inputs(seed: int = 0) -> dict:
    key = jax.random.key(seed)
    ks = iter(jax.random.split(key, 32))

    def w(shape, fan_in, extra=1.0):
        return jax.random.normal(next(ks), shape, jnp.float32) * (fan_in ** -0.5) * extra

    def gain(shape):
        return 1.0 + 0.05 * jax.random.normal(next(ks), shape, jnp.float32)

    res_scale = (2.0 * DEPTH) ** -0.5
    x = jax.random.normal(next(ks), (BATCH, SEQ, D_MODEL), jnp.float32)
    mem = jax.random.normal(next(ks), (BATCH, N_MEM, D_MODEL), jnp.float32)
    offset = jax.random.randint(next(ks), (BATCH, 1), 0, 1024, dtype=jnp.int32)
    positions = offset + jnp.arange(SEQ, dtype=jnp.int32)[None, :]
    return {
        "x": x,
        "mem": mem,
        "positions": positions,
        "ln_attn": gain((DEPTH, D_MODEL)),
        "w_out": w((DEPTH, MIX_WIDTH, D_MODEL), MIX_WIDTH, res_scale),
        "ln_mem": gain((DEPTH, D_MODEL)),
        "w_mem_kv": w((DEPTH, D_MODEL, 2 * MEM_Q), D_MODEL),
        "g_qn_mem": gain((DEPTH, MEM_HEAD_DIM)),
        "g_kn_mem": gain((DEPTH, MEM_HEAD_DIM)),
        "ln_ffn": gain((DEPTH, D_MODEL)),
        "w_ffn_gu": w((DEPTH, D_MODEL, 2 * D_FF), D_MODEL),
        "w_ffn_down": w((DEPTH, D_FF, D_MODEL), D_FF, res_scale),
        "sb_w_in": w((N_SB, D_MODEL, SB_IN), D_MODEL),
        "mla_w_in": w((N_MLA, D_MODEL, MLA_IN), D_MODEL),
        "mla_q_norm": gain((N_MLA, MLA_Q_RANK)),
        "mla_w_q_up": w((N_MLA, MLA_Q_RANK, N_MLA_HEADS * MLA_QK), MLA_Q_RANK),
        "mla_kv_norm": gain((N_MLA, MLA_KV_RANK)),
        "mla_w_kv_up": w((N_MLA, MLA_KV_RANK, N_MLA_HEADS * (MLA_NOPE + MLA_V)), MLA_KV_RANK),
        "mla_g_qn": gain((N_MLA, MLA_QK)),
        "mla_g_kn": gain((N_MLA, MLA_QK)),
    }

def reference(x, mem, positions, ln_attn, w_out, ln_mem, w_mem_kv, g_qn_mem, g_kn_mem,
              ln_ffn, w_ffn_gu, w_ffn_down, sb_w_in, mla_w_in, mla_q_norm, mla_w_q_up,
              mla_kv_norm, mla_w_kv_up, mla_g_qn, mla_g_kn):
    b, s, _ = x.shape
    for i in range(DEPTH):
        h = _rms(x, ln_attn[i])
        j = i // N_MIXERS
        if i % N_MIXERS == 0:
            proj = h @ sb_w_in[j]
            wq = N_SB_HEADS * HEAD_DIM
            q = _heads_first(proj[..., :wq], N_SB_HEADS)
            k = _heads_first(proj[..., wq:2 * wq], N_SB_HEADS)
            v = _heads_first(proj[..., 2 * wq:3 * wq], N_SB_HEADS)
            q_mem = proj[..., 3 * wq:]
            o = _stick_breaking(q, k, v)
        else:
            proj = h @ mla_w_in[j]
            c_q = proj[..., :MLA_Q_RANK]
            c_kv = proj[..., MLA_Q_RANK:MLA_Q_RANK + MLA_KV_RANK]
            k_rope = proj[..., MLA_Q_RANK + MLA_KV_RANK:MLA_Q_RANK + MLA_KV_RANK + MLA_ROPE]
            q_mem = proj[..., MLA_Q_RANK + MLA_KV_RANK + MLA_ROPE:]
            q = (_rms(c_q, mla_q_norm[j]) @ mla_w_q_up[j]).reshape(b, s, N_MLA_HEADS, MLA_QK)
            kv = (_rms(c_kv, mla_kv_norm[j]) @ mla_w_kv_up[j]).reshape(
                b, s, N_MLA_HEADS, MLA_NOPE + MLA_V)
            k_rope_h = jnp.broadcast_to(k_rope[:, :, None, :], (b, s, N_MLA_HEADS, MLA_ROPE))
            k = jnp.concatenate([kv[..., :MLA_NOPE], k_rope_h], axis=-1)
            v = kv[..., MLA_NOPE:]
            q = _rms(q, mla_g_qn[j])
            k = _rms(k, mla_g_kn[j])
            q = jnp.concatenate([q[..., :MLA_NOPE], _rope(q[..., MLA_NOPE:], positions)], -1)
            k = jnp.concatenate([k[..., :MLA_NOPE], _rope(k[..., MLA_NOPE:], positions)], -1)
            o = _causal_softmax_attn(q.transpose(0, 2, 1, 3), k.transpose(0, 2, 1, 3),
                                     v.transpose(0, 2, 1, 3))
        mixer_out = o.transpose(0, 2, 1, 3).reshape(b, s, -1)
        mem_out = _memory_heads(q_mem, mem, ln_mem[i], w_mem_kv[i], g_qn_mem[i], g_kn_mem[i])
        x = x + jnp.concatenate([mixer_out, mem_out], axis=-1) @ w_out[i]
        gu = _rms(x, ln_ffn[i]) @ w_ffn_gu[i]
        x = x + (jax.nn.silu(gu[..., :D_FF]) * gu[..., D_FF:]) @ w_ffn_down[i]
    return x


_drawn_inputs = setup_inputs


def setup_inputs(seed=0):
    import zlib

    import numpy as np

    out = dict(_drawn_inputs(seed))
    spreads = {}
    factors = {'ln_attn': 3.249,
     'ln_mem': 8.0,
     'g_qn_mem': 8.0,
     'g_kn_mem': 8.0,
     'mla_q_norm': 8.0,
     'mla_kv_norm': 8.0,
     'mla_g_qn': 8.0,
     'mla_g_kn': 8.0}
    for name, (base, spread) in spreads.items():
        noise = np.random.default_rng([zlib.crc32(name.encode()), seed]).standard_normal(out[name].shape)
        drawn = base * np.exp(spread * noise) if base else spread * noise
        out[name] = __import__('jax').numpy.asarray(drawn.astype(out[name].dtype))
    for name, factor in factors.items():
        out[name] = (out[name] * factor).astype(out[name].dtype)
    return out
```

```python
from contextlib import ExitStack

import concourse.bass as bass
import numpy as np
from concourse import mybir

P = 128
F32 = mybir.dt.float32
F32R = mybir.dt.float32r
I32 = mybir.dt.int32
ALU = mybir.AluOpType
ACT = mybir.ActivationFunctionType
AX = mybir.AxisListType.X

D = 1024
S = 1024
ND, NS = D // P, S // P
HALF = 512
DEPTH = 2
HD = 64
HEADS = 12
PAIRS = HEADS // 2
NOPE, ROPE = 64, 32
QK = NOPE + ROPE
Q_RANK, KV_RANK = 768, 256
MEM, MEM_HEADS = 256, 4
MEM_Q = MEM_HEADS * HD
FF = 2816
NF = FF // P
SB_Q = HEADS * HD
EPS = 1e-6
THETA = 10000.0
MASKED = -1e30

BASE = 16512
HT_AT = BASE
CONST_AT = HT_AT + 2 * ND * S * 4
WORK_AT = CONST_AT + 5 * 1024
X_AT = 229344 - NS * D * 4


class Memory:

    def __init__(self, nc, at, end):
        self.nc, self.at, self.end = nc, at, end

    def __call__(self, name, shape, dtype=F32):
        size = int(np.prod(shape[1:])) * 4
        t = self.nc.alloc_sbuf_tensor_at(name, shape, dtype, offset=self.at)
        self.at += (size + 31) // 32 * 32
        assert self.at <= self.end, (name, self.at, self.end)
        return t


class Phase(ExitStack):

    def __init__(self, nc):
        super().__init__()
        self.nc, self.semaphores = nc, []

    def semaphore(self, name):
        self.semaphores.append(self.nc.alloc_semaphore(name))
        return self.semaphores[-1]

    def __exit__(self, *exc):
        super().__exit__(*exc)
        if exc[0] is None:
            self.nc.clear_and_free_semaphores(self.semaphores)
            self.nc.all_engine_barrier()


def as_f32(ap):
    return ap.bitcast(F32)


def product3(pe, out, l_hi, l_lo, r_hi, r_lo, first, last):
    pe.matmul(out, l_hi, r_hi, start=first, stop=False, skip_group_check=True)
    pe.matmul(out, l_hi, r_lo, start=False, stop=False, skip_group_check=True)
    return pe.matmul(out, l_lo, r_hi, start=False, stop=last, skip_group_check=True)


def make_constants(nc, k):
    with Phase(nc) as ctx:
        made = ctx.semaphore("const_made")
        filled = ctx.semaphore("const_filled")
        t = [k["ident"], k["tmp_strict"], k["tmp_causal"], k["tmp_upper"], k["tmp_lower"]]
        block = ctx.enter_context(nc.Block())

        @block.gpsimd
        def _(pool):
            for m, v in zip(t, (0.0, 0.0, 0.0, -1.0, -1.0)):
                pool.memset(m[:], v).then_inc(filled, 1)
            pool.wait_ge(filled, 5)
            pool.affine_select(out=t[0][:], in_=t[0][:], compare_op=ALU.not_equal, fill=1.0, base=0,
                               pattern=[[-1, P]], channel_multiplier=1).then_inc(made, 1)
            pool.affine_select(out=t[1][:], in_=t[1][:], compare_op=ALU.is_gt, fill=MASKED, base=0,
                               pattern=[[1, P]], channel_multiplier=-1).then_inc(made, 1)
            pool.affine_select(out=t[2][:], in_=t[2][:], compare_op=ALU.is_ge, fill=MASKED, base=0,
                               pattern=[[-1, P]], channel_multiplier=1).then_inc(made, 1)
            pool.affine_select(out=t[3][:], in_=t[3][:], compare_op=ALU.is_ge, fill=0.0, base=0,
                               pattern=[[-1, P]], channel_multiplier=1).then_inc(made, 1)
            pool.affine_select(out=t[4][:], in_=t[4][:], compare_op=ALU.is_gt, fill=0.0, base=0,
                               pattern=[[1, P]], channel_multiplier=-1).then_inc(made, 1)

        @block.vector
        def _(dve):
            dve.wait_ge(made, 5)
            dve.memset(k["eps"][:], EPS)
            for name, src in (("ident_r", t[0]), ("strict", t[1]), ("causal", t[2]),
                              ("upper", t[3]), ("lower", t[4])):
                dve.tensor_copy(k[name][:], src[:])


def gain_columns(gain):
    return gain.rearrange("(c p) -> p c", p=P)


def norm_transposed(nc, tag, k, x, x_dram, gain, ht, psum, save_to=None):
    nt = x.shape[1]
    mem = Memory(nc, WORK_AT, X_AT)
    xn = mem(f"{tag}_xn", [P, nt, D])
    junk = mem(f"{tag}_junk", [P, D])
    ss = mem(f"{tag}_ss", [P, nt])
    std = mem(f"{tag}_std", [P, nt])
    rstd = mem(f"{tag}_rstd", [P, nt])
    gcol = mem(f"{tag}_gcol", [P, ND])
    group = min(nt, 4)
    banks = [(g, c) for g in range(nt // group) for c in range(ND)]
    with Phase(nc) as ctx:
        sem = lambda n: ctx.semaphore(f"{tag}_{n}")
        x_in = [sem(f"x_in{i}") for i in range(nt)] if x_dram is not None else None
        g_in, squared, root, scale_ready = sem("g_in"), sem("squared"), sem("root"), sem("scale_ready")
        normed, turned, hi_done, lo_done, saved = (
            sem("normed"), sem("turned"), sem("hi_done"), sem("lo_done"), sem("saved"))
        block = ctx.enter_context(nc.Block())

        @block.sync
        def _(sp):
            if x_dram is not None:
                for t in range(nt):
                    sp.dma_start(x[:, t, :], x_dram[t * P:(t + 1) * P, :]).then_inc(x_in[t], 16)
            with nc.allow_non_contiguous_dma("gain"):
                sp.dma_start(gcol[:], gain_columns(gain)).then_inc(g_in, 16)
            if save_to is not None:
                for t in range(nt):
                    sp.dma_start(save_to[t * P:(t + 1) * P, :], x[:, t, :]).then_inc(saved, 16)
                sp.wait_ge(saved, 16 * nt)

        @block.scalar
        def _(act):
            for t in range(nt):
                if x_dram is not None:
                    act.wait_ge(x_in[t], 16)
                if t:
                    act.wait_ge(squared, t)
                act.activation(junk[:], x[:, t, :], ACT.Square, accum_out=ss[:, t:t + 1]).then_inc(squared, 1)
            act.wait_ge(squared, nt)
            act.activation(std[:], ss[:], ACT.Sqrt, bias=k["eps"][:, 0:1], scale=1.0 / D).then_inc(root, 1)
            act.wait_ge(g_in, 16)
            for n, (g, c) in enumerate(banks):
                act.wait_ge(turned, n + 1)
                cols = slice(g * group * P, (g + 1) * group * P)
                act.activation(ht["hi"][:, c, cols], psum[n % 4][:, 0:group * P], ACT.Copy,
                               scale=gcol[:, c:c + 1]).then_inc(hi_done, 1)

        @block.vector
        def _(dve):
            dve.wait_ge(root, 1)
            dve.reciprocal(rstd[:], std[:]).then_inc(scale_ready, 1)
            dve.wait_ge(scale_ready, 1)
            for t in range(nt):
                dve.tensor_scalar(xn[:, t, :], x[:, t, :], rstd[:, t:t + 1], None, ALU.mult).then_inc(normed, 1)
            for n, (g, c) in enumerate(banks):
                dve.wait_ge(hi_done, n + 1)
                cols = slice(g * group * P, (g + 1) * group * P)
                dve.scalar_tensor_tensor(ht["lo"][:, c, cols], psum[n % 4][:, 0:group * P], gcol[:, c:c + 1],
                                         as_f32(ht["hi"][:, c, cols]), ALU.mult, ALU.subtract).then_inc(lo_done, 1)

        @block.tensor
        def _(pe):
            for n, (g, c) in enumerate(banks):
                pe.wait_ge(normed, (g + 1) * group)
                if n >= 4:
                    pe.wait_ge(lo_done, n - 3)
                for i in range(group):
                    last = pe.transpose(psum[n % 4][:, i * P:(i + 1) * P],
                                        xn[:, g * group + i, c * P:(c + 1) * P], k["ident"][:])
                last.then_inc(turned, 1)


def swiglu(nc, tag, k, x, ht, w_gu, w_down, psum, store_to=None):
    mem = Memory(nc, WORK_AT, X_AT)
    gu_raw = [mem(f"{tag}_gu_raw{s}", [P, ND, 2, P]) for s in range(2)]
    gu_hi = [mem(f"{tag}_gu_hi{s}", [P, ND, 2, P], F32R) for s in range(2)]
    gu_lo = [mem(f"{tag}_gu_lo{s}", [P, ND, 2, P], F32R) for s in range(2)]
    dn_raw = [mem(f"{tag}_dn_raw{s}", [P, D]) for s in range(2)]
    dn_hi = [mem(f"{tag}_dn_hi{s}", [P, D], F32R) for s in range(2)]
    dn_lo = [mem(f"{tag}_dn_lo{s}", [P, D], F32R) for s in range(2)]
    a_hi = [mem(f"{tag}_a_hi{s}", [P, S], F32R) for s in range(2)]
    a_lo = [mem(f"{tag}_a_lo{s}", [P, S], F32R) for s in range(2)]
    gate = mem(f"{tag}_gate", [P, 2, HALF])
    hidden = mem(f"{tag}_hidden", [P, 2, HALF])
    gu_rows = w_gu.rearrange("(c p) f -> p c f", p=P)
    outs = [(t, n) for t in range(NS) for n in range(D // HALF)]
    NOUT = len(outs)
    with Phase(nc) as ctx:
        sem = lambda n: ctx.semaphore(f"{tag}_{n}")
        gu_in = [sem(f"gu_in{s}") for s in range(2)]
        dn_in = [sem(f"dn_in{s}") for s in range(2)]
        gu_hi_done, gu_lo_done, dn_hi_done, dn_lo_done = (
            sem("gu_hi_done"), sem("gu_lo_done"), sem("dn_hi_done"), sem("dn_lo_done"))
        gu_made, silu_done, hid_done, a_hi_done, a_lo_done, dn_made, added, stored = (
            sem("gu_made"), sem("silu_done"), sem("hid_done"), sem("a_hi_done"), sem("a_lo_done"),
            sem("dn_made"), sem("added"), sem("stored"))
        block = ctx.enter_context(nc.Block())

        def chunks(eng, step):
            for s in range(2):
                step(0, s, True, False)
            with eng.Fori(1, NF // 2 - 1) as i:
                for s in range(2):
                    step(i, s, False, False)
            for s in range(2):
                step(NF // 2 - 1, s, False, s == 1)

        def following(i, s):
            return (i, 1) if s == 0 else (i + 1, 0)

        @block.sync
        def _(sp):
            def load(i, s):
                for half in range(2):
                    sp.dma_start(gu_raw[s][:, :, half, :],
                                 gu_rows[:, :, bass.ds((2 * i + s) * P + half * FF, P)]).then_inc(gu_in[s], 16)
                sp.dma_start(dn_raw[s][:], w_down[bass.ds((2 * i + s) * P, P), :]).then_inc(dn_in[s], 16)

            for s in range(2):
                load(0, s)
            with sp.Fori(1, NF // 2) as i:
                for s in range(2):
                    sp.wait_ge(gu_lo_done, 2 * i + s - 1)
                    sp.wait_ge(dn_lo_done, 2 * i + s - 1)
                    load(i, s)
            if store_to is not None:
                for t in range(NS):
                    sp.wait_ge(added, (NF - 1) * NOUT + 2 * (t + 1))
                    sp.dma_start(store_to[t * P:(t + 1) * P, :], x[:, t, :]).then_inc(stored, 16)
                sp.wait_ge(stored, 16 * NS)

        @block.gpsimd
        def _(pool):
            def lower_gu(i, s):
                pool.wait_ge(gu_hi_done, 2 * i + s + 1)
                pool.tensor_tensor(gu_lo[s][:], gu_raw[s][:], as_f32(gu_hi[s][:]),
                                   ALU.subtract).then_inc(gu_lo_done, 1)

            def step(i, s, first, last):
                pool.wait_ge(dn_hi_done, 2 * i + s + 1)
                pool.tensor_tensor(dn_lo[s][:], dn_raw[s][:], as_f32(dn_hi[s][:]),
                                   ALU.subtract).then_inc(dn_lo_done, 1)
                if not last:
                    lower_gu(*following(i, s))

            lower_gu(0, 0)
            chunks(pool, step)

        @block.scalar
        def _(act):
            def upper_gu(i, s, first):
                act.wait_ge(gu_in[s], 32 * (i + 1))
                if not first:
                    act.wait_ge(gu_made, 4 * (2 * i + s - 1))
                act.activation(gu_hi[s][:], gu_raw[s][:], ACT.Copy).then_inc(gu_hi_done, 1)

            def step(i, s, first, last):
                f = 2 * i + s
                act.wait_ge(dn_in[s], 16 * (i + 1))
                if not first:
                    act.wait_ge(dn_made, NOUT * (f - 1))
                act.activation(dn_hi[s][:], dn_raw[s][:], ACT.Copy).then_inc(dn_hi_done, 1)
                if not last:
                    upper_gu(*following(i, s), first and s == 0)
                for h in range(2):
                    act.wait_ge(gu_made, 4 * f + 2 * h + 1)
                    if not first or s:
                        act.wait_ge(hid_done, 2 * f + h - 1)
                    act.activation(gate[:, h, :], psum[2 * h][:], ACT.Silu).then_inc(silu_done, 1)
                    act.wait_ge(hid_done, 2 * f + h + 1)
                    act.activation(a_hi[s][:, h * HALF:(h + 1) * HALF], hidden[:, h, :],
                                   ACT.Copy).then_inc(a_hi_done, 1)

            upper_gu(0, 0, True)
            chunks(act, step)

        @block.vector
        def _(dve):
            def add(f):
                for n, (t, half) in enumerate(outs):
                    dve.wait_ge(dn_made, NOUT * f + n + 1)
                    cols = slice(half * HALF, (half + 1) * HALF)
                    dve.tensor_tensor(x[:, t, cols], psum[4 + n % 4][:], x[:, t, cols], ALU.add).then_inc(added, 1)

            def step(i, s, first, last):
                f = 2 * i + s
                for h in range(2):
                    dve.wait_ge(silu_done, 2 * f + h + 1)
                    dve.wait_ge(gu_made, 4 * f + 2 * h + 2)
                    if not first or s:
                        dve.wait_ge(a_lo_done, 2 * f + h - 1)
                    dve.tensor_tensor(hidden[:, h, :], psum[2 * h + 1][:], gate[:, h, :],
                                      ALU.mult).then_inc(hid_done, 1)
                    dve.wait_ge(a_hi_done, 2 * f + h + 1)
                    cols = slice(h * HALF, (h + 1) * HALF)
                    if not first:
                        dve.wait_ge(dn_made, NOUT * (f - 1))
                    dve.tensor_tensor(a_lo[s][:, cols], hidden[:, h, :], as_f32(a_hi[s][:, cols]),
                                      ALU.subtract).then_inc(a_lo_done, 1)
                if not first or s:
                    add(f - 1)

            chunks(dve, step)
            add(NF - 1)

        @block.tensor
        def _(pe):
            def gate_up(i, s, first):
                f = 2 * i + s
                pe.wait_ge(gu_lo_done, f + 1)
                for h in range(2):
                    if not first:
                        pe.wait_ge(hid_done, 2 * f + h - 1)
                    for b in range(2):
                        for c in range(ND):
                            cols = slice(h * HALF, (h + 1) * HALF)
                            last = product3(pe, psum[2 * h + b][:], gu_hi[s][:, c, b, :], gu_lo[s][:, c, b, :],
                                            ht["hi"][:, c, cols], ht["lo"][:, c, cols], c == 0, c == ND - 1)
                        last.then_inc(gu_made, 1)

            def step(i, s, first, last_chunk):
                f = 2 * i + s
                if not last_chunk:
                    gate_up(*following(i, s), False)
                pe.wait_ge(dn_lo_done, f + 1)
                pe.wait_ge(a_lo_done, 2 * f + 2)
                for n, (t, half) in enumerate(outs):
                    if not (first and s == 0 and n < 4):
                        pe.wait_ge(added, NOUT * f + n - 3)
                    cols = slice(half * HALF, (half + 1) * HALF)
                    rows = slice(t * P, (t + 1) * P)
                    product3(pe, psum[4 + n % 4][:], a_hi[s][:, rows], a_lo[s][:, rows], dn_hi[s][:, cols],
                             dn_lo[s][:, cols], True, True).then_inc(dn_made, 1)

            gate_up(0, 0, True)
            chunks(pe, step)


def project_out(nc, tag, x, x_dram, ot_dram, w_out, ot, psum):
    mem = Memory(nc, WORK_AT, X_AT)
    SLOTS = 3
    o_raw = [mem(f"{tag}_o_raw{s}", [P, S]) for s in range(SLOTS)]
    w_raw = [mem(f"{tag}_w_raw{s}", [P, D]) for s in range(SLOTS)]
    w_hi = mem(f"{tag}_w_hi", [P, ND, D], F32R)
    w_lo = mem(f"{tag}_w_lo", [P, ND, D], F32R)
    with Phase(nc) as ctx:
        sem = lambda n: ctx.semaphore(f"{tag}_{n}")
        o_in = [sem(f"o_in{s}") for s in range(SLOTS)]
        w_in = [sem(f"w_in{s}") for s in range(SLOTS)]
        x_in = [sem(f"x_in{t}") for t in range(NS)]
        o_hi_done, o_lo_done, w_hi_done, w_lo_done = sem("o_hi_done"), sem("o_lo_done"), sem("w_hi_done"), sem("w_lo_done")
        made, added = sem("made"), sem("added")
        block = ctx.enter_context(nc.Block())

        @block.sync
        def _(sp):
            for c in range(ND):
                if c >= SLOTS:
                    sp.wait_ge(w_lo_done, c - SLOTS + 1)
                    sp.wait_ge(o_lo_done, c - SLOTS + 1)
                sp.dma_start(w_raw[c % SLOTS][:], w_out[c * P:(c + 1) * P, :]).then_inc(w_in[c % SLOTS], 16)
                sp.dma_start(o_raw[c % SLOTS][:], ot_dram[c * P:(c + 1) * P, :]).then_inc(o_in[c % SLOTS], 16)
            for t in range(NS):
                sp.dma_start(x[:, t, :], x_dram[t * P:(t + 1) * P, :]).then_inc(x_in[t], 16)

        @block.gpsimd
        def _(pool):
            for c in range(ND):
                pool.wait_ge(w_hi_done, c + 1)
                pool.tensor_tensor(w_lo[:, c, :], w_raw[c % SLOTS][:], as_f32(w_hi[:, c, :]),
                                   ALU.subtract).then_inc(w_lo_done, 1)

        @block.scalar
        def _(act):
            for c in range(ND):
                act.wait_ge(w_in[c % SLOTS], 16 * (c // SLOTS + 1))
                act.activation(w_hi[:, c, :], w_raw[c % SLOTS][:], ACT.Copy).then_inc(w_hi_done, 1)
                act.wait_ge(o_in[c % SLOTS], 16 * (c // SLOTS + 1))
                act.activation(ot["hi"][:, c, :], o_raw[c % SLOTS][:], ACT.Copy).then_inc(o_hi_done, 1)

        @block.vector
        def _(dve):
            for c in range(ND):
                dve.wait_ge(o_hi_done, c + 1)
                dve.tensor_tensor(ot["lo"][:, c, :], o_raw[c % SLOTS][:], as_f32(ot["hi"][:, c, :]),
                                  ALU.subtract).then_inc(o_lo_done, 1)
            for n in range(2 * NS):
                t, half = n // 2, n % 2
                cols = slice(half * HALF, (half + 1) * HALF)
                dve.wait_ge(x_in[t], 16)
                dve.wait_ge(made, n + 1)
                dve.tensor_tensor(x[:, t, cols], psum[n % 8][:], x[:, t, cols], ALU.add).then_inc(added, 1)

        @block.tensor
        def _(pe):
            for wave in range(2):
                for c in range(ND):
                    pe.wait_ge(w_lo_done, c + 1)
                    pe.wait_ge(o_lo_done, c + 1)
                    for b in range(8):
                        n = 8 * wave + b
                        t, half = n // 2, n % 2
                        if wave and c == 0:
                            pe.wait_ge(added, b + 1)
                        cols, rows = slice(half * HALF, (half + 1) * HALF), slice(t * P, (t + 1) * P)
                        last = product3(pe, psum[b][:], ot["hi"][:, c, rows], ot["lo"][:, c, rows],
                                        w_hi[:, c, cols], w_lo[:, c, cols], c == 0, c == ND - 1)
                        if c == ND - 1:
                            last.then_inc(made, 1)


class Attend:

    def __init__(self, nc, ctx, tag, mem, psum, k, jobs, keys_of, blocks_of, causal, scores, values, scale, store):
        self.nc, self.k, self.jobs, self.causal, self.scale = nc, k, jobs, causal, scale
        self.keys_of, self.blocks_of, self.scores, self.values, self.store = keys_of, blocks_of, scores, values, store
        most = max(keys_of(half * 4 + 3) for _, half in jobs)
        self.p = [mem(f"{tag}_p{s}", [P, 4, most]) for s in range(2)]
        self.pt_hi = [mem(f"{tag}_pt_hi{s}", [P, HALF], F32R) for s in range(2)]
        self.pt_lo = [mem(f"{tag}_pt_lo{s}", [P, HALF], F32R) for s in range(2)]
        self.mx, self.nmx, self.rsum, self.rinv = (mem(f"{tag}_{n}", [P, 4]) for n in ("mx", "nmx", "rsum", "rinv"))
        self.o_tmp = mem(f"{tag}_o_tmp", [HD, HALF])
        self.o_out = [mem(f"{tag}_o_out{s}", [HD, HALF]) for s in range(2)]
        self.s_ps = [psum["pair"][0], psum["pair"][1]]
        self.t_ps = [psum[4], psum[5]]
        self.o_ps = [psum[6], psum[7]]
        sem = lambda n: ctx.semaphore(f"{tag}_{n}")
        (self.scores_made, self.max_done, self.nmax_done, self.exp_done, self.inv_done, self.rows_done,
         self.turned, self.hi_done, self.split_done, self.pv_made, self.out_made, self.tmp_done, self.out_done) = (
            sem(n) for n in ("scores_made", "max_done", "nmax_done", "exp_done", "inv_done", "rows_done", "turned",
                             "hi_done", "split_done", "pv_made", "out_made", "tmp_done", "out_done"))
        self.stored = [sem(f"stored{s}") for s in range(2)]
        self.steps, tau = [("S", 0, i) for i in range(4)], 0
        for n in range(len(jobs)):
            blocks = blocks_of(jobs[n][1])
            for j in range(blocks):
                self.steps.append(("T", n, j, tau))
                tau += 1
                if j == 0 and n:
                    self.steps.append(("E", n - 1))
                if n + 1 < len(jobs):
                    for i in range(4):
                        if i * blocks // 4 == j:
                            self.steps.append(("S", n + 1, i))
        self.steps += [("F",), ("E", len(jobs) - 1)]
        self.nt = tau

    def columns(self, n, j):
        return max(0, j - 4 * self.jobs[n][1]) * P if self.causal else 0

    def pe(self, pe, turn=0):
        ns, nt, nj = 4 * len(self.jobs), self.nt, len(self.jobs)
        before = None

        def products(n, j, tau):
            c0, h = self.columns(n, j), self.jobs[n][0]
            pe.wait_ge(self.split_done, turn * nt + tau + 1)
            if j == 0:
                pe.wait_ge(self.out_done, 1 + turn * nj + max(n - 1, 0))
            o, last = self.o_ps[n % 2], j == self.blocks_of(self.jobs[n][1]) - 1
            pe.matmul(o[:, c0:HALF], self.values(h, j), self.pt_hi[tau % 2][:, c0:HALF],
                      start=j == 0, stop=False, skip_group_check=True)
            mm = pe.matmul(o[:, c0:HALF], self.values(h, j), self.pt_lo[tau % 2][:, c0:HALF],
                           start=False, stop=last, skip_group_check=True)
            mm.then_inc(self.pv_made, 1)
            return last

        for step in self.steps:
            if step[0] == "S":
                _, n, i = step
                s, (h, half) = 4 * n + i, self.jobs[n]
                if s >= 2:
                    pe.wait_ge(self.exp_done, turn * ns + s - 1)
                self.scores(pe, h, 4 * half + i, self.s_ps[s % 2]).then_inc(self.scores_made, 1)
            elif step[0] == "T":
                _, n, j, tau = step
                pe.wait_ge(self.rows_done, turn * ns + 4 * n + 4)
                if tau >= 2:
                    pe.wait_ge(self.split_done, turn * nt + tau - 1)
                for i in range(self.columns(n, j) // P, 4):
                    last = pe.transpose(self.t_ps[tau % 2][:, i * P:(i + 1) * P],
                                        self.p[n % 2][:, i, j * P:(j + 1) * P], self.k["ident"][:])
                last.then_inc(self.turned, 1)
                if before:
                    products(*before)
                before = (n, j, tau)
            elif step[0] == "F":
                products(*before)

    def act(self, act, turn=0):
        ns, nt, nj = 4 * len(self.jobs), self.nt, len(self.jobs)
        first_of = {}
        for step in self.steps:
            if step[0] == "T":
                first_of.setdefault(step[1], step[3])
        for step in self.steps:
            if step[0] == "S":
                _, n, i = step
                s, keys = 4 * n + i, self.keys_of(4 * self.jobs[n][1] + i)
                act.wait_ge(self.nmax_done, turn * ns + s + 1)
                if n >= 2:
                    act.wait_ge(self.turned, turn * nt + first_of[n - 1])
                act.activation(self.p[n % 2][:, i, 0:keys], self.s_ps[s % 2][:, 0:keys], ACT.Exp,
                               bias=self.nmx[:, s % 4:s % 4 + 1], scale=self.scale,
                               accum_out=self.rsum[:, s % 4:s % 4 + 1]).then_inc(self.exp_done, 1)
            elif step[0] == "T":
                _, n, j, tau = step
                c0 = self.columns(n, j)
                act.wait_ge(self.turned, turn * nt + tau + 1)
                act.wait_ge(self.pv_made, 1 + turn * nt + max(tau - 1, 0))
                act.activation(self.pt_hi[tau % 2][:, c0:HALF], self.t_ps[tau % 2][:, c0:HALF],
                               ACT.Copy).then_inc(self.hi_done, 1)
            elif step[0] == "E":
                n = step[1]
                tau_last = first_of[n + 1] if n + 1 < nj else nt
                act.wait_ge(self.pv_made, 1 + turn * nt + tau_last)
                act.wait_ge(self.out_done, 1 + turn * nj + n)
                act.activation(self.o_tmp[:], self.o_ps[n % 2][HD:2 * HD, :], ACT.Copy).then_inc(self.tmp_done, 1)

    def dve(self, dve, turn=0):
        ns, nt, nj = 4 * len(self.jobs), self.nt, len(self.jobs)
        pending = []

        def rows(s, n, i):
            keys = self.keys_of(4 * self.jobs[n][1] + i)
            dve.wait_ge(self.exp_done, turn * ns + s + 1)
            dve.reciprocal(self.rinv[:, s % 4:s % 4 + 1], self.rsum[:, s % 4:s % 4 + 1]).then_inc(self.inv_done, 1)
            dve.wait_ge(self.inv_done, turn * ns + s + 1)
            dve.tensor_scalar(self.p[n % 2][:, i, 0:keys], self.p[n % 2][:, i, 0:keys],
                              self.rinv[:, s % 4:s % 4 + 1], None, ALU.mult).then_inc(self.rows_done, 1)

        for step in self.steps:
            if step[0] == "S":
                _, n, i = step
                s, keys = 4 * n + i, self.keys_of(4 * self.jobs[n][1] + i)
                one = slice(s % 4, s % 4 + 1)
                dve.wait_ge(self.scores_made, turn * ns + s + 1)
                dve.tensor_reduce(self.mx[:, one], self.s_ps[s % 2][:, 0:keys], AX, ALU.max).then_inc(self.max_done, 1)
                if pending:
                    rows(*pending.pop())
                dve.wait_ge(self.max_done, turn * ns + s + 1)
                dve.tensor_scalar(self.nmx[:, one], self.mx[:, one], -self.scale, None,
                                  ALU.mult).then_inc(self.nmax_done, 1)
                pending.append((s, n, i))
            elif step[0] == "T":
                _, n, j, tau = step
                if pending:
                    rows(*pending.pop())
                c0 = self.columns(n, j)
                dve.wait_ge(self.hi_done, turn * nt + tau + 1)
                dve.tensor_tensor(self.pt_lo[tau % 2][:, c0:HALF], self.t_ps[tau % 2][:, c0:HALF],
                                  as_f32(self.pt_hi[tau % 2][:, c0:HALF]), ALU.subtract).then_inc(self.split_done, 1)
            elif step[0] == "E":
                n = step[1]
                dve.wait_ge(self.tmp_done, turn * nj + n + 1)
                dve.wait_ge(self.stored[n % 2], 16 + 16 * (turn * (nj // 2) + n // 2))
                dve.tensor_tensor(self.o_out[n % 2][:], self.o_ps[n % 2][0:HD, :], self.o_tmp[:],
                                  ALU.add).then_inc(self.out_done, 1)

    def begin(self, sp):
        for s in (self.pv_made, self.out_done):
            sp.sem_inc(s, 1)
        for s in self.stored:
            sp.sem_inc(s, 16)

    def sync(self, sp, turn=0):
        nj = len(self.jobs)
        for n, (h, half) in enumerate(self.jobs):
            sp.wait_ge(self.out_done, 1 + turn * nj + n + 1)
            sp.dma_start(self.store(h, half), self.o_out[n % 2][:]).then_inc(self.stored[n % 2], 16)

    def finish(self, sp, turns=1):
        for s in range(2):
            sp.wait_ge(self.stored[s], 16 + 16 * turns * (len(self.jobs) // 2))


def wide(ap, n, w):
    return ap.unsqueeze(2).broadcast_to([P, n, w])


def rows_of(ap, n, w):
    return ap.unsqueeze(1).broadcast_to([P, n, w])


def memory_heads(nc, tag, k, mem_dram, ln_mem, w_kv, g_q, g_k, w_q, ht, psum, ot_dram):
    top = Memory(nc, X_AT, 229344)
    mem_x = top(f"{tag}_mem_x", [P, MEM // P, D])
    mt = {h: top(f"{tag}_mt_{h}", [P, ND, MEM], F32R) for h in ("hi", "lo")}
    norm_transposed(nc, f"{tag}_mn", k, mem_x, mem_dram, ln_mem, mt, psum)

    NKH, NQH = (MEM // P) * MEM_HEADS, NS * MEM_HEADS
    mem = Memory(nc, WORK_AT, X_AT)
    q_st = mem(f"{tag}_q_st", [P, MEM_HEADS, S], F32R)
    k_hh = mem(f"{tag}_k_hh", [P, MEM_HEADS, MEM], F32R)
    k_ll = mem(f"{tag}_k_ll", [P, MEM_HEADS, MEM], F32R)
    v = mem(f"{tag}_v", [P, MEM // P, MEM_HEADS, 2 * HD], F32R)
    kept = mem.at
    q32 = mem(f"{tag}_q32", [P, NQH, HD])
    k32 = mem(f"{tag}_k32", [P, NKH, 2, HD])
    wkv = [mem(f"{tag}_wkv_{h}", [P, ND // 2, 2 * MEM_Q], dt) for h, dt in (("hi", F32R), ("lo", F32R))]
    wq = [mem(f"{tag}_wq_{h}", [P, ND, MEM_Q], F32R) for h in ("hi", "lo")]
    raw = mem(f"{tag}_raw", [P, ND // 2, 2 * MEM_Q])
    with Phase(nc) as ctx:
        sem = lambda n: ctx.semaphore(f"{tag}p_{n}")
        w_in, hi_done, lo_done, made, evicted = sem("w_in"), sem("hi_done"), sem("lo_done"), sem("made"), sem("evicted")
        block = ctx.enter_context(nc.Block())
        kv_rows, q_rows = w_kv.rearrange("(c p) n -> p c n", p=P), w_q.rearrange("(c p) n -> p c n", p=P)
        raw_q = raw[:].rearrange("p c (a n) -> p (c a) n", a=2)
        raws = [raw[:], raw[:], raw_q]
        his = [wkv[0][:], wkv[0][:], wq[0][:]]
        los = [wkv[1][:], wkv[1][:], wq[1][:]]

        @block.sync
        def _(sp):
            for n, src in enumerate((kv_rows[:, 0:ND // 2, :], kv_rows[:, ND // 2:ND, :], q_rows)):
                if n:
                    sp.wait_ge(lo_done, n)
                sp.dma_start(raws[n], src).then_inc(w_in, 16)

        @block.scalar
        def _(act):
            for n in range(3):
                act.wait_ge(w_in, 16 * (n + 1))
                if n == 1:
                    act.wait_ge(made, 1)
                act.activation(his[n], raws[n], ACT.Copy).then_inc(hi_done, 1)

        @block.vector
        def _(dve):
            for n in range(3):
                dve.wait_ge(hi_done, n + 1)
                dve.tensor_tensor(los[n], raws[n], as_f32(his[n]), ALU.subtract).then_inc(lo_done, 1)
            dve.wait_ge(made, 2)
            for t in range(MEM // P):
                dve.tensor_copy(k32[:, t * MEM_HEADS:(t + 1) * MEM_HEADS, :, :],
                                psum[t][:].rearrange("p (h a d) -> p h a d", h=MEM_HEADS, a=2))
            for t in range(NS):
                dve.wait_ge(made, 3 + t)
                dve.tensor_copy(q32[:, t * MEM_HEADS:(t + 1) * MEM_HEADS, :],
                                psum[2 + t % 4][:, 0:MEM_Q].rearrange("p (h d) -> p h d", h=MEM_HEADS)).then_inc(evicted, 1)

        @block.tensor
        def _(pe):
            for part in range(2):
                pe.wait_ge(lo_done, part + 1)
                for t in range(MEM // P):
                    for c in range(ND // 2):
                        cc = part * (ND // 2) + c
                        rows = slice(t * P, (t + 1) * P)
                        last = product3(pe, psum[t][:], mt["hi"][:, cc, rows], mt["lo"][:, cc, rows],
                                        wkv[0][:, c, :], wkv[1][:, c, :], cc == 0, cc == ND - 1)
                last.then_inc(made, 1)
            pe.wait_ge(lo_done, 3)
            for t in range(NS):
                if t >= 4:
                    pe.wait_ge(evicted, t - 3)
                rows = slice(t * P, (t + 1) * P)
                for c in range(ND):
                    last = product3(pe, psum[2 + t % 4][:, 0:MEM_Q], ht["hi"][:, c, rows], ht["lo"][:, c, rows],
                                    wq[0][:, c, :], wq[1][:, c, :], c == 0, c == ND - 1)
                last.then_inc(made, 1)

    mem = Memory(nc, mem.at - 0, X_AT)
    mem.at = kept + NQH * HD * 4 + NKH * 2 * HD * 4
    sq = mem(f"{tag}_sq", [P, NQH, HD])
    q_hl = mem(f"{tag}_q_hl", [P, NQH, 2, HD], F32R)
    k_hl = mem(f"{tag}_k_hl", [P, 2, NKH, 2, HD], F32R)
    ss, std, rstd = (mem(f"{tag}_{n}", [P, NKH + NQH]) for n in ("hss", "hstd", "hrstd"))
    gq, gk = mem(f"{tag}_gq", [P, HD]), mem(f"{tag}_gk", [P, HD])
    with Phase(nc) as ctx:
        sem = lambda n: ctx.semaphore(f"{tag}h_{n}")
        g_in, chain, sums, root, normed, hi_done, lo_done, turned, stacked = (
            sem(n) for n in ("g_in", "chain", "sums", "root", "normed", "hi_done", "lo_done", "turned", "stacked"))
        block = ctx.enter_context(nc.Block())
        kk = k32[:, :, 0, :]
        v_flat = v[:].rearrange("p t h (a d) -> p (t h) a d", a=2)
        turns = [("k", a, t) for a in range(2) for t in range(MEM // P)] + [("q", 0, t) for t in range(NS)]

        @block.sync
        def _(sp):
            sp.dma_start(gq[:], g_q.partition_broadcast(P)).then_inc(g_in, 16)
            sp.dma_start(gk[:], g_k.partition_broadcast(P)).then_inc(g_in, 16)

        @block.vector
        def _(dve):
            dve.tensor_tensor(sq[:, 0:NKH, :], kk, kk, ALU.mult).then_inc(chain, 1)
            dve.wait_ge(chain, 1)
            dve.tensor_reduce(ss[:, 0:NKH], sq[:, 0:NKH, :], AX, ALU.add).then_inc(chain, 1)
            dve.wait_ge(chain, 2)
            dve.tensor_tensor(sq[:], q32[:], q32[:], ALU.mult).then_inc(chain, 1)
            dve.wait_ge(chain, 3)
            dve.tensor_reduce(ss[:, NKH:], sq[:], AX, ALU.add).then_inc(sums, 1)
            dve.wait_ge(root, 1)
            dve.reciprocal(rstd[:], std[:]).then_inc(chain, 1)
            dve.wait_ge(chain, 4)
            dve.tensor_tensor(kk, kk, wide(rstd[:, 0:NKH], NKH, HD), ALU.mult).then_inc(chain, 1)
            dve.tensor_tensor(q32[:], q32[:], wide(rstd[:, NKH:], NQH, HD), ALU.mult).then_inc(chain, 1)
            dve.wait_ge(g_in, 32)
            dve.wait_ge(chain, 5)
            dve.tensor_tensor(kk, kk, rows_of(gk[:], NKH, HD), ALU.mult).then_inc(normed, 1)
            dve.wait_ge(chain, 6)
            dve.tensor_tensor(q32[:], q32[:], rows_of(gq[:], NQH, HD), ALU.mult).then_inc(normed, 1)
            dve.wait_ge(hi_done, 3)
            for a in range(2):
                dve.tensor_tensor(k_hl[:, 1, :, a, :], kk, as_f32(k_hl[:, 0, :, a, :]), ALU.subtract).then_inc(lo_done, 1)
            dve.tensor_tensor(v_flat[:, :, 1, :], k32[:, :, 1, :], as_f32(v_flat[:, :, 0, :]), ALU.subtract)
            dve.wait_ge(hi_done, 4)
            dve.tensor_tensor(q_hl[:, :, 1, :], q32[:], as_f32(q_hl[:, :, 0, :]), ALU.subtract).then_inc(lo_done, 1)
            for n, (what, a, t) in enumerate(turns):
                if n % 2:
                    dve.wait_ge(turned, n + 1)
                    dst = q_st if what == "q" else (k_hh, k_ll)[a]
                    dve.tensor_copy(dst[:, :, t * P:(t + 1) * P],
                                    psum[n % 8][:].rearrange("p (h q) -> p h q", h=MEM_HEADS)).then_inc(stacked, 1)

        @block.scalar
        def _(act):
            act.wait_ge(sums, 1)
            act.activation(std[:], ss[:], ACT.Sqrt, bias=k["eps"][:, 0:1], scale=1.0 / HD).then_inc(root, 1)
            act.wait_ge(normed, 1)
            for a in range(2):
                act.activation(k_hl[:, 0, :, a, :], kk, ACT.Copy).then_inc(hi_done, 1)
            act.activation(v_flat[:, :, 0, :], k32[:, :, 1, :], ACT.Copy).then_inc(hi_done, 1)
            act.wait_ge(normed, 2)
            act.activation(q_hl[:, :, 0, :], q32[:], ACT.Copy).then_inc(hi_done, 1)
            for n, (what, a, t) in enumerate(turns):
                if n % 2 == 0:
                    act.wait_ge(turned, n + 1)
                    dst = q_st if what == "q" else (k_hh, k_ll)[a]
                    act.activation(dst[:, :, t * P:(t + 1) * P],
                                   psum[n % 8][:].rearrange("p (h q) -> p h q", h=MEM_HEADS), ACT.Copy).then_inc(stacked, 1)

        @block.tensor
        def _(pe):
            pe.wait_ge(lo_done, 2)
            for n, (what, a, t) in enumerate(turns):
                if what == "q" and t == 0:
                    pe.wait_ge(lo_done, 3)
                if n >= 8:
                    pe.wait_ge(stacked, 8)
                for h in range(MEM_HEADS):
                    g = t * MEM_HEADS + h
                    src = q_hl[:, g, :, :] if what == "q" else k_hl[:, a, g, :, :]
                    last = pe.transpose(psum[n % 8][:, h * P:(h + 1) * P],
                                        as_f32(src.rearrange("p a d -> p (a d)")), k["ident"][:])
                last.then_inc(turned, 1)

    mem = Memory(nc, kept, X_AT)
    with Phase(nc) as ctx:
        def scores(pe, h, tile, out):
            rows = slice(tile * P, (tile + 1) * P)
            pe.matmul(out[:, 0:MEM], q_st[:, h, rows], k_hh[:, h, :], start=True, stop=False, skip_group_check=True)
            return pe.matmul(out[:, 0:MEM], q_st[:, h, rows], k_ll[:, h, :], start=False, stop=True, skip_group_check=True)

        jobs = [(h, half) for h in range(MEM_HEADS) for half in range(2)]
        at = Attend(nc, ctx, f"{tag}a", mem, psum, k, jobs, lambda tile: MEM, lambda half: MEM // P, False, scores,
                    lambda h, j: v[:, j, h, :], float(HD) ** -0.5,
                    lambda h, half: ot_dram[SB_Q + h * HD:SB_Q + (h + 1) * HD, half * HALF:(half + 1) * HALF])
        block = ctx.enter_context(nc.Block())

        @block.sync
        def _(sp):
            at.begin(sp)
            at.sync(sp)
            at.finish(sp)

        @block.tensor
        def _(pe):
            at.pe(pe)

        @block.scalar
        def _(act):
            at.act(act)

        @block.vector
        def _(dve):
            at.dve(dve)


def stick_breaking(nc, tag, k, w_in_dram, ht, psum, ot_dram):
    mem = Memory(nc, WORK_AT, 229344)
    q_st = mem(f"{tag}_q_st", [P, 2, S], F32R)
    k_hh = mem(f"{tag}_k_hh", [P, 2, S], F32R)
    k_ll = mem(f"{tag}_k_ll", [P, 2, S], F32R)
    v = mem(f"{tag}_v", [P, NS, 2, 2 * HD], F32R)
    v_t = mem(f"{tag}_v_t", [P, S])
    raw = [mem(f"{tag}_raw{i}", [P, ND, P]) for i in range(3)]
    w_hi = [mem(f"{tag}_w_hi{i}", [P, ND, P], F32R) for i in range(3)]
    w_lo = [mem(f"{tag}_w_lo{i}", [P, ND, P], F32R) for i in range(3)]
    NA, NR, NW = 2, 6, 2
    soft = [mem(f"{tag}_soft{s}", [P, HALF]) for s in range(NA)]
    run = [mem(f"{tag}_run{s}", [P, HALF]) for s in range(NR)]
    run_hi = [mem(f"{tag}_run_hi{s}", [P, HALF], F32R) for s in range(NR)]
    run_lo = [mem(f"{tag}_run_lo{s}", [P, HALF], F32R) for s in range(NR)]
    wt = [mem(f"{tag}_wt{s}", [P, HALF]) for s in range(NW)]
    wt_hi = [mem(f"{tag}_wt_hi{s}", [P, HALF], F32R) for s in range(NW)]
    wt_lo = [mem(f"{tag}_wt_lo{s}", [P, HALF], F32R) for s in range(NW)]
    o_tmp = mem(f"{tag}_o_tmp", [HD, HALF])
    o_out = [mem(f"{tag}_o_out{s}", [HD, HALF]) for s in range(2)]
    rows = w_in_dram.rearrange("(c p) n -> p c n", p=P)

    blocks = [(c, j, h) for c in range(2) for j in reversed(range(4 * c + 4)) for h in range(2)]
    NB = len(blocks)
    NZ = 6
    first_col = [max(0, j - 4 * c) * P for c, j, h in blocks]
    chained = [b for b, (c, j, h) in enumerate(blocks) if j < 4 * c + 3]
    n_chained = [sum(1 for x in chained if x <= b) for b in range(NB)]
    NC = len(chained)
    next_col = [first_col[b - 2] for b in range(NB)]
    OUT_AT = {b: 2 * c + h for b, (c, j, h) in enumerate(blocks) if j == 0}
    LAG_U, LAG_SPLIT, LAG_PV = 3, 4, 5
    HI = [2, 4, 6 + 0]
    with Phase(nc) as ctx:
        sem = lambda n: ctx.semaphore(f"{tag}_{n}")
        w_in = [sem(f"w_in{i}") for i in range(3)]
        w_hi_done = [sem(f"w_hi_done{i}") for i in range(3)]
        w_lo_done = [sem(f"w_lo_done{i}") for i in range(3)]
        (proj_made, proj_hi, proj_split, scores_made, abs_done, exp_done, soft_done, sp_done, run_added, run_hi_done,
         run_split, sums_made, weight_done, weight_hi, weight_split, pv_made, tmp_done, out_done) = (
            sem(n) for n in ("proj_made", "proj_hi", "proj_split", "scores_made", "abs_done", "exp_done", "soft_done",
                             "sp_done", "run_added", "run_hi_done", "run_split", "sums_made", "weight_done",
                             "weight_hi", "weight_split", "pv_made", "tmp_done", "out_done"))
        stored = [sem(f"stored{s}") for s in range(2)]
        block = ctx.enter_context(nc.Block())
        hi_after = [2, 4, 8, 12, 12, 12, 13, 14]

        @block.sync
        def _(sp):
            def load(i, g):
                sp.dma_start(raw[i][:], rows[:, :, bass.ds(g * P + i * SB_Q, P)]).then_inc(w_in[i], 16)

            for s in (sp_done, weight_split, out_done, run_split, sums_made, pv_made, weight_done):
                sp.sem_inc(s, 1)
            for s in stored:
                sp.sem_inc(s, 16)
            for i in range(3):
                load(i, 0)
            with sp.Fori(0, PAIRS) as g:
                for i in range(3):
                    sp.wait_ge(w_lo_done[i], g + 1)
                    load(i, g + 1)
                for n in range(4):
                    sp.wait_ge(out_done, 1 + 4 * g + n + 1)
                    sp.dma_start(ot_dram[bass.ds(g * P + (n % 2) * HD, HD), (n // 2) * HALF:(n // 2 + 1) * HALF],
                                 o_out[n % 2][:]).then_inc(stored[n % 2], 16)
            for s in range(2):
                sp.wait_ge(stored[s], 16 + 16 * 2 * PAIRS)

        @block.gpsimd
        def _(pool):
            def lower(i, g):
                pool.wait_ge(w_hi_done[i], g + 1)
                pool.tensor_tensor(w_lo[i][:], raw[i][:], as_f32(w_hi[i][:]), ALU.subtract).then_inc(w_lo_done[i], 1)

            for i in range(3):
                lower(i, 0)
            with pool.Fori(0, PAIRS) as g:
                for i in range(3):
                    lower(i, g + 1)
                for t in range(NB + 1):
                    if t in chained:
                        f = next_col[t]
                        pool.wait_ge(sp_done, 1 + g * NB + t + 1)
                        pool.tensor_tensor(run[t % NR][:, f:HALF], run[t % NR][:, f:HALF],
                                           run[(t - 2) % NR][:, f:HALF], ALU.add).then_inc(run_added, 1)
                    b = t - 1
                    if b >= 0:
                        f = first_col[b]
                        pool.wait_ge(run_hi_done, g * NB + b + 1)
                        pool.tensor_tensor(run_lo[b % NR][:, f:HALF], run[b % NR][:, f:HALF],
                                           as_f32(run_hi[b % NR][:, f:HALF]), ALU.subtract).then_inc(run_split, 1)

        @block.scalar
        def _(act):
            def upper(i, g):
                act.wait_ge(w_in[i], 16 * (g + 1))
                act.activation(w_hi[i][:], raw[i][:], ACT.Copy).then_inc(w_hi_done[i], 1)

            for i in range(3):
                upper(i, 0)
            act.preload_act_table_set("natural_log_exp_and_others")
            with act.Fori(0, PAIRS) as g:
                for u in range(8):
                    half = u % 2
                    cols = slice(half * HALF, (half + 1) * HALF)
                    z = psum[u % 4]
                    if u // 2 != 2:
                        act.wait_ge(proj_made, 8 * g + u + 1)
                    if u // 2 == 0:
                        for h in range(2):
                            r = slice(h * HD, (h + 1) * HD)
                            act.activation(q_st[r, h, cols], z[r, :], ACT.Copy, scale=0.125).then_inc(proj_hi, 1)
                    elif u // 2 == 1:
                        for h in range(2):
                            for a in range(2):
                                act.activation(k_hh[a * HD:(a + 1) * HD, h, cols], z[h * HD:(h + 1) * HD, :],
                                               ACT.Copy).then_inc(proj_hi, 1)
                    elif u // 2 == 3:
                        act.activation(v[:, 4 * half:4 * half + 4, :, 0:HD],
                                       z.rearrange("p (t h d) -> p t h d", t=4, h=2), ACT.Copy).then_inc(proj_hi, 1)
                    if u in (1, 3, 5):
                        act.wait_ge(proj_made, 8 * g + u + 1)
                        upper(u // 2, g + 1)
                for t in range(NB + LAG_PV + 2):
                    if t < NB:
                        f, s = first_col[t], soft[t % NA]
                        act.wait_ge(scores_made, g * NB + t + 1)
                        act.wait_ge(sp_done, 1 + g * NB + max(t - 1, 0))
                        act.activation(s[:, f:HALF], psum[t % NZ][:, f:HALF], ACT.Abs).then_inc(abs_done, 1)
                        act.wait_ge(abs_done, g * NB + t + 1)
                        act.activation(s[:, f:HALF], s[:, f:HALF], ACT.Exp, scale=-1.0).then_inc(exp_done, 1)
                        act.wait_ge(exp_done, g * NB + t + 1)
                        act.activation(s[:, f:HALF], s[:, f:HALF], ACT.Ln, bias=1.0).then_inc(soft_done, 1)
                    b = t - LAG_U
                    if 0 <= b < NB:
                        f = first_col[b]
                        act.wait_ge(sums_made, 1 + g * NB + b + 1)
                        act.wait_ge(weight_split, 1 + g * NB + max(b - 1, 0))
                        act.activation(wt[b % NW][:, f:HALF], psum[b % NZ][:, f:HALF], ACT.Exp).then_inc(weight_done, 1)
                    b = t - LAG_PV - 1
                    if b in OUT_AT:
                        n = OUT_AT[b]
                        act.wait_ge(pv_made, 1 + g * NB + b + 1)
                        act.wait_ge(out_done, 1 + 4 * g + n)
                        act.activation(o_tmp[:], psum[6 + n % 2][HD:2 * HD, :], ACT.Copy).then_inc(tmp_done, 1)

        @block.vector
        def _(dve):
            with dve.Fori(0, PAIRS) as g:
                for u in range(8):
                    half = u % 2
                    cols = slice(half * HALF, (half + 1) * HALF)
                    z = psum[u % 4]
                    if u // 2 == 2:
                        dve.wait_ge(proj_made, 8 * g + u + 1)
                        dve.tensor_copy(v_t[:, cols], z[:]).then_inc(proj_split, 1)
                        continue
                    dve.wait_ge(proj_hi, 14 * g + hi_after[u])
                    if u // 2 == 0:
                        for h in range(2):
                            r, o = slice(h * HD, (h + 1) * HD), slice((1 - h) * HD, (2 - h) * HD)
                            last = dve.scalar_tensor_tensor(q_st[o, h, cols], z[r, :], 0.125,
                                                            as_f32(q_st[r, h, cols]), ALU.mult, ALU.subtract)
                    elif u // 2 == 1:
                        for h in range(2):
                            r = slice(h * HD, (h + 1) * HD)
                            for a in range(2):
                                last = dve.tensor_tensor(k_ll[a * HD:(a + 1) * HD, h, cols], z[r, :],
                                                         as_f32(k_hh[r, h, cols]), ALU.subtract)
                    else:
                        last = dve.tensor_tensor(
                            v[:, 4 * half:4 * half + 4, :, HD:2 * HD], z.rearrange("p (t h d) -> p t h d", t=4, h=2),
                            as_f32(v[:, 4 * half:4 * half + 4, :, 0:HD]), ALU.subtract)
                    last.then_inc(proj_split, 1)
                for t in range(NB + LAG_PV + 2):
                    if t < NB:
                        f = first_col[t]
                        dve.wait_ge(soft_done, g * NB + t + 1)
                        dve.wait_ge(run_split, 1 + g * NB + max(t - 3, 0))
                        dve.scalar_tensor_tensor(run[t % NR][:, f:HALF], psum[t % NZ][:, f:HALF], 0.0,
                                                 soft[t % NA][:, f:HALF], ALU.max, ALU.add).then_inc(sp_done, 1)
                    b = t - 1
                    if 0 <= b < NB:
                        f = first_col[b]
                        if b in chained:
                            dve.wait_ge(run_added, g * NC + n_chained[b])
                        else:
                            dve.wait_ge(sp_done, 1 + g * NB + b + 1)
                        dve.wait_ge(sums_made, 1 + g * NB + max(b - 3, 0))
                        dve.tensor_copy(run_hi[b % NR][:, f:HALF], run[b % NR][:, f:HALF]).then_inc(run_hi_done, 1)
                    b = t - LAG_SPLIT
                    if 0 <= b < NB:
                        f = first_col[b]
                        dve.wait_ge(weight_done, 1 + g * NB + b + 1)
                        dve.wait_ge(pv_made, 1 + g * NB + max(b - 1, 0))
                        dve.tensor_copy(wt_hi[b % NW][:, f:HALF], wt[b % NW][:, f:HALF]).then_inc(weight_hi, 1)
                        dve.wait_ge(weight_hi, g * NB + b + 1)
                        dve.tensor_tensor(wt_lo[b % NW][:, f:HALF], wt[b % NW][:, f:HALF],
                                          as_f32(wt_hi[b % NW][:, f:HALF]), ALU.subtract).then_inc(weight_split, 1)
                    b = t - LAG_PV - 1
                    if b in OUT_AT:
                        n = OUT_AT[b]
                        dve.wait_ge(tmp_done, 4 * g + n + 1)
                        dve.wait_ge(stored[n % 2], 16 + 16 * (2 * g + n // 2))
                        dve.tensor_tensor(o_out[n % 2][:], psum[6 + n % 2][0:HD, :], o_tmp[:], ALU.add).then_inc(out_done, 1)

        @block.tensor
        def _(pe):
            with pe.Fori(0, PAIRS) as g:
                for u in range(6):
                    i, half = u // 2, u % 2
                    cols = slice(half * HALF, (half + 1) * HALF)
                    pe.wait_ge(w_lo_done[i], g + 1)
                    if u < 4:
                        pe.wait_ge(weight_done, 1 + g * NB)
                    else:
                        pe.wait_ge(proj_split, 8 * g + u - 3)
                    for c in range(ND):
                        last = product3(pe, psum[u % 4][:], w_hi[i][:, c, :], w_lo[i][:, c, :],
                                        ht["hi"][:, c, cols], ht["lo"][:, c, cols], c == 0, c == ND - 1)
                    last.then_inc(proj_made, 1)
                for half in range(2):
                    pe.wait_ge(proj_split, 8 * g + 5 + half)
                    for i in range(4):
                        tt = 4 * half + i
                        last = pe.transpose(psum[2 + half][:, i * P:(i + 1) * P], v_t[:, tt * P:(tt + 1) * P], k["ident"][:])
                    last.then_inc(proj_made, 1)
                pe.wait_ge(proj_split, 8 * g + 8)
                for t in range(NB + LAG_PV):
                    if t < NB:
                        c, j, h = blocks[t]
                        f, z = first_col[t], psum[t % NZ]
                        if t >= NZ:
                            pe.wait_ge(weight_done, 1 + g * NB + t - NZ + 1)
                        q = q_st[:, h, c * HALF + f:(c + 1) * HALF]
                        diagonal = j >= 4 * c
                        pe.matmul(z[:, f:HALF], k_hh[:, h, j * P:(j + 1) * P], q, start=True, stop=False, skip_group_check=True)
                        last = pe.matmul(z[:, f:HALF], k_ll[:, h, j * P:(j + 1) * P], q, start=False,
                                         stop=not diagonal, skip_group_check=True)
                        if diagonal:
                            last = pe.matmul(z[:, f:f + P], k["ident_r"][:], k["strict"][:], start=False, stop=True,
                                             skip_group_check=True)
                        last.then_inc(scores_made, 1)
                    b = t - LAG_U
                    if 0 <= b < NB:
                        f, fn, z, s = first_col[b], next_col[b], psum[b % NZ], b % NR
                        pe.wait_ge(run_split, 1 + g * NB + b + 1)
                        pe.wait_ge(sp_done, 1 + g * NB + b + 1)
                        pe.matmul(z[:, f:HALF], k["upper"][:], run_hi[s][:, f:HALF], start=False, stop=False, skip_group_check=True)
                        last = pe.matmul(z[:, f:HALF], k["upper"][:], run_lo[s][:, f:HALF], start=False,
                                         stop=b not in chained, skip_group_check=True)
                        if b in chained:
                            s = (b - 2) % NR
                            pe.matmul(z[:, fn:HALF], k["lower"][:], run_hi[s][:, fn:HALF], start=False, stop=False, skip_group_check=True)
                            last = pe.matmul(z[:, fn:HALF], k["lower"][:], run_lo[s][:, fn:HALF], start=False,
                                             stop=True, skip_group_check=True)
                        last.then_inc(sums_made, 1)
                    b = t - LAG_PV
                    if 0 <= b < NB:
                        c, j, h = blocks[b]
                        f, o = first_col[b], psum[6 + h]
                        pe.wait_ge(weight_split, 1 + g * NB + b + 1)
                        if b not in chained:
                            pe.wait_ge(out_done, 1 + 4 * g + (0 if c == 0 else h + 1))
                        pe.matmul(o[:, f:HALF], v[:, j, h, :], wt_hi[b % NW][:, f:HALF], start=b not in chained,
                                  stop=False, skip_group_check=True)
                        pe.matmul(o[:, f:HALF], v[:, j, h, :], wt_lo[b % NW][:, f:HALF], start=False,
                                  stop=j == 0, skip_group_check=True).then_inc(pv_made, 1)


def down_project(nc, tag, k, w_dram, width, rank, gain, ht, out, extra, at, psum):
    mem = Memory(nc, at, 229344)
    raw = [mem(f"{tag}_raw{s}", [P, width]) for s in range(2)]
    w_hi = mem(f"{tag}_w_hi", [P, ND, width], F32R)
    w_lo = mem(f"{tag}_w_lo", [P, ND, width], F32R)
    c32 = mem(f"{tag}_c32", [P, 4, rank])
    ss, std, rstd = (mem(f"{tag}_{n}", [P, NS]) for n in ("ss", "std", "rstd"))
    junk = mem(f"{tag}_junk", [P, rank])
    nr = rank // P
    gcol = mem(f"{tag}_gcol", [P, nr])
    pieces = 2 if width > HALF else 1
    pw = width // pieces
    rw = rank // pieces
    rows = w_dram.rearrange("(c p) n -> c p n", p=P)
    with Phase(nc) as ctx:
        sem = lambda n: ctx.semaphore(f"{tag}_{n}")
        w_in = [sem(f"w_in{s}") for s in range(2)]
        g_in, w_hi_done, w_lo_done, made, copied, squared, root, inverse, normed, turned, hi_done, lo_done = (
            sem(n) for n in ("g_in", "w_hi_done", "w_lo_done", "made", "copied", "squared", "root", "inverse",
                             "normed", "turned", "hi_done", "lo_done"))
        block = ctx.enter_context(nc.Block())

        @block.sync
        def _(sp):
            with nc.allow_non_contiguous_dma("gain"):
                sp.dma_start(gcol[:], gain_columns(gain)).then_inc(g_in, 16)
            for c in range(ND):
                if c >= 2:
                    sp.wait_ge(w_lo_done, c - 1)
                sp.dma_start(raw[c % 2][:], rows[c]).then_inc(w_in[c % 2], 16)

        @block.gpsimd
        def _(pool):
            for c in range(1, ND, 2):
                pool.wait_ge(w_hi_done, c + 1)
                pool.wait_ge(w_lo_done, c)
                pool.tensor_tensor(w_lo[:, c, :], raw[c % 2][:], as_f32(w_hi[:, c, :]), ALU.subtract).then_inc(w_lo_done, 1)

        @block.scalar
        def _(act):
            for c in range(ND):
                act.wait_ge(w_in[c % 2], 16 * (c // 2 + 1))
                act.activation(w_hi[:, c, :], raw[c % 2][:], ACT.Copy).then_inc(w_hi_done, 1)
            act.wait_ge(g_in, 16)
            for grp in range(2):
                for i in range(4):
                    act.wait_ge(copied, 4 * grp + i + 1)
                    t = 4 * grp + i
                    if t:
                        act.wait_ge(squared, t)
                    act.activation(junk[:], c32[:, i, :], ACT.Square, accum_out=ss[:, t:t + 1]).then_inc(squared, 1)
                act.wait_ge(squared, 4 * grp + 4)
                g4 = slice(4 * grp, 4 * grp + 4)
                act.activation(std[:, g4], ss[:, g4], ACT.Sqrt, bias=k["eps"][:, 0:1], scale=1.0 / rank).then_inc(root, 1)
                for c in range(nr):
                    n = grp * nr + c
                    act.wait_ge(turned, n + 1)
                    act.activation(out["hi"][:, c, grp * HALF:(grp + 1) * HALF], psum[4 + n % 4][:], ACT.Copy,
                                   scale=gcol[:, c:c + 1]).then_inc(hi_done, 1)

        @block.vector
        def _(dve):
            for c in range(0, ND, 2):
                dve.wait_ge(w_hi_done, c + 1)
                if c:
                    dve.wait_ge(w_lo_done, c)
                dve.tensor_tensor(w_lo[:, c, :], raw[c % 2][:], as_f32(w_hi[:, c, :]), ALU.subtract).then_inc(w_lo_done, 1)
            for grp in range(2):
                for i in range(4):
                    t = 4 * grp + i
                    dve.wait_ge(made, t + 1)
                    if grp:
                        dve.wait_ge(turned, nr)
                    for p in range(pieces):
                        bank = psum[(t % 2) * pieces + p]
                        last = dve.tensor_copy(c32[:, i, p * rw:(p + 1) * rw], bank[:, 0:rw])
                    if extra is not None:
                        last = dve.tensor_copy(extra[:, t, :], bank[:, rw:pw])
                    last.then_inc(copied, 1)
                dve.wait_ge(root, grp + 1)
                g4 = slice(4 * grp, 4 * grp + 4)
                dve.reciprocal(rstd[:, g4], std[:, g4]).then_inc(inverse, 1)
                dve.wait_ge(inverse, grp + 1)
                for i in range(4):
                    t = 4 * grp + i
                    dve.tensor_scalar(c32[:, i, :], c32[:, i, :], rstd[:, t:t + 1], None, ALU.mult).then_inc(normed, 1)
                for c in range(nr):
                    n = grp * nr + c
                    cols = slice(grp * HALF, (grp + 1) * HALF)
                    dve.wait_ge(hi_done, n + 1)
                    dve.scalar_tensor_tensor(out["lo"][:, c, cols], psum[4 + n % 4][:], gcol[:, c:c + 1],
                                             as_f32(out["hi"][:, c, cols]), ALU.mult, ALU.subtract).then_inc(lo_done, 1)

        @block.tensor
        def _(pe):
            pe.wait_ge(w_lo_done, ND)
            for grp in range(2):
                for i in range(4):
                    t = 4 * grp + i
                    if t >= 2:
                        pe.wait_ge(copied, t - 1)
                    r = slice(t * P, (t + 1) * P)
                    for p in range(pieces):
                        cols = slice(p * pw, (p + 1) * pw)
                        for c in range(ND):
                            last = product3(pe, psum[(t % 2) * pieces + p][:, 0:pw], ht["hi"][:, c, r], ht["lo"][:, c, r],
                                            w_hi[:, c, cols], w_lo[:, c, cols], c == 0, c == ND - 1)
                    last.then_inc(made, 1)
                pe.wait_ge(normed, 4 * grp + 4)
                for c in range(nr):
                    n = grp * nr + c
                    if n >= 4:
                        pe.wait_ge(lo_done, n - 3)
                    for i in range(4):
                        last = pe.transpose(psum[4 + n % 4][:, i * P:(i + 1) * P], c32[:, i, c * P:(c + 1) * P], k["ident"][:])
                    last.then_inc(turned, 1)


TWO_PI = 6.283185307179586
TURN = (6.28125, float(np.float32(np.int64(0.0019353071795864769 * 2**22) / 2.0**22)))
TURN += (float(np.float32(TWO_PI - TURN[0] - TURN[1])),)
ROUND = 1.5 * 2.0**23
PI_IN = 3.1415925


def rotary_tables(nc, tag, k, positions, g_q, g_k, k_rope, tab, k_rot, k_ss, at):
    mem = Memory(nc, at, 229344)
    H = ROPE // 2
    pos_i, pos = mem(f"{tag}_pos_i", [P, NS], I32), mem(f"{tag}_pos", [P, NS])
    freq, gq, gk = mem(f"{tag}_freq", [P, H]), mem(f"{tag}_gq", [P, ROPE]), mem(f"{tag}_gk", [P, ROPE])
    ang, turns, a, b, c, cos, sin = (mem(f"{tag}_{n}", [P, NS, H]) for n in ("ang", "turns", "a", "b", "c", "cos", "sin"))
    sq = mem(f"{tag}_sq", [P, NS, ROPE])
    kg = mem(f"{tag}_kg", [P, NS, ROPE])
    with Phase(nc) as ctx:
        loaded, done, sines = (ctx.semaphore(f"{tag}_{n}") for n in ("loaded", "done", "sines"))
        block = ctx.enter_context(nc.Block())
        count, angles_ready = [0], []

        @block.sync
        def _(sp):
            with nc.allow_non_contiguous_dma("positions"):
                sp.dma_start(pos_i[:], positions.rearrange("b (t p) -> p (b t)", p=P)).then_inc(loaded, 16)
            sp.dma_start(gq[:], g_q[NOPE:QK].partition_broadcast(P)).then_inc(loaded, 16)
            sp.dma_start(gk[:], g_k[NOPE:QK].partition_broadcast(P)).then_inc(loaded, 16)

        @block.vector
        def _(dve):
            def then(ins):
                count[0] += 1
                ins.then_inc(done, 1)
                dve.wait_ge(done, count[0])

            for i in range(H):
                last = dve.memset(freq[:, i:i + 1], float(np.float32(THETA) ** np.float32(-i / H)))
            then(last)
            dve.wait_ge(loaded, 48)
            then(dve.tensor_copy(pos[:], pos_i[:]))
            then(dve.tensor_tensor(ang[:], wide(pos[:], NS, H), rows_of(freq[:], NS, H), ALU.mult))
            then(dve.tensor_scalar(turns[:], ang[:], 1.0 / TWO_PI, ROUND, ALU.mult, ALU.add))
            then(dve.tensor_scalar(turns[:], turns[:], ROUND, None, ALU.subtract))
            for part in TURN:
                then(dve.scalar_tensor_tensor(ang[:], turns[:], -part, ang[:], ALU.mult, ALU.add))
            then(dve.tensor_scalar(a[:], ang[:], PI_IN, -PI_IN, ALU.min, ALU.max))
            then(dve.tensor_scalar(b[:], ang[:], TWO_PI / 4, None, ALU.add))
            then(dve.tensor_scalar(c[:], b[:], TWO_PI / 2, -TWO_PI, ALU.is_gt, ALU.mult))
            then(dve.tensor_tensor(b[:], b[:], c[:], ALU.add))
            then(dve.tensor_scalar(b[:], b[:], PI_IN, -PI_IN, ALU.min, ALU.max))
            angles_ready.append(count[0])
            dve.wait_ge(sines, 2)
            for n, (g, f) in enumerate(((0, cos), (1, sin), (1, cos), (0, sin))):
                dve.tensor_tensor(tab[n][:], f[:], rows_of(gq[:, g * H:(g + 1) * H], NS, H), ALU.mult)
            then(dve.tensor_tensor(sq[:], k_rope[:], k_rope[:], ALU.mult))
            dve.tensor_reduce(k_ss[:], sq[:], AX, ALU.add)
            then(dve.tensor_tensor(kg[:], k_rope[:], rows_of(gk[:], NS, ROPE), ALU.mult))
            for first, second, op, out in ((cos, sin, ALU.subtract, 0), (sin, cos, ALU.add, H)):
                then(dve.tensor_tensor(a[:], kg[:, :, 0:H], first[:], ALU.mult))
                then(dve.tensor_tensor(b[:], kg[:, :, H:ROPE], second[:], ALU.mult))
                then(dve.tensor_tensor(k_rot[:, :, out:out + H], a[:], b[:], op))

        @block.scalar
        def _(act):
            act.wait_ge(done, angles_ready[0])
            act.activation(sin[:], a[:], ACT.Sin).then_inc(sines, 1)
            act.activation(cos[:], b[:], ACT.Sin).then_inc(sines, 1)


def latent_heads(nc, tag, k, w_q_up, w_kv_up, g_q, g_k, cq, ckv, tab, k_rot, k_ss, at, psum, ot_dram):
    mem = Memory(nc, at, 229344)
    low = Memory(nc, HT_AT, CONST_AT)
    NQ, NK = Q_RANK // P, KV_RANK // P
    QW, KW = 2 * QK, 2 * (NOPE + HD)
    G = NS * 2
    wq = {n: mem(f"{tag}_wq_{n}", [P, NQ, QW], F32 if n == "raw" else F32R) for n in ("raw", "hi", "lo")}
    wk = {n: mem(f"{tag}_wk_{n}", [P, NK, KW], F32 if n == "raw" else F32R) for n in ("raw", "hi", "lo")}
    q32, k32, sq = mem(f"{tag}_q32", [P, G, QK]), mem(f"{tag}_k32", [P, G, QK]), mem(f"{tag}_sq", [P, G, QK])
    qt = {n: mem(f"{tag}_qt_{n}", [QK, 2, S], F32R) for n in ("hi", "lo")}
    kt = {n: mem(f"{tag}_kt_{n}", [QK, 2, S], F32R) for n in ("hi", "lo")}
    ss, std, rstd = (mem(f"{tag}_{n}", [P, 2, G]) for n in ("ss", "std", "rstd"))
    gcol = mem(f"{tag}_gcol", [QK, 2])
    v = low(f"{tag}_v", [P, NS, 2, 2 * HD], F32R)
    H = ROPE // 2
    ra, rb, rc, rd = (low(f"{tag}_{n}", [P, G, H]) for n in ("ra", "rb", "rc", "rd"))
    q_rows, k_rows = w_q_up.rearrange("(c p) n -> p c n", p=P), w_kv_up.rearrange("(c p) n -> p c n", p=P)
    turns = [(a, h, half) for a in range(2) for h in range(2) for half in range(2)]
    with Phase(nc) as ctx:
        def scores(pe, h, tile, out):
            rows, keys = slice(tile * P, (tile + 1) * P), (tile + 1) * P
            for at_key in range(0, keys, HALF):
                cols = slice(at_key, min(at_key + HALF, keys))
                product3(pe, out[:, cols], qt["hi"][:, h, rows], qt["lo"][:, h, rows],
                         kt["hi"][:, h, cols], kt["lo"][:, h, cols], True, cols.stop < keys)
            return pe.matmul(out[:, rows], k["ident_r"][:], k["causal"][:], start=False, stop=True, skip_group_check=True)

        turn = [0]
        at_ = Attend(nc, ctx, f"{tag}a", low, psum, k, [(h, half) for h in range(2) for half in range(2)],
                     lambda tile: (tile + 1) * P, lambda half: 4 * half + 4, True, scores,
                     lambda h, j: v[:, j, h, :], float(QK) ** -0.5,
                     lambda h, half: ot_dram[bass.ds(turn[0] * P + h * HD, HD), half * HALF:(half + 1) * HALF])
        sem = lambda n: ctx.semaphore(f"{tag}_{n}")
        (g_in, wq_in, wk_in, wq_hi, wk_hi, wq_lo, wk_lo, made, v_hi, q_out, k_out, q_sq, k_sq, sums, root, inverse,
         q_norm, k_norm, k_rope_done, rot_dve, rot_pool, q_rot, turned, t_hi, t_split, ones) = (
            sem(n) for n in ("g_in", "wq_in", "wk_in", "wq_hi", "wk_hi", "wq_lo", "wk_lo", "made", "v_hi", "q_out",
                             "k_out", "q_sq", "k_sq", "sums", "root", "inverse", "q_norm", "k_norm", "k_rope_done",
                             "rot_dve", "rot_pool", "q_rot", "turned", "t_hi", "t_split", "ones"))
        block = ctx.enter_context(nc.Block())
        q4 = q32[:].rearrange("p (t h) d -> p t h d", h=2)
        x1, x2 = q4[:, :, :, NOPE:NOPE + H], q4[:, :, :, NOPE + H:QK]
        four = lambda tile: tile[:].rearrange("p (t h) d -> p t h d", h=2)
        table = lambda n: tab[n][:].unsqueeze(2).broadcast_to([P, NS, 2, H])

        @block.sync
        def _(sp):
            def load(g):
                sp.dma_start(wq["raw"][:], q_rows[:, :, bass.ds(g * QW, QW)]).then_inc(wq_in, 16)
                sp.dma_start(wk["raw"][:], k_rows[:, :, bass.ds(g * KW, KW)]).then_inc(wk_in, 16)

            at_.begin(sp)
            for s in (sums, turned):
                sp.sem_inc(s, 1)
            sp.wait_ge(ones, 1)
            with nc.allow_non_contiguous_dma("gains"):
                sp.dma_start(gcol[0:NOPE, 0:1], g_q[0:NOPE].unsqueeze(1)).then_inc(g_in, 16)
                sp.dma_start(gcol[0:NOPE, 1:2], g_k[0:NOPE].unsqueeze(1)).then_inc(g_in, 16)
            load(0)
            with sp.Fori(0, PAIRS - 1) as g:
                sp.wait_ge(wq_lo, g + 1)
                sp.wait_ge(wk_lo, g + 1)
                load(g + 1)
                turn[0] = g
                at_.sync(sp, g)
            turn[0] = PAIRS - 1
            at_.sync(sp, PAIRS - 1)
            at_.finish(sp, PAIRS)

        @block.gpsimd
        def _(pool):
            with pool.Fori(0, PAIRS) as g:
                for w, hi, lo in ((wq, wq_hi, wq_lo), (wk, wk_hi, wk_lo)):
                    pool.wait_ge(hi, g + 1)
                    pool.tensor_tensor(w["lo"][:], w["raw"][:], as_f32(w["hi"][:]), ALU.subtract).then_inc(lo, 1)
                pool.wait_ge(k_out, 4 * (g + 1))
                pool.wait_ge(sums, 1 + 2 * g)
                pool.tensor_tensor(sq[:, :, 0:NOPE], k32[:, :, 0:NOPE], k32[:, :, 0:NOPE], ALU.mult).then_inc(k_sq, 1)
                pool.wait_ge(inverse, g + 1)
                pool.wait_ge(turned, 1 + 8 * g)
                pool.tensor_tensor(k32[:, :, NOPE:QK].rearrange("p (t h) d -> p t h d", h=2),
                                   k_rot[:].unsqueeze(2).broadcast_to([P, NS, 2, ROPE]),
                                   rstd[:, 1, :].rearrange("p (t h) -> p t h", h=2).unsqueeze(3).broadcast_to([P, NS, 2, ROPE]),
                                   ALU.mult).then_inc(k_rope_done, 1)
                pool.wait_ge(q_norm, g + 1)
                pool.tensor_tensor(four(rc), x2, table(2), ALU.mult).then_inc(rot_pool, 1)
                pool.tensor_tensor(four(rd), x1, table(3), ALU.mult).then_inc(rot_pool, 1)
                pool.wait_ge(rot_pool, 2 * g + 2)
                pool.wait_ge(rot_dve, 2 * g + 2)
                pool.tensor_tensor(x2, four(rc), four(rd), ALU.add).then_inc(q_rot, 1)

        @block.scalar
        def _(act):
            act.wait_ge(g_in, 32)
            with act.Fori(0, PAIRS) as g:
                act.wait_ge(wq_in, 16 * (g + 1))
                act.activation(wq["hi"][:], wq["raw"][:], ACT.Copy).then_inc(wq_hi, 1)
                act.wait_ge(wk_in, 16 * (g + 1))
                act.activation(wk["hi"][:], wk["raw"][:], ACT.Copy).then_inc(wk_hi, 1)
                for b in range(4):
                    act.wait_ge(made, 8 * g + b + 1)
                    act.activation(q32[:, 4 * b:4 * b + 4, :], psum[b][:, 0:2 * QW].rearrange("p (g d) -> p g d", d=QK),
                                   ACT.Copy).then_inc(q_out, 1)
                for b in range(4):
                    act.wait_ge(k_out, 4 * g + b + 1)
                    act.activation(v[:, 2 * b:2 * b + 2, :, 0:HD].rearrange("p t h d -> p (t h) d"),
                                   psum[4 + b][:].rearrange("p (g d) -> p g d", d=NOPE + HD)[:, :, NOPE:],
                                   ACT.Copy).then_inc(v_hi, 1)
                act.wait_ge(q_out, 4 * (g + 1))
                act.wait_ge(sums, 1 + 2 * g + 1)
                act.activation(sq[:], q32[:], ACT.Square).then_inc(q_sq, 1)
                act.wait_ge(sums, 1 + 2 * g + 2)
                act.activation(std[:], ss[:], ACT.Sqrt, bias=k["eps"][:, 0:1], scale=1.0 / QK).then_inc(root, 1)
                for n, (a, h, half) in enumerate(turns):
                    act.wait_ge(turned, 1 + 8 * g + n + 1)
                    act.activation((qt, kt)[a]["hi"][:, h, half * HALF:(half + 1) * HALF], psum[n][0:QK, :], ACT.Copy,
                                   scale=gcol[:, a:a + 1]).then_inc(t_hi, 1)
                at_.act(act, g)

        @block.vector
        def _(dve):
            dve.memset(gcol[:], 1.0).then_inc(ones, 1)
            with dve.Fori(0, PAIRS) as g:
                for b in range(4):
                    dve.wait_ge(made, 8 * g + 4 + b + 1)
                    kv = psum[4 + b][:].rearrange("p (g d) -> p g d", d=NOPE + HD)
                    dve.tensor_copy(k32[:, 4 * b:4 * b + 4, 0:NOPE], kv[:, :, 0:NOPE]).then_inc(k_out, 1)
                    dve.wait_ge(v_hi, 4 * g + b + 1)
                    vt = v[:, 2 * b:2 * b + 2, :, :].rearrange("p t h d -> p (t h) d")
                    dve.tensor_tensor(vt[:, :, HD:], kv[:, :, NOPE:], as_f32(vt[:, :, 0:HD]), ALU.subtract)
                dve.wait_ge(k_sq, g + 1)
                dve.tensor_reduce(ss[:, 1, :], sq[:, :, 0:NOPE], AX, ALU.add).then_inc(sums, 1)
                dve.wait_ge(sums, 1 + 2 * g + 1)
                ks = ss[:, 1, :].rearrange("p (t h) -> p t h", h=2)
                dve.tensor_tensor(ks, ks, k_ss[:].unsqueeze(2).broadcast_to([P, NS, 2]), ALU.add)
                dve.wait_ge(q_sq, g + 1)
                dve.tensor_reduce(ss[:, 0, :], sq[:], AX, ALU.add).then_inc(sums, 1)
                dve.wait_ge(root, g + 1)
                dve.reciprocal(rstd[:], std[:]).then_inc(inverse, 1)
                dve.wait_ge(inverse, g + 1)
                dve.tensor_tensor(q32[:], q32[:], wide(rstd[:, 0, :], G, QK), ALU.mult).then_inc(q_norm, 1)
                dve.tensor_tensor(k32[:, :, 0:NOPE], k32[:, :, 0:NOPE], wide(rstd[:, 1, :], G, NOPE), ALU.mult).then_inc(k_norm, 1)
                dve.wait_ge(q_norm, g + 1)
                dve.tensor_tensor(four(ra), x1, table(0), ALU.mult).then_inc(rot_dve, 1)
                dve.tensor_tensor(four(rb), x2, table(1), ALU.mult).then_inc(rot_dve, 1)
                dve.wait_ge(rot_dve, 2 * g + 2)
                dve.wait_ge(rot_pool, 2 * g + 2)
                dve.tensor_tensor(x1, four(ra), four(rb), ALU.subtract).then_inc(q_rot, 1)
                for n, (a, h, half) in enumerate(turns):
                    dve.wait_ge(t_hi, 8 * g + n + 1)
                    cols = slice(half * HALF, (half + 1) * HALF)
                    t = (qt, kt)[a]
                    dve.scalar_tensor_tensor(t["lo"][:, h, cols], psum[n][0:QK, :], gcol[:, a:a + 1],
                                             as_f32(t["hi"][:, h, cols]), ALU.mult, ALU.subtract).then_inc(t_split, 1)
                at_.dve(dve, g)

        @block.tensor
        def _(pe):
            with pe.Fori(0, PAIRS) as g:
                pe.wait_ge(at_.out_done, 1 + 4 * g)
                pe.wait_ge(wq_lo, g + 1)
                for t in range(NS):
                    rows = slice(t * P, (t + 1) * P)
                    for c in range(NQ):
                        last = product3(pe, psum[t // 2][:, (t % 2) * QW:(t % 2 + 1) * QW], cq["hi"][:, c, rows],
                                        cq["lo"][:, c, rows], wq["hi"][:, c, :], wq["lo"][:, c, :], c == 0, c == NQ - 1)
                    if t % 2:
                        last.then_inc(made, 1)
                pe.wait_ge(wk_lo, g + 1)
                for t in range(NS):
                    rows = slice(t * P, (t + 1) * P)
                    for c in range(NK):
                        last = product3(pe, psum[4 + t // 2][:, (t % 2) * KW:(t % 2 + 1) * KW], ckv["hi"][:, c, rows],
                                        ckv["lo"][:, c, rows], wk["hi"][:, c, :], wk["lo"][:, c, :], c == 0, c == NK - 1)
                    if t % 2:
                        last.then_inc(made, 1)
                pe.wait_ge(q_rot, 2 * g + 2)
                pe.wait_ge(k_norm, g + 1)
                pe.wait_ge(k_rope_done, g + 1)
                for n, (a, h, half) in enumerate(turns):
                    src = (q32, k32)[a]
                    for i in range(4):
                        last = pe.transpose(psum[n][0:QK, i * P:(i + 1) * P], src[:, 2 * (4 * half + i) + h, :], k["ident"][:])
                    last.then_inc(turned, 1)
                pe.wait_ge(t_split, 8 * g + 8)
                at_.pe(pe, g)


def build(nc, a, out):
    with ExitStack() as ctx:
        banks = ctx.enter_context(nc.psum_tensor("banks", [P, 8, HALF], F32))
        psum = {b: banks[:, b, :] for b in range(8)}
        psum["pair"] = [banks[:, 2 * i:2 * i + 2, :].rearrange("p a b -> p (a b)") for i in range(2)]
        x_mid = nc.dram_tensor("x_mid", (S, D), F32, kind="Internal").ap()
        ot_dram = nc.dram_tensor("attention_out_t", (D, S), F32, kind="Internal").ap()

        k, mem = {}, Memory(nc, CONST_AT, WORK_AT)
        for n, dt in (("ident", F32), ("ident_r", F32R), ("strict", F32R), ("causal", F32R), ("upper", F32R), ("lower", F32R)):
            k[n] = mem(n, [P, P], dt)
        k["eps"] = mem("eps", [P, 1])
        mem = Memory(nc, WORK_AT, X_AT)
        for n in ("strict", "causal", "upper", "lower"):
            k["tmp_" + n] = mem("tmp_" + n, [P, P])
        make_constants(nc, k)
        mem = Memory(nc, HT_AT, CONST_AT)
        ht = {h: mem(f"ht_{h}", [P, ND, S], F32R) for h in ("hi", "lo")}
        x = Memory(nc, X_AT, 229344)("x", [P, NS, D])

        for layer in range(DEPTH):
            tag = f"l{layer}"
            x_dram = a["x"].rearrange("b s d -> (b s) d") if layer == 0 else x_mid
            norm_transposed(nc, f"{tag}n", k, x, x_dram if layer == 0 else None, a["ln_attn"][layer], ht, psum)
            w_in = (a["sb_w_in"] if layer == 0 else a["mla_w_in"])[0]
            q_mem_at = w_in.shape[1] - MEM_Q
            memory_heads(nc, f"{tag}m", k, a["mem"][0], a["ln_mem"][layer], a["w_mem_kv"][layer], a["g_qn_mem"][layer],
                         a["g_kn_mem"][layer], w_in[:, q_mem_at:], ht, psum, ot_dram)
            if layer == 0:
                stick_breaking(nc, f"{tag}s", k, w_in, ht, psum, ot_dram)
            else:
                mem = Memory(nc, WORK_AT, 229344)
                cq = {h: mem(f"cq_{h}", [P, Q_RANK // P, S], F32R) for h in ("hi", "lo")}
                ckv = {h: mem(f"ckv_{h}", [P, KV_RANK // P, S], F32R) for h in ("hi", "lo")}
                k_rope, k_rot = mem("k_rope", [P, NS, ROPE]), mem("k_rot", [P, NS, ROPE])
                tab = [mem(f"rope_tab{n}", [P, NS, ROPE // 2]) for n in range(4)]
                k_ss = mem("k_ss", [P, NS])
                down_project(nc, f"{tag}q", k, w_in[:, 0:Q_RANK], Q_RANK, Q_RANK, a["mla_q_norm"][0], ht, cq, None,
                             mem.at, psum)
                down_project(nc, f"{tag}c", k, w_in[:, Q_RANK:q_mem_at], KV_RANK + ROPE, KV_RANK, a["mla_kv_norm"][0],
                             ht, ckv, k_rope, mem.at, psum)
                rotary_tables(nc, f"{tag}r", k, a["positions"], a["mla_g_qn"][0], a["mla_g_kn"][0], k_rope, tab, k_rot,
                              k_ss, mem.at)
                latent_heads(nc, f"{tag}a", k, a["mla_w_q_up"][0], a["mla_w_kv_up"][0], a["mla_g_qn"][0],
                             a["mla_g_kn"][0], cq, ckv, tab, k_rot, k_ss, mem.at, psum, ot_dram)
            project_out(nc, f"{tag}o", x, x_dram, ot_dram, a["w_out"][layer], ht, psum)
            norm_transposed(nc, f"{tag}f", k, x, None, a["ln_ffn"][layer], ht, psum)
            swiglu(nc, f"{tag}g", k, x, ht, a["w_ffn_gu"][layer], a["w_ffn_down"][layer], psum,
                   x_mid if layer == 0 else out.rearrange("b s d -> (b s) d"))


_INS = ["x", "mem", "positions", "ln_attn", "w_out", "ln_mem", "w_mem_kv", "g_qn_mem", "g_kn_mem", "ln_ffn", "w_ffn_gu",
        "w_ffn_down", "sb_w_in", "mla_w_in", "mla_q_norm", "mla_w_q_up", "mla_kv_norm", "mla_w_kv_up", "mla_g_qn",
        "mla_g_kn"]


def kernel(**inputs):
    import numpy as _np
    import concourse.bacc as _bacc
    from concourse import mybir as _mybir
    from concourse.bass_utils import run_bass_kernel_spmd as _run

    nc = _bacc.Bacc("TRN2", target_bir_lowering=False, num_devices=1)
    arrays, args = {}, {}
    for name in _INS:
        v = _np.ascontiguousarray(inputs[name])
        arrays[f"in_{name}_dram"] = v
        args[name] = nc.dram_tensor(f"in_{name}_dram", v.shape, _mybir.dt.from_np(v.dtype), kind="ExternalInput").ap()
    out = nc.dram_tensor("out_0_dram", (1, S, D), F32, kind="ExternalOutput").ap()
    build(nc, args, out)
    r = _run(nc, [arrays], core_ids=[0])
    return r.results[0]["out_0_dram"]
```

```python
from contextlib import ExitStack

import concourse.bass as bass
import numpy as np
from concourse import mybir

P = 128
F32 = mybir.dt.float32
F32R = mybir.dt.float32r
I32 = mybir.dt.int32
ALU = mybir.AluOpType
ACT = mybir.ActivationFunctionType
AX = mybir.AxisListType.X

D = 1024
S = 1024
ND, NS = D // P, S // P
HALF = 512
DEPTH = 2
HD = 64
HEADS = 12
PAIRS = HEADS // 2
NOPE, ROPE = 64, 32
QK = NOPE + ROPE
Q_RANK, KV_RANK = 768, 256
MEM, MEM_HEADS = 256, 4
MEM_Q = MEM_HEADS * HD
FF = 2816
NF = FF // P
SB_Q = HEADS * HD
EPS = 1e-6
THETA = 10000.0
MASKED = -1e30

BASE = 16512
HT_AT = BASE
CONST_AT = HT_AT + 2 * ND * S * 4
WORK_AT = CONST_AT + 5 * 1024
X_AT = 229344 - NS * D * 4


class Memory:

    def __init__(self, nc, at, end):
        self.nc, self.at, self.end = nc, at, end

    def __call__(self, name, shape, dtype=F32):
        size = int(np.prod(shape[1:])) * 4
        t = self.nc.alloc_sbuf_tensor_at(name, shape, dtype, offset=self.at)
        self.at += (size + 31) // 32 * 32
        assert self.at <= self.end, (name, self.at, self.end)
        return t


class Phase(ExitStack):

    def __init__(self, nc):
        super().__init__()
        self.nc, self.semaphores = nc, []

    def semaphore(self, name):
        self.semaphores.append(self.nc.alloc_semaphore(name))
        return self.semaphores[-1]

    def __exit__(self, *exc):
        super().__exit__(*exc)
        if exc[0] is None:
            self.nc.clear_and_free_semaphores(self.semaphores)
            self.nc.all_engine_barrier()


def as_f32(ap):
    return ap.bitcast(F32)


def product3(pe, out, l_hi, l_lo, r_hi, r_lo, first, last):
    pe.matmul(out, l_hi, r_hi, start=first, stop=False, skip_group_check=True)
    pe.matmul(out, l_hi, r_lo, start=False, stop=False, skip_group_check=True)
    return pe.matmul(out, l_lo, r_hi, start=False, stop=last, skip_group_check=True)


def make_constants(nc, k):
    with Phase(nc) as ctx:
        made = ctx.semaphore("const_made")
        filled = ctx.semaphore("const_filled")
        t = [k["ident"], k["tmp_strict"], k["tmp_causal"], k["tmp_upper"], k["tmp_lower"]]
        block = ctx.enter_context(nc.Block())

        @block.gpsimd
        def _(pool):
            for m, v in zip(t, (0.0, 0.0, 0.0, -1.0, -1.0)):
                pool.memset(m[:], v).then_inc(filled, 1)
            pool.wait_ge(filled, 5)
            pool.affine_select(out=t[0][:], in_=t[0][:], compare_op=ALU.not_equal, fill=1.0, base=0,
                               pattern=[[-1, P]], channel_multiplier=1).then_inc(made, 1)
            pool.affine_select(out=t[1][:], in_=t[1][:], compare_op=ALU.is_gt, fill=MASKED, base=0,
                               pattern=[[1, P]], channel_multiplier=-1).then_inc(made, 1)
            pool.affine_select(out=t[2][:], in_=t[2][:], compare_op=ALU.is_ge, fill=MASKED, base=0,
                               pattern=[[-1, P]], channel_multiplier=1).then_inc(made, 1)
            pool.affine_select(out=t[3][:], in_=t[3][:], compare_op=ALU.is_ge, fill=0.0, base=0,
                               pattern=[[-1, P]], channel_multiplier=1).then_inc(made, 1)
            pool.affine_select(out=t[4][:], in_=t[4][:], compare_op=ALU.is_gt, fill=0.0, base=0,
                               pattern=[[1, P]], channel_multiplier=-1).then_inc(made, 1)

        @block.vector
        def _(dve):
            dve.wait_ge(made, 5)
            dve.memset(k["eps"][:], EPS)
            for name, src in (("ident_r", t[0]), ("strict", t[1]), ("causal", t[2]),
                              ("upper", t[3]), ("lower", t[4])):
                dve.tensor_copy(k[name][:], src[:])


def gain_columns(gain):
    return gain.rearrange("(c p) -> p c", p=P)


def norm_transposed(nc, tag, k, x, x_dram, gain, ht, psum, save_to=None):
    nt = x.shape[1]
    mem = Memory(nc, WORK_AT, X_AT)
    xn = mem(f"{tag}_xn", [P, nt, D])
    junk = mem(f"{tag}_junk", [P, D])
    ss = mem(f"{tag}_ss", [P, nt])
    std = mem(f"{tag}_std", [P, nt])
    rstd = mem(f"{tag}_rstd", [P, nt])
    gcol = mem(f"{tag}_gcol", [P, ND])
    group = min(nt, 4)
    banks = [(g, c) for g in range(nt // group) for c in range(ND)]
    with Phase(nc) as ctx:
        sem = lambda n: ctx.semaphore(f"{tag}_{n}")
        x_in = [sem(f"x_in{i}") for i in range(nt)] if x_dram is not None else None
        g_in, squared, root, scale_ready = sem("g_in"), sem("squared"), sem("root"), sem("scale_ready")
        normed, turned, hi_done, lo_done, saved = (
            sem("normed"), sem("turned"), sem("hi_done"), sem("lo_done"), sem("saved"))
        block = ctx.enter_context(nc.Block())

        @block.sync
        def _(sp):
            if x_dram is not None:
                for t in range(nt):
                    sp.dma_start(x[:, t, :], x_dram[t * P:(t + 1) * P, :]).then_inc(x_in[t], 16)
            with nc.allow_non_contiguous_dma("gain"):
                sp.dma_start(gcol[:], gain_columns(gain)).then_inc(g_in, 16)
            if save_to is not None:
                for t in range(nt):
                    sp.dma_start(save_to[t * P:(t + 1) * P, :], x[:, t, :]).then_inc(saved, 16)
                sp.wait_ge(saved, 16 * nt)

        @block.scalar
        def _(act):
            for t in range(nt):
                if x_dram is not None:
                    act.wait_ge(x_in[t], 16)
                if t:
                    act.wait_ge(squared, t)
                act.activation(junk[:], x[:, t, :], ACT.Square, accum_out=ss[:, t:t + 1]).then_inc(squared, 1)
            act.wait_ge(squared, nt)
            act.activation(std[:], ss[:], ACT.Sqrt, bias=k["eps"][:, 0:1], scale=1.0 / D).then_inc(root, 1)
            act.wait_ge(g_in, 16)
            for n, (g, c) in enumerate(banks):
                act.wait_ge(turned, n + 1)
                cols = slice(g * group * P, (g + 1) * group * P)
                act.activation(ht["hi"][:, c, cols], psum[n % 4][:, 0:group * P], ACT.Copy,
                               scale=gcol[:, c:c + 1]).then_inc(hi_done, 1)

        @block.vector
        def _(dve):
            dve.wait_ge(root, 1)
            dve.reciprocal(rstd[:], std[:]).then_inc(scale_ready, 1)
            dve.wait_ge(scale_ready, 1)
            for t in range(nt):
                dve.tensor_scalar(xn[:, t, :], x[:, t, :], rstd[:, t:t + 1], None, ALU.mult).then_inc(normed, 1)
            for n, (g, c) in enumerate(banks):
                dve.wait_ge(hi_done, n + 1)
                cols = slice(g * group * P, (g + 1) * group * P)
                dve.scalar_tensor_tensor(ht["lo"][:, c, cols], psum[n % 4][:, 0:group * P], gcol[:, c:c + 1],
                                         as_f32(ht["hi"][:, c, cols]), ALU.mult, ALU.subtract).then_inc(lo_done, 1)

        @block.tensor
        def _(pe):
            for n, (g, c) in enumerate(banks):
                pe.wait_ge(normed, (g + 1) * group)
                if n >= 4:
                    pe.wait_ge(lo_done, n - 3)
                for i in range(group):
                    last = pe.transpose(psum[n % 4][:, i * P:(i + 1) * P],
                                        xn[:, g * group + i, c * P:(c + 1) * P], k["ident"][:])
                last.then_inc(turned, 1)




def project_and_swiglu(nc, tag, k, x, x_dram, ot_dram, w_out, gain, w_gu, w_down, ht, psum, store_to):
    KB = 1024
    def place(name, at, shape, dtype=F32):
        return Memory(nc, WORK_AT + at * KB, X_AT)(f"{tag}_{name}", shape, dtype)

    gu_raw = [place(f"gu_raw{s}", 8 * s, [P, ND, 2, P]) for s in range(2)]
    gu_hi = [place(f"gu_hi{s}", 16 + 16 * s, [P, ND, 2, P], F32R) for s in range(2)]
    gu_lo = [place(f"gu_lo{s}", 24 + 16 * s, [P, ND, 2, P], F32R) for s in range(2)]
    dn_raw = [place(f"dn_raw{s}", 48 + 4 * s, [P, D]) for s in range(2)]
    dn_hi = [place(f"dn_hi{s}", 56 + 8 * s, [P, D], F32R) for s in range(2)]
    dn_lo = [place(f"dn_lo{s}", 60 + 8 * s, [P, D], F32R) for s in range(2)]
    a_hi = [place(f"a_hi{s}", 72 + 8 * s, [P, S], F32R) for s in range(2)]
    a_lo = [place(f"a_lo{s}", 76 + 8 * s, [P, S], F32R) for s in range(2)]
    hidden = place("hidden", 92, [P, 2, HALF])
    gate = place("gate", 100, [P, 2, HALF])
    w_raw = [place(f"w_raw{s}", 4 * s, [P, D]) for s in range(2)]
    o_raw = [place(f"o_raw{s}", 8 + 4 * s, [P, S]) for s in range(3)]
    w_hi = [place(f"w_hi{c}", 20 + 8 * c, [P, D], F32R) for c in range(ND)]
    w_lo = [place(f"w_lo{c}", 24 + 8 * c, [P, D], F32R) for c in range(ND)]
    xn = place("xn", 84, [P, 4, D])
    junk = place("junk", 100, [P, D])
    small = Memory(nc, WORK_AT + 104 * KB, X_AT)
    ss, std, rstd = (small(f"{tag}_{n}", [P, NS]) for n in ("ss", "std", "rstd"))
    gcol = small(f"{tag}_gcol", [P, ND])
    ot = ht
    gu_rows = w_gu.rearrange("(c p) f -> p c f", p=P)
    outs = [(t, n) for t in range(NS) for n in range(D // HALF)]
    NOUT = len(outs)
    four = lambda g: slice(4 * g, 4 * g + 4)
    group = lambda g: slice(g * HALF, (g + 1) * HALF)
    mix_bank = lambda n: n if n < 8 else n - 8
    norm_bank = lambda g, c: 4 * g + c % 4
    with Phase(nc) as ctx:
        sem = lambda n: ctx.semaphore(f"{tag}_{n}")
        x_in = [sem(f"x_in{t}") for t in range(NS)]
        w_in, o_in = [sem(f"w_in{s}") for s in range(2)], [sem(f"o_in{s}") for s in range(3)]
        (g_in, w_hi_done, w_lo_done, o_hi_done, o_lo_done, w_used, made, mixed, squared, root, inverse, normed, turned,
         hi_done, lo_done) = (
            sem(n) for n in ("g_in", "w_hi_done", "w_lo_done", "o_hi_done", "o_lo_done", "w_used", "made", "mixed",
                             "squared", "root", "inverse", "normed", "turned", "hi_done", "lo_done"))
        gu_in = [sem(f"gu_in{s}") for s in range(2)]
        dn_in = [sem(f"dn_in{s}") for s in range(2)]
        gu_hi_done, gu_lo_done, dn_hi_done, dn_lo_done = (
            sem("gu_hi_done"), sem("gu_lo_done"), sem("dn_hi_done"), sem("dn_lo_done"))
        gu_made, silu_done, hid_done, a_hi_done, a_lo_done, dn_made, added, stored = (
            sem("gu_made"), sem("silu_done"), sem("hid_done"), sem("a_hi_done"), sem("a_lo_done"),
            sem("dn_made"), sem("added"), sem("stored"))
        block = ctx.enter_context(nc.Block())

        def chunks(eng, step):
            for s in range(2):
                step(0, s, True, False)
            with eng.Fori(1, NF // 2 - 1) as i:
                for s in range(2):
                    step(i, s, False, False)
            for s in range(2):
                step(NF // 2 - 1, s, False, s == 1)

        def following(i, s):
            return (i, 1) if s == 0 else (i + 1, 0)

        @block.sync
        def _(sp):
            def load_gu(i, s):
                for half in range(2):
                    sp.dma_start(gu_raw[s][:, :, half, :],
                                 gu_rows[:, :, bass.ds((2 * i + s) * P + half * FF, P)]).then_inc(gu_in[s], 16)

            def load_dn(i, s):
                sp.dma_start(dn_raw[s][:], w_down[bass.ds((2 * i + s) * P, P), :]).then_inc(dn_in[s], 16)

            for c in range(ND):
                if c >= 2:
                    sp.wait_ge(w_lo_done, c - 1)
                sp.dma_start(w_raw[c % 2][:], w_out[c * P:(c + 1) * P, :]).then_inc(w_in[c % 2], 16)
                if c >= 3:
                    sp.wait_ge(o_lo_done, c - 2)
                sp.dma_start(o_raw[c % 3][:], ot_dram[c * P:(c + 1) * P, :]).then_inc(o_in[c % 3], 16)
            for t in range(NS):
                sp.dma_start(x[:, t, :], x_dram[t * P:(t + 1) * P, :]).then_inc(x_in[t], 16)
            with nc.allow_non_contiguous_dma("gain"):
                sp.dma_start(gcol[:], gain_columns(gain)).then_inc(g_in, 16)
            sp.wait_ge(w_lo_done, ND)
            sp.wait_ge(o_lo_done, ND)
            for s in range(2):
                load_gu(0, s)
            for s in range(2):
                sp.wait_ge(w_used, 4 + s)
                load_dn(0, s)
            with sp.Fori(1, NF // 2) as i:
                for s in range(2):
                    sp.wait_ge(gu_lo_done, 2 * i + s - 1)
                    sp.wait_ge(dn_lo_done, 2 * i + s - 1)
                    load_gu(i, s)
                    load_dn(i, s)
            for t in range(NS):
                sp.wait_ge(added, (NF - 1) * NOUT + 2 * (t + 1))
                sp.dma_start(store_to[t * P:(t + 1) * P, :], x[:, t, :]).then_inc(stored, 16)
            sp.wait_ge(stored, 16 * NS)

        @block.gpsimd
        def _(pool):
            def lower_gu(i, s):
                pool.wait_ge(gu_hi_done, 2 * i + s + 1)
                pool.tensor_tensor(gu_lo[s][:], gu_raw[s][:], as_f32(gu_hi[s][:]),
                                   ALU.subtract).then_inc(gu_lo_done, 1)

            def step(i, s, first, last):
                pool.wait_ge(dn_hi_done, 2 * i + s + 1)
                pool.tensor_tensor(dn_lo[s][:], dn_raw[s][:], as_f32(dn_hi[s][:]),
                                   ALU.subtract).then_inc(dn_lo_done, 1)
                if not last:
                    lower_gu(*following(i, s))

            for c in range(ND):
                pool.wait_ge(w_hi_done, c + 1)
                pool.tensor_tensor(w_lo[c][:], w_raw[c % 2][:], as_f32(w_hi[c][:]), ALU.subtract).then_inc(w_lo_done, 1)
            lower_gu(0, 0)
            chunks(pool, step)

        @block.scalar
        def _(act):
            def upper_gu(i, s, first):
                act.wait_ge(gu_in[s], 32 * (i + 1))
                if not first:
                    act.wait_ge(gu_made, 4 * (2 * i + s - 1))
                act.activation(gu_hi[s][:], gu_raw[s][:], ACT.Copy).then_inc(gu_hi_done, 1)

            def step(i, s, first, last):
                f = 2 * i + s
                act.wait_ge(dn_in[s], 16 * (i + 1))
                if not first:
                    act.wait_ge(dn_made, NOUT * (f - 1))
                act.activation(dn_hi[s][:], dn_raw[s][:], ACT.Copy).then_inc(dn_hi_done, 1)
                if not last:
                    upper_gu(*following(i, s), first and s == 0)
                for h in range(2):
                    act.wait_ge(gu_made, 4 * f + 2 * h + 1)
                    if not first or s:
                        act.wait_ge(hid_done, 2 * f + h - 1)
                    act.activation(gate[:, h, :], psum[2 * h][:], ACT.Silu).then_inc(silu_done, 1)
                    act.wait_ge(hid_done, 2 * f + h + 1)
                    act.activation(a_hi[s][:, h * HALF:(h + 1) * HALF], hidden[:, h, :],
                                   ACT.Copy).then_inc(a_hi_done, 1)

            def squares(t):
                act.wait_ge(mixed, 2 * (t + 1))
                if t:
                    act.wait_ge(squared, t)
                act.activation(junk[:], x[:, t, :], ACT.Square, accum_out=ss[:, t:t + 1]).then_inc(squared, 1)

            def deviations(g):
                act.wait_ge(squared, 4 * (g + 1))
                act.activation(std[:, four(g)], ss[:, four(g)], ACT.Sqrt, bias=k["eps"][:, 0:1],
                               scale=1.0 / D).then_inc(root, 1)

            def upper_normed(g, c):
                act.wait_ge(turned, ND * g + c + 1)
                act.activation(ht["hi"][:, c, group(g)], psum[norm_bank(g, c)][:], ACT.Copy,
                               scale=gcol[:, c:c + 1]).then_inc(hi_done, 1)

            for c in range(ND):
                act.wait_ge(w_in[c % 2], 16 * (c // 2 + 1))
                act.activation(w_hi[c][:], w_raw[c % 2][:], ACT.Copy).then_inc(w_hi_done, 1)
                act.wait_ge(o_in[c % 3], 16 * (c // 3 + 1))
                act.activation(ot["hi"][:, c, :], o_raw[c % 3][:], ACT.Copy).then_inc(o_hi_done, 1)
            for t in range(4):
                squares(t)
            deviations(0)
            for t in (4, 5):
                squares(t)
            act.wait_ge(g_in, 16)
            for c in range(ND):
                upper_normed(0, c)
                if c == 2:
                    act.wait_ge(w_used, 2)
                    upper_gu(0, 0, True)
            for t in (6, 7):
                squares(t)
            deviations(1)
            for c in range(ND):
                upper_normed(1, c)
            chunks(act, step)

        @block.vector
        def _(dve):
            def add(f):
                for n, (t, half) in enumerate(outs):
                    dve.wait_ge(dn_made, NOUT * f + n + 1)
                    cols = slice(half * HALF, (half + 1) * HALF)
                    dve.tensor_tensor(x[:, t, cols], psum[4 + n % 4][:], x[:, t, cols], ALU.add).then_inc(added, 1)

            def step(i, s, first, last):
                f = 2 * i + s
                for h in range(2):
                    dve.wait_ge(silu_done, 2 * f + h + 1)
                    dve.wait_ge(gu_made, 4 * f + 2 * h + 2)
                    if not first or s:
                        dve.wait_ge(a_lo_done, 2 * f + h - 1)
                    dve.tensor_tensor(hidden[:, h, :], psum[2 * h + 1][:], gate[:, h, :],
                                      ALU.mult).then_inc(hid_done, 1)
                    dve.wait_ge(a_hi_done, 2 * f + h + 1)
                    cols = slice(h * HALF, (h + 1) * HALF)
                    if not first:
                        dve.wait_ge(dn_made, NOUT * (f - 1))
                    dve.tensor_tensor(a_lo[s][:, cols], hidden[:, h, :], as_f32(a_hi[s][:, cols]),
                                      ALU.subtract).then_inc(a_lo_done, 1)
                if not first or s:
                    add(f - 1)

            def mix(tiles):
                for t in tiles:
                    dve.wait_ge(x_in[t], 16)
                    for half in range(2):
                        n, cols = 2 * t + half, slice(half * HALF, (half + 1) * HALF)
                        dve.wait_ge(made, n + 1)
                        dve.tensor_tensor(x[:, t, cols], psum[mix_bank(n)][:], x[:, t, cols], ALU.add).then_inc(mixed, 1)

            def normalise(g):
                dve.wait_ge(root, g + 1)
                dve.reciprocal(rstd[:, four(g)], std[:, four(g)]).then_inc(inverse, 1)
                dve.wait_ge(inverse, g + 1)
                for t in range(4 * g, 4 * g + 4):
                    dve.tensor_scalar(xn[:, t % 4, :], x[:, t, :], rstd[:, t:t + 1], None, ALU.mult).then_inc(normed, 1)

            def lower_normed(g):
                for c in range(ND):
                    dve.wait_ge(hi_done, ND * g + c + 1)
                    dve.scalar_tensor_tensor(ht["lo"][:, c, group(g)], psum[norm_bank(g, c)][:], gcol[:, c:c + 1],
                                             as_f32(ht["hi"][:, c, group(g)]), ALU.mult, ALU.subtract).then_inc(lo_done, 1)

            for c in range(ND):
                dve.wait_ge(o_hi_done, c + 1)
                dve.tensor_tensor(ot["lo"][:, c, :], o_raw[c % 3][:], as_f32(ot["hi"][:, c, :]),
                                  ALU.subtract).then_inc(o_lo_done, 1)
            mix((0, 1, 2, 3))
            normalise(0)
            mix((4, 5))
            lower_normed(0)
            mix((6, 7))
            normalise(1)
            lower_normed(1)
            chunks(dve, step)
            add(NF - 1)

        @block.tensor
        def _(pe):
            def gate_up(i, s, first, halves=(0, 1)):
                f = 2 * i + s
                pe.wait_ge(gu_lo_done, f + 1)
                for h in halves:
                    if not first:
                        pe.wait_ge(hid_done, 2 * f + h - 1)
                    for b in range(2):
                        for c in range(ND):
                            cols = slice(h * HALF, (h + 1) * HALF)
                            last = product3(pe, psum[2 * h + b][:], gu_hi[s][:, c, b, :], gu_lo[s][:, c, b, :],
                                            ht["hi"][:, c, cols], ht["lo"][:, c, cols], c == 0, c == ND - 1)
                        last.then_inc(gu_made, 1)

            def step(i, s, first, last_chunk):
                f = 2 * i + s
                if not last_chunk:
                    gate_up(*following(i, s), False)
                pe.wait_ge(dn_lo_done, f + 1)
                pe.wait_ge(a_lo_done, 2 * f + 2)
                for n, (t, half) in enumerate(outs):
                    if not (first and s == 0 and n < 4):
                        pe.wait_ge(added, NOUT * f + n - 3)
                    cols = slice(half * HALF, (half + 1) * HALF)
                    rows = slice(t * P, (t + 1) * P)
                    product3(pe, psum[4 + n % 4][:], a_hi[s][:, rows], a_lo[s][:, rows], dn_hi[s][:, cols],
                             dn_lo[s][:, cols], True, True).then_inc(dn_made, 1)

            def turn(g, c):
                n = ND * g + c
                pe.wait_ge(normed, 4 * (g + 1))
                if c < 4:
                    pe.wait_ge(mixed, 9 + c if g == 0 else 13 + c)
                else:
                    pe.wait_ge(lo_done, n - 3)
                for i in range(4):
                    last = pe.transpose(psum[norm_bank(g, c)][:, i * P:(i + 1) * P], xn[:, i, c * P:(c + 1) * P],
                                        k["ident"][:])
                last.then_inc(turned, 1)

            for wave, ns in enumerate((range(8), range(8, 12), range(12, 16))):
                for c in range(ND):
                    pe.wait_ge(w_lo_done, c + 1)
                    pe.wait_ge(o_lo_done, c + 1)
                    for n in ns:
                        t, half = n // 2, n % 2
                        if wave and c == 0:
                            pe.wait_ge(mixed, n - 7)
                        cols, rows = slice(half * HALF, (half + 1) * HALF), slice(t * P, (t + 1) * P)
                        last = product3(pe, psum[mix_bank(n)][:], ot["hi"][:, c, rows], ot["lo"][:, c, rows],
                                        w_hi[c][:, cols], w_lo[c][:, cols], c == 0, c == ND - 1)
                        if c == ND - 1:
                            last.then_inc(made, 1)
                    if wave == 2:
                        if c < ND - 1:
                            last.then_inc(w_used, 1)
                        turn(0, c)
            pe.wait_ge(lo_done, ND)
            gate_up(0, 0, True, (0,))
            for c in range(ND):
                turn(1, c)
            pe.wait_ge(lo_done, 2 * ND)
            gate_up(0, 0, True, (1,))
            chunks(pe, step)


class Attend:

    def __init__(self, nc, ctx, tag, mem, psum, k, jobs, keys_of, blocks_of, causal, scores, values, store,
                 rows_mem, ring, out_banks=(6, 7), plan=None, extras={}):
        self.nc, self.k, self.jobs, self.causal, self.ring = nc, k, jobs, causal, ring
        self.keys_of, self.blocks_of, self.scores, self.values, self.store = keys_of, blocks_of, scores, values, store
        self.p = [[rows_mem(f"{tag}_p{n}_{i}", [P, keys_of(4 * jobs[n][1] + i)]) for i in range(4)] for n in range(ring)]
        self.pt_hi = [mem(f"{tag}_pt_hi{s}", [P, HALF], F32R) for s in range(2)]
        self.pt_lo = [mem(f"{tag}_pt_lo{s}", [P, HALF], F32R) for s in range(2)]
        self.nmx, self.rsum, self.rinv = (mem(f"{tag}_{n}", [P, 4]) for n in ("nmx", "rsum", "rinv"))
        self.o_tmp = mem(f"{tag}_o_tmp", [HD, HALF])
        self.o_out = [mem(f"{tag}_o_out{s}", [HD, HALF]) for s in range(2)]
        self.s_ps = [psum["pair"][0], psum["pair"][1]]
        self.t_ps = [psum[4], psum[5]]
        self.o_ps = [psum[b] for b in out_banks]
        (self.scores_made, self.nmax_done, self.exp_done, self.inv_done, self.rows_done,
         self.turned, self.hi_done, self.split_done, self.pv_made, self.tmp_done, self.out_done) = (
            ctx.semaphore(f"{tag}_{n}") for n in (
                "scores_made", "nmax_done", "exp_done", "inv_done", "rows_done", "turned",
                "hi_done", "split_done", "pv_made", "tmp_done", "out_done"))
        self.stored = [ctx.semaphore(f"{tag}_stored{s}") for s in range(2)]
        self.ns, self.nj = 4 * len(jobs), len(jobs)
        self.first = [sum(blocks_of(half) for _, half in jobs[:n]) for n in range(len(jobs) + 1)]
        self.nt = self.first[-1]

        if plan is None:
            plan = [6] + [min(self.ns, 4 * n + 6 + 4 * (j + 1) // blocks_of(half)) for n, (h, half) in enumerate(jobs)
                          for j in range(blocks_of(half))]
        steps, made, exps, inverses, rows = [], 0, 0, 0, 0

        def score_up_to(count):
            nonlocal made
            while made < count:
                exp_up_to(made)
                row_up_to(made - 1)
                steps.append(("S", made // 4, made % 4))
                made += 1

        def exp_up_to(count):
            nonlocal exps
            while exps < count:
                steps.append(("P", exps // 4, exps % 4))
                exps += 1

        def inverse_up_to(count):
            nonlocal inverses
            exp_up_to(count)
            while inverses < count:
                steps.append(("I", inverses // 4, inverses % 4))
                inverses += 1

        def row_up_to(count):
            nonlocal rows
            inverse_up_to(count)
            while rows < count:
                steps.append(("R", rows // 4, rows % 4))
                rows += 1

        score_up_to(plan[0])
        row_up_to(plan[0])
        self.opening, steps = steps, []
        for n in range(self.nj):
            blocks = blocks_of(jobs[n][1])
            for j in range(blocks):
                tau = self.first[n] + j
                row_up_to(max(rows, 4 * n + 4))
                inverse_up_to(exps - 1)
                steps.append(("T", n, j, tau))
                if tau:
                    steps.append(("V",) + self.of(tau - 1))
                    if j == 0:
                        steps.append(("E", n - 1))
                exp_up_to(made)
                score_up_to(plan[tau + 1])
                steps += [("X", x) for x in extras.get(tau, ())]
        steps += [("V",) + self.of(self.nt - 1), ("E", self.nj - 1)]
        row_up_to(plan[-1])
        self.steps = steps
        self.closing = [s for s in steps if s[0] not in "SPIR" or s[1] < self.nj]

    def of(self, tau):
        n = max(m for m in range(self.nj) if self.first[m] <= tau)
        return n, tau - self.first[n], tau

    def columns(self, n, j):
        return max(0, j - 4 * self.jobs[n][1]) * P if self.causal else 0

    def pe(self, pe, steps, turn=0, extra=None):
        for kind, *step in steps:
            if kind == "S":
                n, i = step
                s, (h, half) = 4 * n + i, self.jobs[n % self.nj]
                if s >= 2:
                    pe.wait_ge(self.exp_done, turn * self.ns + s - 1)
                self.scores(pe, h, 4 * half + i, self.s_ps[s % 2]).then_inc(self.scores_made, 1)
            elif kind == "T":
                n, j, tau = step
                pe.wait_ge(self.rows_done, turn * self.ns + 4 * n + 4)
                if tau >= 2:
                    pe.wait_ge(self.split_done, turn * self.nt + tau - 1)
                for i in range(self.columns(n, j) // P, 4):
                    last = pe.transpose(self.t_ps[tau % 2][:, i * P:(i + 1) * P],
                                        self.p[n % self.ring][i][:, j * P:(j + 1) * P], self.k["ident"][:])
                last.then_inc(self.turned, 1)
            elif kind == "V":
                n, j, tau = step
                c0, h, o = self.columns(n, j), self.jobs[n][0], self.o_ps[n % len(self.o_ps)]
                pe.wait_ge(self.split_done, turn * self.nt + tau + 1)
                if j == 0:
                    pe.wait_ge(self.out_done, 1 + turn * self.nj + max(n + 1 - len(self.o_ps), 0))
                pe.matmul(o[:, c0:HALF], self.values(h, j), self.pt_hi[tau % 2][:, c0:HALF],
                          start=j == 0, stop=False, skip_group_check=True)
                pe.matmul(o[:, c0:HALF], self.values(h, j), self.pt_lo[tau % 2][:, c0:HALF], start=False,
                          stop=tau + 1 == self.first[n + 1], skip_group_check=True).then_inc(self.pv_made, 1)
            elif kind == "X" and extra:
                extra(pe, step[0], turn)

    def act(self, act, steps, turn=0, extra=None):
        for kind, *step in steps:
            if kind == "P":
                n, i = step
                s, keys = 4 * n + i, self.keys_of(4 * self.jobs[n % self.nj][1] + i)
                act.wait_ge(self.nmax_done, turn * self.ns + s + 1)
                if n >= self.ring:
                    act.wait_ge(self.turned, turn * self.nt + self.first[n - self.ring + 1])
                act.activation(self.p[n % self.ring][i][:, 0:keys], self.s_ps[s % 2][:, 0:keys], ACT.Exp,
                               bias=self.nmx[:, s % 4:s % 4 + 1],
                               accum_out=self.rsum[:, s % 4:s % 4 + 1]).then_inc(self.exp_done, 1)
            elif kind == "T":
                n, j, tau = step
                c0 = self.columns(n, j)
                act.wait_ge(self.turned, turn * self.nt + tau + 1)
                act.wait_ge(self.pv_made, 1 + turn * self.nt + max(tau - 1, 0))
                act.activation(self.pt_hi[tau % 2][:, c0:HALF], self.t_ps[tau % 2][:, c0:HALF],
                               ACT.Copy).then_inc(self.hi_done, 1)
            elif kind == "E":
                n = step[0]
                act.wait_ge(self.pv_made, 1 + turn * self.nt + self.first[n + 1])
                act.wait_ge(self.out_done, 1 + turn * self.nj + n)
                act.activation(self.o_tmp[:], self.o_ps[n % len(self.o_ps)][HD:2 * HD, :], ACT.Copy).then_inc(self.tmp_done, 1)
            elif kind == "X" and extra:
                extra(act, step[0], turn)

    def dve(self, dve, steps, turn=0, extra=None):
        for kind, *step in steps:
            if kind == "S":
                n, i = step
                s, keys = 4 * n + i, self.keys_of(4 * self.jobs[n % self.nj][1] + i)
                one = slice(s % 4, s % 4 + 1)
                dve.wait_ge(self.scores_made, turn * self.ns + s + 1)
                dve.tensor_reduce(self.nmx[:, one], self.s_ps[s % 2][:, 0:keys], AX, ALU.max,
                                  negate=True).then_inc(self.nmax_done, 1)
            elif kind == "I":
                s = 4 * step[0] + step[1]
                one = slice(s % 4, s % 4 + 1)
                dve.wait_ge(self.exp_done, turn * self.ns + s + 1)
                dve.reciprocal(self.rinv[:, one], self.rsum[:, one]).then_inc(self.inv_done, 1)
            elif kind == "R":
                n, i = step
                s = 4 * n + i
                one, row = slice(s % 4, s % 4 + 1), self.p[n % self.ring][i]
                dve.wait_ge(self.inv_done, turn * self.ns + s + 1)
                dve.tensor_scalar(row[:], row[:], self.rinv[:, one], None, ALU.mult).then_inc(self.rows_done, 1)
            elif kind == "T":
                n, j, tau = step
                c0 = self.columns(n, j)
                dve.wait_ge(self.hi_done, turn * self.nt + tau + 1)
                dve.tensor_tensor(self.pt_lo[tau % 2][:, c0:HALF], self.t_ps[tau % 2][:, c0:HALF],
                                  as_f32(self.pt_hi[tau % 2][:, c0:HALF]), ALU.subtract).then_inc(self.split_done, 1)
            elif kind == "E":
                n = step[0]
                dve.wait_ge(self.tmp_done, turn * self.nj + n + 1)
                dve.wait_ge(self.stored[n % 2], 16 + 16 * (turn * (self.nj // 2) + n // 2))
                dve.tensor_tensor(self.o_out[n % 2][:], self.o_ps[n % len(self.o_ps)][0:HD, :], self.o_tmp[:],
                                  ALU.add).then_inc(self.out_done, 1)
            elif kind == "X" and extra:
                extra(dve, step[0], turn)

    def begin(self, sp):
        for s in (self.pv_made, self.out_done):
            sp.sem_inc(s, 1)
        for s in self.stored:
            sp.sem_inc(s, 16)

    def sync(self, sp, turn=0):
        for n, (h, half) in enumerate(self.jobs):
            sp.wait_ge(self.out_done, 1 + turn * self.nj + n + 1)
            sp.dma_start(self.store(h, half, turn), self.o_out[n % 2][:]).then_inc(self.stored[n % 2], 16)

    def finish(self, sp, turns=1):
        for s in range(2):
            sp.wait_ge(self.stored[s], 16 + 16 * turns * (self.nj // 2))


def wide(ap, n, w):
    return ap.unsqueeze(2).broadcast_to([P, n, w])


def rows_of(ap, n, w):
    return ap.unsqueeze(1).broadcast_to([P, n, w])


def memory_heads(nc, tag, k, mem_dram, ln_mem, w_kv, g_q, g_k, w_q, ht, psum, ot_dram):
    top = Memory(nc, X_AT, 229344)
    mem_x = top(f"{tag}_mem_x", [P, MEM // P, D])
    mt = {h: top(f"{tag}_mt_{h}", [P, ND, MEM], F32R) for h in ("hi", "lo")}
    norm_transposed(nc, f"{tag}_mn", k, mem_x, mem_dram, ln_mem, mt, psum)

    NKH, NQH = (MEM // P) * MEM_HEADS, NS * MEM_HEADS
    mem = Memory(nc, WORK_AT, X_AT)
    q_st = mem(f"{tag}_q_st", [P, MEM_HEADS, S], F32R)
    k_hh = mem(f"{tag}_k_hh", [P, MEM_HEADS, MEM], F32R)
    k_ll = mem(f"{tag}_k_ll", [P, MEM_HEADS, MEM], F32R)
    v = mem(f"{tag}_v", [P, MEM // P, MEM_HEADS, 2 * HD], F32R)
    kept = mem.at
    q32 = mem(f"{tag}_q32", [P, NQH, HD])
    k32 = mem(f"{tag}_k32", [P, NKH, 2, HD])
    wkv = [mem(f"{tag}_wkv_{h}", [P, ND // 2, 2 * MEM_Q], dt) for h, dt in (("hi", F32R), ("lo", F32R))]
    wq = [mem(f"{tag}_wq_{h}", [P, ND, MEM_Q], F32R) for h in ("hi", "lo")]
    raw = mem(f"{tag}_raw", [P, ND // 2, 2 * MEM_Q])
    with Phase(nc) as ctx:
        sem = lambda n: ctx.semaphore(f"{tag}p_{n}")
        w_in, hi_done, lo_done, made, evicted = sem("w_in"), sem("hi_done"), sem("lo_done"), sem("made"), sem("evicted")
        block = ctx.enter_context(nc.Block())
        kv_rows, q_rows = w_kv.rearrange("(c p) n -> p c n", p=P), w_q.rearrange("(c p) n -> p c n", p=P)
        raw_q = raw[:].rearrange("p c (a n) -> p (c a) n", a=2)
        raws = [raw[:], raw[:], raw_q]
        his = [wkv[0][:], wkv[0][:], wq[0][:]]
        los = [wkv[1][:], wkv[1][:], wq[1][:]]

        @block.sync
        def _(sp):
            for n, src in enumerate((kv_rows[:, 0:ND // 2, :], kv_rows[:, ND // 2:ND, :], q_rows)):
                if n:
                    sp.wait_ge(lo_done, n)
                sp.dma_start(raws[n], src).then_inc(w_in, 16)

        @block.scalar
        def _(act):
            for n in range(3):
                act.wait_ge(w_in, 16 * (n + 1))
                if n == 1:
                    act.wait_ge(made, 1)
                act.activation(his[n], raws[n], ACT.Copy).then_inc(hi_done, 1)

        @block.vector
        def _(dve):
            for n in range(3):
                dve.wait_ge(hi_done, n + 1)
                dve.tensor_tensor(los[n], raws[n], as_f32(his[n]), ALU.subtract).then_inc(lo_done, 1)
            dve.wait_ge(made, 2)
            for t in range(MEM // P):
                dve.tensor_copy(k32[:, t * MEM_HEADS:(t + 1) * MEM_HEADS, :, :],
                                psum[t][:].rearrange("p (h a d) -> p h a d", h=MEM_HEADS, a=2))
            for t in range(NS):
                dve.wait_ge(made, 3 + t)
                dve.tensor_copy(q32[:, t * MEM_HEADS:(t + 1) * MEM_HEADS, :],
                                psum[2 + t % 4][:, 0:MEM_Q].rearrange("p (h d) -> p h d", h=MEM_HEADS)).then_inc(evicted, 1)

        @block.tensor
        def _(pe):
            for part in range(2):
                pe.wait_ge(lo_done, part + 1)
                for t in range(MEM // P):
                    for c in range(ND // 2):
                        cc = part * (ND // 2) + c
                        rows = slice(t * P, (t + 1) * P)
                        last = product3(pe, psum[t][:], mt["hi"][:, cc, rows], mt["lo"][:, cc, rows],
                                        wkv[0][:, c, :], wkv[1][:, c, :], cc == 0, cc == ND - 1)
                last.then_inc(made, 1)
            pe.wait_ge(lo_done, 3)
            for t in range(NS):
                if t >= 4:
                    pe.wait_ge(evicted, t - 3)
                rows = slice(t * P, (t + 1) * P)
                for c in range(ND):
                    last = product3(pe, psum[2 + t % 4][:, 0:MEM_Q], ht["hi"][:, c, rows], ht["lo"][:, c, rows],
                                    wq[0][:, c, :], wq[1][:, c, :], c == 0, c == ND - 1)
                last.then_inc(made, 1)

    mem = Memory(nc, mem.at - 0, X_AT)
    mem.at = kept + NQH * HD * 4 + NKH * 2 * HD * 4
    sq = mem(f"{tag}_sq", [P, NQH, HD])
    q_hl = mem(f"{tag}_q_hl", [P, NQH, 2, HD], F32R)
    k_hl = mem(f"{tag}_k_hl", [P, 2, NKH, 2, HD], F32R)
    ss, std, rstd = (mem(f"{tag}_{n}", [P, NKH + NQH]) for n in ("hss", "hstd", "hrstd"))
    gq, gk = mem(f"{tag}_gq", [P, HD]), mem(f"{tag}_gk", [P, HD])
    with Phase(nc) as ctx:
        sem = lambda n: ctx.semaphore(f"{tag}h_{n}")
        g_in, chain, sums, root, normed, hi_done, lo_done, turned, stacked = (
            sem(n) for n in ("g_in", "chain", "sums", "root", "normed", "hi_done", "lo_done", "turned", "stacked"))
        block = ctx.enter_context(nc.Block())
        kk = k32[:, :, 0, :]
        v_flat = v[:].rearrange("p t h (a d) -> p (t h) a d", a=2)
        turns = [("k", a, t) for a in range(2) for t in range(MEM // P)] + [("q", 0, t) for t in range(NS)]

        @block.sync
        def _(sp):
            sp.dma_start(gq[:], g_q.partition_broadcast(P)).then_inc(g_in, 16)
            sp.dma_start(gk[:], g_k.partition_broadcast(P)).then_inc(g_in, 16)

        @block.vector
        def _(dve):
            dve.tensor_tensor(sq[:, 0:NKH, :], kk, kk, ALU.mult).then_inc(chain, 1)
            dve.wait_ge(chain, 1)
            dve.tensor_reduce(ss[:, 0:NKH], sq[:, 0:NKH, :], AX, ALU.add).then_inc(chain, 1)
            dve.wait_ge(chain, 2)
            dve.tensor_tensor(sq[:], q32[:], q32[:], ALU.mult).then_inc(chain, 1)
            dve.wait_ge(chain, 3)
            dve.tensor_reduce(ss[:, NKH:], sq[:], AX, ALU.add).then_inc(sums, 1)
            dve.wait_ge(root, 1)
            dve.reciprocal(rstd[:], std[:]).then_inc(chain, 1)
            dve.wait_ge(chain, 4)
            dve.tensor_tensor(kk, kk, wide(rstd[:, 0:NKH], NKH, HD), ALU.mult).then_inc(chain, 1)
            dve.tensor_tensor(q32[:], q32[:], wide(rstd[:, NKH:], NQH, HD), ALU.mult).then_inc(chain, 1)
            dve.wait_ge(g_in, 32)
            dve.tensor_scalar(gq[:], gq[:], float(HD) ** -0.5, None, ALU.mult).then_inc(chain, 1)
            dve.wait_ge(chain, 5)
            dve.tensor_tensor(kk, kk, rows_of(gk[:], NKH, HD), ALU.mult).then_inc(normed, 1)
            dve.wait_ge(chain, 7)
            dve.tensor_tensor(q32[:], q32[:], rows_of(gq[:], NQH, HD), ALU.mult).then_inc(normed, 1)
            dve.wait_ge(hi_done, 3)
            for a in range(2):
                dve.tensor_tensor(k_hl[:, 1, :, a, :], kk, as_f32(k_hl[:, 0, :, a, :]), ALU.subtract).then_inc(lo_done, 1)
            dve.tensor_tensor(v_flat[:, :, 1, :], k32[:, :, 1, :], as_f32(v_flat[:, :, 0, :]), ALU.subtract)
            dve.wait_ge(hi_done, 4)
            dve.tensor_tensor(q_hl[:, :, 1, :], q32[:], as_f32(q_hl[:, :, 0, :]), ALU.subtract).then_inc(lo_done, 1)
            for n, (what, a, t) in enumerate(turns):
                if n % 2:
                    dve.wait_ge(turned, n + 1)
                    dst = q_st if what == "q" else (k_hh, k_ll)[a]
                    dve.tensor_copy(dst[:, :, t * P:(t + 1) * P],
                                    psum[n % 8][:].rearrange("p (h q) -> p h q", h=MEM_HEADS)).then_inc(stacked, 1)

        @block.scalar
        def _(act):
            act.wait_ge(sums, 1)
            act.activation(std[:], ss[:], ACT.Sqrt, bias=k["eps"][:, 0:1], scale=1.0 / HD).then_inc(root, 1)
            act.wait_ge(normed, 1)
            for a in range(2):
                act.activation(k_hl[:, 0, :, a, :], kk, ACT.Copy).then_inc(hi_done, 1)
            act.activation(v_flat[:, :, 0, :], k32[:, :, 1, :], ACT.Copy).then_inc(hi_done, 1)
            act.wait_ge(normed, 2)
            act.activation(q_hl[:, :, 0, :], q32[:], ACT.Copy).then_inc(hi_done, 1)
            for n, (what, a, t) in enumerate(turns):
                if n % 2 == 0:
                    act.wait_ge(turned, n + 1)
                    dst = q_st if what == "q" else (k_hh, k_ll)[a]
                    act.activation(dst[:, :, t * P:(t + 1) * P],
                                   psum[n % 8][:].rearrange("p (h q) -> p h q", h=MEM_HEADS), ACT.Copy).then_inc(stacked, 1)

        @block.tensor
        def _(pe):
            pe.wait_ge(lo_done, 2)
            for n, (what, a, t) in enumerate(turns):
                if what == "q" and t == 0:
                    pe.wait_ge(lo_done, 3)
                if n >= 8:
                    pe.wait_ge(stacked, 8)
                for h in range(MEM_HEADS):
                    g = t * MEM_HEADS + h
                    src = q_hl[:, g, :, :] if what == "q" else k_hl[:, a, g, :, :]
                    last = pe.transpose(psum[n % 8][:, h * P:(h + 1) * P],
                                        as_f32(src.rearrange("p a d -> p (a d)")), k["ident"][:])
                last.then_inc(turned, 1)

    mem = Memory(nc, kept, X_AT)
    with Phase(nc) as ctx:
        def scores(pe, h, tile, out):
            rows = slice(tile * P, (tile + 1) * P)
            pe.matmul(out[:, 0:MEM], q_st[:, h, rows], k_hh[:, h, :], start=True, stop=False, skip_group_check=True)
            return pe.matmul(out[:, 0:MEM], q_st[:, h, rows], k_ll[:, h, :], start=False, stop=True, skip_group_check=True)

        jobs = [(h, half) for h in range(MEM_HEADS) for half in range(2)]
        at = Attend(nc, ctx, f"{tag}a", mem, psum, k, jobs, lambda tile: MEM, lambda half: MEM // P, False, scores,
                    lambda h, j: v[:, j, h, :],
                    lambda h, half, turn: ot_dram[SB_Q + h * HD:SB_Q + (h + 1) * HD, half * HALF:(half + 1) * HALF],
                    mem, 3)
        block = ctx.enter_context(nc.Block())

        @block.sync
        def _(sp):
            at.begin(sp)
            at.sync(sp)
            at.finish(sp)

        @block.tensor
        def _(pe):
            at.pe(pe, at.opening + at.steps)

        @block.scalar
        def _(act):
            at.act(act, at.opening + at.steps)

        @block.vector
        def _(dve):
            at.dve(dve, at.opening + at.steps)



def stick_breaking(nc, tag, k, w_in_dram, ht, psum, ot_dram):
    mem = Memory(nc, WORK_AT, 229344)
    q_st = mem(f"{tag}_q_st", [P, 2, S], F32R)
    k_hh = mem(f"{tag}_k_hh", [P, 2, S], F32R)
    k_ll = mem(f"{tag}_k_ll", [P, 2, S], F32R)
    v = mem(f"{tag}_v", [P, NS, 2, HD])
    v_t = mem(f"{tag}_v_t", [P, S])
    raw = [mem(f"{tag}_raw{i}", [P, ND, P]) for i in range(3)]
    w_hi = [mem(f"{tag}_w_hi{i}", [P, ND, P], F32R) for i in range(3)]
    w_lo = [mem(f"{tag}_w_lo{i}", [P, ND, P], F32R) for i in range(3)]
    NA, NR, NW = 3, 6, 3
    soft = [mem(f"{tag}_soft{s}", [P, HALF]) for s in range(NA)]
    run = [mem(f"{tag}_run{s}", [P, HALF]) for s in range(NR)]
    run_hi = [mem(f"{tag}_run_hi{s}", [P, HALF], F32R) for s in range(NR)]
    run_lo = [mem(f"{tag}_run_lo{s}", [P, HALF], F32R) for s in range(NR)]
    wt = [mem(f"{tag}_wt{s}", [P, HALF]) for s in range(NW)]
    o_out = [mem(f"{tag}_o_out{s}", [HD, HALF]) for s in range(2)]
    rows = w_in_dram.rearrange("(c p) n -> p c n", p=P)

    blocks = [(c, j, h) for c in range(2) for j in reversed(range(4 * c + 4)) for h in range(2)]
    NB = len(blocks)
    NZ = 6
    first_col = [max(0, j - 4 * c) * P for c, j, h in blocks]
    chained = [b for b, (c, j, h) in enumerate(blocks) if j < 4 * c + 3]
    n_chained = [sum(1 for x in chained if x <= b) for b in range(NB)]
    NC = len(chained)
    next_col = [first_col[b - 2] for b in range(NB)]
    OUT_AT = {b: 2 * c + h for b, (c, j, h) in enumerate(blocks) if j == 0}
    LEAD, LAG_U, LAG_PV = 1, 3, 4
    with Phase(nc) as ctx:
        sem = lambda n: ctx.semaphore(f"{tag}_{n}")
        w_in = [sem(f"w_in{i}") for i in range(3)]
        w_hi_done = [sem(f"w_hi_done{i}") for i in range(3)]
        w_lo_done = [sem(f"w_lo_done{i}") for i in range(3)]
        (proj_made, proj_hi, proj_split, scores_made, abs_done, exp_done, soft_done, sp_done, run_added, run_hi_done,
         run_split, sums_made, weight_done, pv_made, out_done, v_done) = (
            sem(n) for n in ("proj_made", "proj_hi", "proj_split", "scores_made", "abs_done", "exp_done", "soft_done",
                             "sp_done", "run_added", "run_hi_done", "run_split", "sums_made", "weight_done",
                             "pv_made", "out_done", "v_done"))
        stored = [sem(f"stored{s}") for s in range(2)]
        block = ctx.enter_context(nc.Block())
        hi_after = [2, 4, 8, 12]

        @block.sync
        def _(sp):
            def load(i, g):
                sp.dma_start(raw[i][:], rows[:, :, bass.ds(g * P + i * SB_Q, P)]).then_inc(w_in[i], 16)

            for s in (sp_done, out_done, run_split, sums_made, pv_made, weight_done):
                sp.sem_inc(s, 1)
            for s in stored:
                sp.sem_inc(s, 16)
            for i in range(3):
                load(i, 0)
            with sp.Fori(0, PAIRS) as g:
                for i in range(3):
                    sp.wait_ge(w_lo_done[i], g + 1)
                    load(i, g + 1)
                for n in range(4):
                    sp.wait_ge(out_done, 1 + 4 * g + n + 1)
                    sp.dma_start(ot_dram[bass.ds(g * P + (n % 2) * HD, HD), (n // 2) * HALF:(n // 2 + 1) * HALF],
                                 o_out[n % 2][:]).then_inc(stored[n % 2], 16)
            for s in range(2):
                sp.wait_ge(stored[s], 16 + 16 * 2 * PAIRS)

        @block.gpsimd
        def _(pool):
            def lower(i, g):
                pool.wait_ge(w_hi_done[i], g + 1)
                pool.tensor_tensor(w_lo[i][:], raw[i][:], as_f32(w_hi[i][:]), ALU.subtract).then_inc(w_lo_done[i], 1)

            for i in range(3):
                lower(i, 0)
            with pool.Fori(0, PAIRS) as g:
                for i in range(3):
                    lower(i, g + 1)
                for b in range(NB):
                    f = first_col[b]
                    pool.wait_ge(run_hi_done, g * NB + b + 1)
                    pool.wait_ge(sums_made, 1 + g * NB + max(b - NR + 3, 0))
                    pool.tensor_tensor(run_lo[b % NR][:, f:HALF], run[b % NR][:, f:HALF],
                                       as_f32(run_hi[b % NR][:, f:HALF]), ALU.subtract).then_inc(run_split, 1)

        @block.scalar
        def _(act):
            def upper(i, g):
                act.wait_ge(w_in[i], 16 * (g + 1))
                act.activation(w_hi[i][:], raw[i][:], ACT.Copy).then_inc(w_hi_done[i], 1)

            for i in range(3):
                upper(i, 0)
            act.preload_act_table_set("natural_log_exp_and_others")
            with act.Fori(0, PAIRS) as g:
                for u in range(8):
                    half = u % 2
                    cols = slice(half * HALF, (half + 1) * HALF)
                    z = psum[u % 4]
                    if u // 2 != 2:
                        act.wait_ge(proj_made, 8 * g + u + 1)
                    if u // 2 == 0:
                        for h in range(2):
                            r = slice(h * HD, (h + 1) * HD)
                            act.activation(q_st[r, h, cols], z[r, :], ACT.Copy, scale=0.125).then_inc(proj_hi, 1)
                    elif u // 2 == 1:
                        for h in range(2):
                            for a in range(2):
                                act.activation(k_hh[a * HD:(a + 1) * HD, h, cols], z[h * HD:(h + 1) * HD, :],
                                               ACT.Copy).then_inc(proj_hi, 1)
                    elif u // 2 == 3:
                        act.activation(v[:, 4 * half:4 * half + 4, :, :].rearrange("p t h d -> p (t h d)"), z[:],
                                       ACT.Copy).then_inc(v_done, 1)
                    if u in (1, 3, 5):
                        act.wait_ge(proj_made, 8 * g + u + 1)
                        upper(u // 2, g + 1)
                def magnitude(b):
                    f, s = first_col[b], soft[b % NA]
                    act.wait_ge(scores_made, g * NB + b + 1)
                    act.wait_ge(sp_done, 1 + g * NB + max(b - NA + 1, 0))
                    act.activation(s[:, f:HALF], psum[b % NZ][:, f:HALF], ACT.Abs).then_inc(abs_done, 1)

                magnitude(0)
                for t in range(NB + LAG_U):
                    if t < NB:
                        f, s = first_col[t], soft[t % NA]
                        act.wait_ge(abs_done, g * NB + t + 1)
                        act.activation(s[:, f:HALF], s[:, f:HALF], ACT.Exp, scale=-1.0).then_inc(exp_done, 1)
                    if t + 1 < NB:
                        magnitude(t + 1)
                    if t < NB:
                        act.wait_ge(exp_done, g * NB + t + 1)
                        act.activation(s[:, f:HALF], s[:, f:HALF], ACT.Ln, bias=1.0).then_inc(soft_done, 1)
                    b = t - LAG_U
                    if 0 <= b < NB:
                        f = first_col[b]
                        act.wait_ge(sums_made, 1 + g * NB + b + 1)
                        act.wait_ge(pv_made, 1 + g * NB + max(b - NW + 1, 0))
                        act.activation(wt[b % NW][:, f:HALF], psum[b % NZ][:, f:HALF], ACT.Exp).then_inc(weight_done, 1)

        @block.vector
        def _(dve):
            with dve.Fori(0, PAIRS) as g:
                for u in range(8):
                    half = u % 2
                    cols = slice(half * HALF, (half + 1) * HALF)
                    z = psum[u % 4]
                    if u // 2 == 2:
                        dve.wait_ge(proj_made, 8 * g + u + 1)
                        dve.tensor_copy(v_t[:, cols], z[:]).then_inc(proj_split, 1)
                        continue
                    if u // 2 == 3:
                        continue
                    dve.wait_ge(proj_hi, 12 * g + hi_after[u])
                    if u // 2 == 0:
                        for h in range(2):
                            r, o = slice(h * HD, (h + 1) * HD), slice((1 - h) * HD, (2 - h) * HD)
                            last = dve.scalar_tensor_tensor(q_st[o, h, cols], z[r, :], 0.125,
                                                            as_f32(q_st[r, h, cols]), ALU.mult, ALU.subtract)
                    elif u // 2 == 1:
                        for h in range(2):
                            r = slice(h * HD, (h + 1) * HD)
                            for a in range(2):
                                last = dve.tensor_tensor(k_ll[a * HD:(a + 1) * HD, h, cols], z[r, :],
                                                         as_f32(k_hh[r, h, cols]), ALU.subtract)
                    last.then_inc(proj_split, 1)
                for t in range(NB + LAG_PV + 2):
                    if t < NB:
                        f, r = first_col[t], run[t % NR]
                        dve.wait_ge(soft_done, g * NB + t + 1)
                        dve.wait_ge(run_split, 1 + g * NB + max(t - NR + 1, 0))
                        dve.scalar_tensor_tensor(r[:, f:HALF], psum[t % NZ][:, f:HALF], 0.0,
                                                 soft[t % NA][:, f:HALF], ALU.max, ALU.add).then_inc(sp_done, 1)
                    b = t - 1
                    if 0 <= b < NB:
                        f, r = first_col[b], run[b % NR]
                        if b in chained:
                            dve.wait_ge(run_added, g * NC + n_chained[b])
                        else:
                            dve.wait_ge(sp_done, 1 + g * NB + b + 1)
                        dve.wait_ge(sums_made, 1 + g * NB + max(b - NR + 3, 0))
                        dve.tensor_copy(run_hi[b % NR][:, f:HALF], r[:, f:HALF]).then_inc(run_hi_done, 1)
                    if t in chained:
                        fn, r = next_col[t], run[t % NR]
                        dve.wait_ge(sp_done, 1 + g * NB + t + 1)
                        dve.tensor_tensor(r[:, fn:HALF], r[:, fn:HALF], run[(t - 2) % NR][:, fn:HALF],
                                          ALU.add).then_inc(run_added, 1)
                    b = t - LAG_PV - 1
                    if b in OUT_AT:
                        n = OUT_AT[b]
                        dve.wait_ge(pv_made, 1 + g * NB + b + 1)
                        dve.wait_ge(stored[n % 2], 16 + 16 * (2 * g + n // 2))
                        dve.tensor_copy(o_out[n % 2][:], psum[6 + n % 2][0:HD, :]).then_inc(out_done, 1)

        @block.tensor
        def _(pe):
            with pe.Fori(0, PAIRS) as g:
                for u in range(6):
                    i, half = u // 2, u % 2
                    cols = slice(half * HALF, (half + 1) * HALF)
                    pe.wait_ge(w_lo_done[i], g + 1)
                    if u < 4:
                        pe.wait_ge(weight_done, 1 + g * NB)
                    else:
                        pe.wait_ge(proj_split, 6 * g + u - 3)
                    for c in range(ND):
                        last = product3(pe, psum[u % 4][:], w_hi[i][:, c, :], w_lo[i][:, c, :],
                                        ht["hi"][:, c, cols], ht["lo"][:, c, cols], c == 0, c == ND - 1)
                    last.then_inc(proj_made, 1)
                for half in range(2):
                    pe.wait_ge(proj_split, 6 * g + 5 + half)
                    for i in range(4):
                        tt = 4 * half + i
                        last = pe.transpose(psum[2 + half][:, i * P:(i + 1) * P], v_t[:, tt * P:(tt + 1) * P], k["ident"][:])
                    last.then_inc(proj_made, 1)
                pe.wait_ge(v_done, 2 * g + 2)
                for t in range(-LEAD, NB + LAG_PV):
                    b = t + LEAD
                    if b < NB:
                        c, j, h = blocks[b]
                        f, z = first_col[b], psum[b % NZ]
                        if b >= NZ:
                            pe.wait_ge(weight_done, 1 + g * NB + b - NZ + 1)
                        q = q_st[:, h, c * HALF + f:(c + 1) * HALF]
                        diagonal = j >= 4 * c
                        pe.matmul(z[:, f:HALF], k_hh[:, h, j * P:(j + 1) * P], q, start=True, stop=False, skip_group_check=True)
                        last = pe.matmul(z[:, f:HALF], k_ll[:, h, j * P:(j + 1) * P], q, start=False,
                                         stop=not diagonal, skip_group_check=True)
                        if diagonal:
                            last = pe.matmul(z[:, f:f + P], k["ident_r"][:], k["strict"][:], start=False, stop=True,
                                             skip_group_check=True)
                        last.then_inc(scores_made, 1)
                    b = t - LAG_U
                    if 0 <= b < NB:
                        f, fn, z, s = first_col[b], next_col[b], psum[b % NZ], b % NR
                        pe.wait_ge(run_split, 1 + g * NB + b + 1)
                        pe.wait_ge(sp_done, 1 + g * NB + b + 1)
                        pe.matmul(z[:, f:HALF], k["upper"][:], run_hi[s][:, f:HALF], start=False, stop=False, skip_group_check=True)
                        last = pe.matmul(z[:, f:HALF], k["upper"][:], run_lo[s][:, f:HALF], start=False,
                                         stop=b not in chained, skip_group_check=True)
                        if b in chained:
                            s = (b - 2) % NR
                            pe.matmul(z[:, fn:HALF], k["lower"][:], run_hi[s][:, fn:HALF], start=False, stop=False, skip_group_check=True)
                            last = pe.matmul(z[:, fn:HALF], k["lower"][:], run_lo[s][:, fn:HALF], start=False,
                                             stop=True, skip_group_check=True)
                        last.then_inc(sums_made, 1)
                    b = t - LAG_PV
                    if 0 <= b < NB:
                        c, j, h = blocks[b]
                        f, o = first_col[b], psum[6 + h]
                        pe.wait_ge(weight_done, 1 + g * NB + b + 1)
                        if b not in chained:
                            pe.wait_ge(out_done, 1 + 4 * g + (0 if c == 0 else h + 1))
                        pe.matmul(o[0:HD, f:HALF], v[:, j, h, :], wt[b % NW][:, f:HALF], start=b not in chained,
                                  stop=j == 0, skip_group_check=True).then_inc(pv_made, 1)


def down_project(nc, tag, k, w_dram, width, rank, gain, ht, out, extra, at, psum):
    mem = Memory(nc, at, 229344)
    raw = [mem(f"{tag}_raw{s}", [P, width]) for s in range(2)]
    w_hi = mem(f"{tag}_w_hi", [P, ND, width], F32R)
    w_lo = mem(f"{tag}_w_lo", [P, ND, width], F32R)
    c32 = mem(f"{tag}_c32", [P, 4, rank])
    ss, std, rstd = (mem(f"{tag}_{n}", [P, NS]) for n in ("ss", "std", "rstd"))
    junk = mem(f"{tag}_junk", [P, rank])
    nr = rank // P
    gcol = mem(f"{tag}_gcol", [P, nr])
    pieces = 2 if width > HALF else 1
    pw = width // pieces
    rw = rank // pieces
    rows = w_dram.rearrange("(c p) n -> c p n", p=P)
    with Phase(nc) as ctx:
        sem = lambda n: ctx.semaphore(f"{tag}_{n}")
        w_in = [sem(f"w_in{s}") for s in range(2)]
        g_in, w_hi_done, w_lo_done, made, copied, squared, root, inverse, normed, turned, hi_done, lo_done = (
            sem(n) for n in ("g_in", "w_hi_done", "w_lo_done", "made", "copied", "squared", "root", "inverse",
                             "normed", "turned", "hi_done", "lo_done"))
        block = ctx.enter_context(nc.Block())

        @block.sync
        def _(sp):
            with nc.allow_non_contiguous_dma("gain"):
                sp.dma_start(gcol[:], gain_columns(gain)).then_inc(g_in, 16)
            for c in range(ND):
                if c >= 2:
                    sp.wait_ge(w_lo_done, c - 1)
                sp.dma_start(raw[c % 2][:], rows[c]).then_inc(w_in[c % 2], 16)

        @block.gpsimd
        def _(pool):
            for c in range(1, ND, 2):
                pool.wait_ge(w_hi_done, c + 1)
                pool.wait_ge(w_lo_done, c)
                pool.tensor_tensor(w_lo[:, c, :], raw[c % 2][:], as_f32(w_hi[:, c, :]), ALU.subtract).then_inc(w_lo_done, 1)

        @block.scalar
        def _(act):
            for c in range(ND):
                act.wait_ge(w_in[c % 2], 16 * (c // 2 + 1))
                act.activation(w_hi[:, c, :], raw[c % 2][:], ACT.Copy).then_inc(w_hi_done, 1)
            act.wait_ge(g_in, 16)
            for grp in range(2):
                for i in range(4):
                    act.wait_ge(copied, 4 * grp + i + 1)
                    t = 4 * grp + i
                    if t:
                        act.wait_ge(squared, t)
                    act.activation(junk[:], c32[:, i, :], ACT.Square, accum_out=ss[:, t:t + 1]).then_inc(squared, 1)
                act.wait_ge(squared, 4 * grp + 4)
                g4 = slice(4 * grp, 4 * grp + 4)
                act.activation(std[:, g4], ss[:, g4], ACT.Sqrt, bias=k["eps"][:, 0:1], scale=1.0 / rank).then_inc(root, 1)
                for c in range(nr):
                    n = grp * nr + c
                    act.wait_ge(turned, n + 1)
                    act.activation(out["hi"][:, c, grp * HALF:(grp + 1) * HALF], psum[4 + n % 4][:], ACT.Copy,
                                   scale=gcol[:, c:c + 1]).then_inc(hi_done, 1)

        @block.vector
        def _(dve):
            for c in range(0, ND, 2):
                dve.wait_ge(w_hi_done, c + 1)
                if c:
                    dve.wait_ge(w_lo_done, c)
                dve.tensor_tensor(w_lo[:, c, :], raw[c % 2][:], as_f32(w_hi[:, c, :]), ALU.subtract).then_inc(w_lo_done, 1)
            for grp in range(2):
                for i in range(4):
                    t = 4 * grp + i
                    dve.wait_ge(made, t + 1)
                    if grp:
                        dve.wait_ge(turned, nr)
                    for p in range(pieces):
                        bank = psum[(t % 2) * pieces + p]
                        last = dve.tensor_copy(c32[:, i, p * rw:(p + 1) * rw], bank[:, 0:rw])
                    if extra is not None:
                        last = dve.tensor_copy(extra[:, t, :], bank[:, rw:pw])
                    last.then_inc(copied, 1)
                dve.wait_ge(root, grp + 1)
                g4 = slice(4 * grp, 4 * grp + 4)
                dve.reciprocal(rstd[:, g4], std[:, g4]).then_inc(inverse, 1)
                dve.wait_ge(inverse, grp + 1)
                for i in range(4):
                    t = 4 * grp + i
                    dve.tensor_scalar(c32[:, i, :], c32[:, i, :], rstd[:, t:t + 1], None, ALU.mult).then_inc(normed, 1)
                for c in range(nr):
                    n = grp * nr + c
                    cols = slice(grp * HALF, (grp + 1) * HALF)
                    dve.wait_ge(hi_done, n + 1)
                    dve.scalar_tensor_tensor(out["lo"][:, c, cols], psum[4 + n % 4][:], gcol[:, c:c + 1],
                                             as_f32(out["hi"][:, c, cols]), ALU.mult, ALU.subtract).then_inc(lo_done, 1)

        @block.tensor
        def _(pe):
            pe.wait_ge(w_lo_done, ND)
            for grp in range(2):
                for i in range(4):
                    t = 4 * grp + i
                    if t >= 2:
                        pe.wait_ge(copied, t - 1)
                    r = slice(t * P, (t + 1) * P)
                    for p in range(pieces):
                        cols = slice(p * pw, (p + 1) * pw)
                        for c in range(ND):
                            last = product3(pe, psum[(t % 2) * pieces + p][:, 0:pw], ht["hi"][:, c, r], ht["lo"][:, c, r],
                                            w_hi[:, c, cols], w_lo[:, c, cols], c == 0, c == ND - 1)
                    last.then_inc(made, 1)
                pe.wait_ge(normed, 4 * grp + 4)
                for c in range(nr):
                    n = grp * nr + c
                    if n >= 4:
                        pe.wait_ge(lo_done, n - 3)
                    for i in range(4):
                        last = pe.transpose(psum[4 + n % 4][:, i * P:(i + 1) * P], c32[:, i, c * P:(c + 1) * P], k["ident"][:])
                    last.then_inc(turned, 1)


TWO_PI = 6.283185307179586
TURN = (6.28125, float(np.float32(np.int64(0.0019353071795864769 * 2**22) / 2.0**22)))
TURN += (float(np.float32(TWO_PI - TURN[0] - TURN[1])),)
ROUND = 1.5 * 2.0**23
PI_IN = 3.1415925


def rotary_tables(nc, tag, k, positions, g_q, g_k, k_rope, tab, k_rot, k_ss, at):
    mem = Memory(nc, at, 229344)
    H = ROPE // 2
    pos_i, pos = mem(f"{tag}_pos_i", [P, NS], I32), mem(f"{tag}_pos", [P, NS])
    freq, gq, gk = mem(f"{tag}_freq", [P, H]), mem(f"{tag}_gq", [P, ROPE]), mem(f"{tag}_gk", [P, ROPE])
    ang, turns, a, b, c, cos, sin = (mem(f"{tag}_{n}", [P, NS, H]) for n in ("ang", "turns", "a", "b", "c", "cos", "sin"))
    sq = mem(f"{tag}_sq", [P, NS, ROPE])
    kg = mem(f"{tag}_kg", [P, NS, ROPE])
    with Phase(nc) as ctx:
        loaded, done, sines = (ctx.semaphore(f"{tag}_{n}") for n in ("loaded", "done", "sines"))
        block = ctx.enter_context(nc.Block())
        count, angles_ready = [0], []

        @block.sync
        def _(sp):
            with nc.allow_non_contiguous_dma("positions"):
                sp.dma_start(pos_i[:], positions.rearrange("b (t p) -> p (b t)", p=P)).then_inc(loaded, 16)
            sp.dma_start(gq[:], g_q[NOPE:QK].partition_broadcast(P)).then_inc(loaded, 16)
            sp.dma_start(gk[:], g_k[NOPE:QK].partition_broadcast(P)).then_inc(loaded, 16)

        @block.vector
        def _(dve):
            def then(ins):
                count[0] += 1
                ins.then_inc(done, 1)
                dve.wait_ge(done, count[0])

            for i in range(H):
                last = dve.memset(freq[:, i:i + 1], float(np.float32(THETA) ** np.float32(-i / H)))
            then(last)
            dve.wait_ge(loaded, 48)
            then(dve.tensor_copy(pos[:], pos_i[:]))
            then(dve.tensor_tensor(ang[:], wide(pos[:], NS, H), rows_of(freq[:], NS, H), ALU.mult))
            then(dve.tensor_scalar(turns[:], ang[:], 1.0 / TWO_PI, ROUND, ALU.mult, ALU.add))
            then(dve.tensor_scalar(turns[:], turns[:], ROUND, None, ALU.subtract))
            for part in TURN:
                then(dve.scalar_tensor_tensor(ang[:], turns[:], -part, ang[:], ALU.mult, ALU.add))
            then(dve.tensor_scalar(a[:], ang[:], PI_IN, -PI_IN, ALU.min, ALU.max))
            then(dve.tensor_scalar(b[:], ang[:], TWO_PI / 4, None, ALU.add))
            then(dve.tensor_scalar(c[:], b[:], TWO_PI / 2, -TWO_PI, ALU.is_gt, ALU.mult))
            then(dve.tensor_tensor(b[:], b[:], c[:], ALU.add))
            then(dve.tensor_scalar(b[:], b[:], PI_IN, -PI_IN, ALU.min, ALU.max))
            angles_ready.append(count[0])
            dve.wait_ge(sines, 2)
            for n, (g, f) in enumerate(((0, cos), (1, sin), (1, cos), (0, sin))):
                dve.tensor_tensor(tab[n][:], f[:], rows_of(gq[:, g * H:(g + 1) * H], NS, H), ALU.mult)
            then(dve.tensor_tensor(sq[:], k_rope[:], k_rope[:], ALU.mult))
            dve.tensor_reduce(k_ss[:], sq[:], AX, ALU.add)
            then(dve.tensor_tensor(kg[:], k_rope[:], rows_of(gk[:], NS, ROPE), ALU.mult))
            for first, second, op, out in ((cos, sin, ALU.subtract, 0), (sin, cos, ALU.add, H)):
                then(dve.tensor_tensor(a[:], kg[:, :, 0:H], first[:], ALU.mult))
                then(dve.tensor_tensor(b[:], kg[:, :, H:ROPE], second[:], ALU.mult))
                then(dve.tensor_tensor(k_rot[:, :, out:out + H], a[:], b[:], op))

        @block.scalar
        def _(act):
            act.wait_ge(done, angles_ready[0])
            act.activation(sin[:], a[:], ACT.Sin).then_inc(sines, 1)
            act.activation(cos[:], b[:], ACT.Sin).then_inc(sines, 1)


def latent_heads(nc, tag, k, w_q_up, w_kv_up, g_q, g_k, cq, ckv, tab, k_rot, k_ss, at, psum, ot_dram):
    mem = Memory(nc, at, 229344)
    low = Memory(nc, HT_AT, CONST_AT)
    NQ, NK = Q_RANK // P, KV_RANK // P
    QW, KW = 2 * QK, 2 * (NOPE + HD)
    G = NS * 2
    H = ROPE // 2
    wq = {n: mem(f"{tag}_wq_{n}", [P, NQ, QW], F32 if n == "raw" else F32R) for n in ("raw", "hi", "lo")}
    wk = {n: mem(f"{tag}_wk_{n}", [P, NK, KW], F32 if n == "raw" else F32R) for n in ("raw", "hi", "lo")}
    q32, k32 = mem(f"{tag}_q32", [P, G, QK]), mem(f"{tag}_k32", [P, G, QK])
    junk = mem(f"{tag}_junk", [P, 2, QK + NOPE])
    ra, rb, rc, rd = (mem(f"{tag}_{n}", [P, G, H]) for n in ("ra", "rb", "rc", "rd"))
    qt = {n: mem(f"{tag}_qt_{n}", [QK, 2, S], F32R) for n in ("hi", "lo")}
    kt = {n: mem(f"{tag}_kt_{n}", [QK, 2, S], F32R) for n in ("hi", "lo")}
    ss, std, rstd = (mem(f"{tag}_{n}", [P, 2, G]) for n in ("ss", "std", "rstd"))
    gcol = mem(f"{tag}_gcol", [QK, 2])
    v32 = low(f"{tag}_v32", [P, G, HD])
    v = low(f"{tag}_v", [P, 2, NS, 2 * HD], F32R)
    q_rows, k_rows = w_q_up.rearrange("(c p) n -> p c n", p=P), w_kv_up.rearrange("(c p) n -> p c n", p=P)
    turns = [(a, h, half) for h in range(2) for half in range(2) for a in range(2)]
    PREPARE = (["project 0", "project 1", "project 2", "project 3", "sum 0", "root 0", "normalise 0", "rotate 0",
                "project 4", "project 5", "project 6", "project 7", "next weights", "sum 1", "root 1", "normalise 1",
                "rotate 1", "values 0"] + [f"turn {n}" for n in range(8)])
    extras = {0: ["values 1", "project 0"], 1: ["project 1"], 2: ["project 2"], 3: ["project 3"],
              4: ["project 4", "sum 0", "root 0"], 5: ["project 5", "normalise 0"], 6: ["project 6", "rotate 0"],
              7: ["project 7"], 8: ["next weights", "sum 1", "root 1"], 9: ["normalise 1"],
              10: ["rotate 1", "turn 0"], 11: ["used 1", "turn 1"], 12: ["turn 2"], 13: ["values 0", "turn 3"],
              14: ["turn 4"], 16: ["turn 5"], 18: ["turn 6"], 21: ["turn 7"]}
    plan = [8, 9, 10, 11, 12, 13, 13, 14, 14, 15, 15, 16, 16, 16, 17, 18, 19, 20, 21, 21, 22, 23, 23, 24, 24]
    OWN = ("values 1", "used 1")
    group = lambda n: slice(G // 2 * n, G // 2 * (n + 1))
    tiles = lambda n: slice(NS // 2 * n, NS // 2 * (n + 1))
    with Phase(nc) as ctx:
        def scores(pe, h, tile, out):
            rows, keys = slice(tile * P, (tile + 1) * P), (tile + 1) * P
            for at_key in range(0, keys, HALF):
                cols = slice(at_key, min(at_key + HALF, keys))
                product3(pe, out[:, cols], qt["hi"][:, h, rows], qt["lo"][:, h, rows],
                         kt["hi"][:, h, cols], kt["lo"][:, h, cols], True, cols.stop < keys)
            return pe.matmul(out[:, rows], k["ident_r"][:], k["causal"][:], start=False, stop=True, skip_group_check=True)

        at_ = Attend(nc, ctx, f"{tag}a", low, psum, k, [(h, half) for h in range(2) for half in range(2)],
                     lambda tile: (tile + 1) * P, lambda half: 4 * half + 4, True, scores,
                     lambda h, j: v[:, h, j, :],
                     lambda h, half, g: ot_dram[bass.ds(g * P + h * HD, HD), half * HALF:(half + 1) * HALF],
                     low, 4, (6,), plan, extras)
        sem = lambda n: ctx.semaphore(f"{tag}_{n}")
        (g_in, wq_in, wk_in, wq_hi, wk_hi, wq_lo, wk_lo, made, evicted, squared, v_hi, v_split, sums, root, inverse,
         q_norm, k_norm, k_rope_done, rot_dve, rot_pool, q_rot, turned, t_hi, t_split, ones, scaled) = (
            sem(n) for n in ("g_in", "wq_in", "wk_in", "wq_hi", "wk_hi", "wq_lo", "wk_lo", "made", "evicted", "squared", "v_hi",
                             "v_split", "sums", "root", "inverse", "q_norm", "k_norm", "k_rope_done",
                             "rot_dve", "rot_pool", "q_rot", "turned", "t_hi", "t_split", "ones", "scaled"))
        block = ctx.enter_context(nc.Block())
        bank = psum[7]
        q4 = q32[:].rearrange("p (t h) d -> p t h d", h=2)
        x1, x2 = q4[:, :, :, NOPE:NOPE + H], q4[:, :, :, NOPE + H:QK]
        four = lambda tile, n: tile[:, group(n), :].rearrange("p (t h) d -> p t h d", h=2)
        table = lambda m, n: tab[m][:, tiles(n), :].unsqueeze(2).broadcast_to([P, NS // 2, 2, H])
        v_head = lambda h: v32[:].rearrange("p (t h) d -> p t h d", h=2)[:, :, h, :]

        @block.sync
        def _(sp):
            def load(g):
                sp.dma_start(wq["raw"][:], q_rows[:, :, bass.ds(g * QW, QW)]).then_inc(wq_in, 16)
                sp.dma_start(wk["raw"][:], k_rows[:, :, bass.ds(g * KW, KW)]).then_inc(wk_in, 16)

            at_.begin(sp)
            for s in (made, evicted, squared, v_split, turned, t_split):
                sp.sem_inc(s, 1)
            load(0)
            sp.wait_ge(ones, 1)
            with nc.allow_non_contiguous_dma("gains"):
                sp.dma_start(gcol[0:NOPE, 0:1], g_q[0:NOPE].unsqueeze(1)).then_inc(g_in, 16)
                sp.dma_start(gcol[0:NOPE, 1:2], g_k[0:NOPE].unsqueeze(1)).then_inc(g_in, 16)
            sp.wait_ge(wq_lo, 1)
            sp.wait_ge(wk_lo, 1)
            load(1)
            with sp.Fori(0, PAIRS - 2) as g:
                sp.wait_ge(wq_lo, g + 2)
                sp.wait_ge(wk_lo, g + 2)
                load(g + 2)
                at_.sync(sp, g)
            sp.wait_ge(wq_lo, PAIRS)
            sp.wait_ge(wk_lo, PAIRS)
            load(PAIRS - 1)
            for g in range(PAIRS - 2, PAIRS):
                at_.sync(sp, g)
            at_.finish(sp, PAIRS)

        @block.gpsimd
        def _(pool):
            def lower_values(h, n):
                pool.wait_ge(v_hi, n + 1)
                pool.tensor_tensor(v[:, h, :, HD:], v_head(h), as_f32(v[:, h, :, 0:HD]), ALU.subtract).then_inc(v_split, 1)

            def lower_weights(g):
                for w, hi, lo in ((wq, wq_hi, wq_lo), (wk, wk_hi, wk_lo)):
                    pool.wait_ge(hi, g + 1)
                    pool.tensor_tensor(w["lo"][:], w["raw"][:], as_f32(w["hi"][:]), ALU.subtract).then_inc(lo, 1)

            def rotate(n, g):
                e, x1n, x2n = 2 * g + n, x1[:, tiles(n)], x2[:, tiles(n)]
                pool.wait_ge(inverse, e + 1)
                pool.tensor_tensor(k32[:, group(n), NOPE:QK].rearrange("p (t h) d -> p t h d", h=2),
                                   k_rot[:, tiles(n), :].unsqueeze(2).broadcast_to([P, NS // 2, 2, ROPE]),
                                   rstd[:, 1, group(n)].rearrange("p (t h) -> p t h", h=2).unsqueeze(3).broadcast_to([P, NS // 2, 2, ROPE]),
                                   ALU.mult).then_inc(k_rope_done, 1)
                pool.wait_ge(q_norm, e + 1)
                pool.tensor_tensor(four(rc, n), x2n, table(2, n), ALU.mult).then_inc(rot_pool, 1)
                pool.tensor_tensor(four(rd, n), x1n, table(3, n), ALU.mult).then_inc(rot_pool, 1)
                pool.wait_ge(rot_pool, 2 * e + 2)
                pool.wait_ge(rot_dve, 2 * e + 2)
                pool.tensor_tensor(x2n, four(rc, n), four(rd, n), ALU.add).then_inc(q_rot, 1)

            def prepare(g):
                rotate(0, g)
                lower_weights(g + 1)
                rotate(1, g)
                lower_values(0, 2 * g)

            lower_weights(0)
            prepare(0)
            with pool.Fori(0, PAIRS - 1) as g:
                lower_values(1, 2 * g + 1)
                prepare(g + 1)
            lower_values(1, 2 * PAIRS - 1)

        @block.scalar
        def _(act):
            def upper_weights(g):
                act.wait_ge(made, 1 + NS * g)
                act.wait_ge(wq_in, 16 * (g + 1))
                act.activation(wq["hi"][:], wq["raw"][:], ACT.Copy).then_inc(wq_hi, 1)
                act.wait_ge(wk_in, 16 * (g + 1))
                act.activation(wk["hi"][:], wk["raw"][:], ACT.Copy).then_inc(wk_hi, 1)

            def prepare(act, step, g):
                what, n = step.split()[0], int(step[-1]) if step[-1].isdigit() else 0
                if what == "next":
                    upper_weights(g + 1)
                elif what == "project":
                    act.wait_ge(made, 1 + NS * g + n + 1)
                    if n == 0:
                        act.wait_ge(turned, 1 + 8 * g)
                        act.wait_ge(v_split, 1 + 2 * g)
                    kv = bank[:, QW:QW + KW].rearrange("p (g d) -> p g d", d=NOPE + HD)
                    two = slice(2 * n, 2 * n + 2)
                    act.activation(q32[:, two, :], bank[:, 0:QW].rearrange("p (g d) -> p g d", d=QK), ACT.Copy)
                    act.activation(k32[:, two, 0:NOPE], kv[:, :, 0:NOPE], ACT.Copy)
                    act.activation(v32[:, two, :], kv[:, :, NOPE:], ACT.Copy).then_inc(evicted, 1)
                    act.wait_ge(evicted, 1 + NS * g + n + 1)
                    act.wait_ge(squared, 1 + NS * g + n)
                    for h in range(2):
                        one = slice(2 * n + h, 2 * n + h + 1)
                        act.activation(junk[:, h, 0:QK], q32[:, 2 * n + h, :], ACT.Square, accum_out=ss[:, 0, one])
                        last = act.activation(junk[:, h, QK:], k32[:, 2 * n + h, 0:NOPE], ACT.Square, accum_out=ss[:, 1, one])
                    last.then_inc(squared, 1)
                elif what == "root":
                    act.wait_ge(sums, 2 * g + n + 1)
                    act.activation(std[:, :, group(n)], ss[:, :, group(n)], ACT.Sqrt, bias=k["eps"][:, 0:1],
                                   scale=1.0 / QK).then_inc(root, 1)
                elif what == "values":
                    act.activation(v[:, 0, :, 0:HD], v_head(0), ACT.Copy).then_inc(v_hi, 1)
                elif what == "turn":
                    a, h, half = turns[n]
                    act.wait_ge(turned, 1 + 8 * g + n + 1)
                    act.activation((qt, kt)[a]["hi"][:, h, half * HALF:(half + 1) * HALF], bank[0:QK, :], ACT.Copy,
                                   scale=gcol[:, a:a + 1]).then_inc(t_hi, 1)

            def own(act, step, g):
                if step == "values 1":
                    act.wait_ge(at_.pv_made, 1 + g * at_.nt)
                    act.activation(v[:, 1, :, 0:HD], v_head(1), ACT.Copy).then_inc(v_hi, 1)

            def extra(act, step, g):
                if step in OWN:
                    own(act, step, g)
                else:
                    prepare(act, step, g + 1)

            act.wait_ge(g_in, 32)
            act.activation(gcol[:, 0:1], gcol[:, 0:1], ACT.Copy, scale=float(QK) ** -0.5).then_inc(scaled, 1)
            act.wait_ge(scaled, 1)
            upper_weights(0)
            for step in PREPARE:
                prepare(act, step, 0)
            at_.act(act, at_.opening)
            with act.Fori(0, PAIRS - 1) as g:
                at_.act(act, at_.steps, g, extra)
            at_.act(act, at_.closing, PAIRS - 1, own)

        @block.vector
        def _(dve):
            def prepare(dve, step, g):
                what, n = step.split()[0], int(step[-1]) if step[-1].isdigit() else 0
                e = 2 * g + n
                if what == "sum":
                    dve.wait_ge(squared, 1 + NS * g + NS // 2 * (n + 1))
                    ks = ss[:, 1, group(n)].rearrange("p (t h) -> p t h", h=2)
                    dve.tensor_tensor(ks, ks, k_ss[:, tiles(n)].unsqueeze(2).broadcast_to([P, NS // 2, 2]),
                                      ALU.add).then_inc(sums, 1)
                elif what == "normalise":
                    dve.wait_ge(root, e + 1)
                    dve.reciprocal(rstd[:, :, group(n)], std[:, :, group(n)]).then_inc(inverse, 1)
                    dve.wait_ge(inverse, e + 1)
                    dve.tensor_tensor(q32[:, group(n), :], q32[:, group(n), :], wide(rstd[:, 0, group(n)], G // 2, QK),
                                      ALU.mult).then_inc(q_norm, 1)
                    dve.tensor_tensor(k32[:, group(n), 0:NOPE], k32[:, group(n), 0:NOPE],
                                      wide(rstd[:, 1, group(n)], G // 2, NOPE), ALU.mult).then_inc(k_norm, 1)
                elif what == "rotate":
                    x1n, x2n = x1[:, tiles(n)], x2[:, tiles(n)]
                    dve.wait_ge(q_norm, e + 1)
                    dve.tensor_tensor(four(ra, n), x1n, table(0, n), ALU.mult).then_inc(rot_dve, 1)
                    dve.tensor_tensor(four(rb, n), x2n, table(1, n), ALU.mult).then_inc(rot_dve, 1)
                    dve.wait_ge(rot_dve, 2 * e + 2)
                    dve.wait_ge(rot_pool, 2 * e + 2)
                    dve.tensor_tensor(x1n, four(ra, n), four(rb, n), ALU.subtract).then_inc(q_rot, 1)
                elif what == "turn":
                    a, h, half = turns[n]
                    dve.wait_ge(t_hi, 8 * g + n + 1)
                    cols, t = slice(half * HALF, (half + 1) * HALF), (qt, kt)[a]
                    dve.scalar_tensor_tensor(t["lo"][:, h, cols], bank[0:QK, :], gcol[:, a:a + 1],
                                             as_f32(t["hi"][:, h, cols]), ALU.mult, ALU.subtract).then_inc(t_split, 1)

            dve.memset(gcol[:], 1.0).then_inc(ones, 1)
            for step in PREPARE:
                prepare(dve, step, 0)
            at_.dve(dve, at_.opening)
            with dve.Fori(0, PAIRS - 1) as g:
                at_.dve(dve, at_.steps, g, lambda dve, step, g: step not in OWN and prepare(dve, step, g + 1))
            at_.dve(dve, at_.closing, PAIRS - 1)

        @block.tensor
        def _(pe):
            def prepare(pe, step, g):
                what, n = step.split()[0], int(step[-1]) if step[-1].isdigit() else 0
                if what == "project":
                    if n == 0:
                        pe.wait_ge(wq_lo, g + 1)
                        pe.wait_ge(wk_lo, g + 1)
                        pe.wait_ge(t_split, 1 + 8 * g)
                    pe.wait_ge(evicted, 1 + NS * g + n)
                    rows = slice(n * P, (n + 1) * P)
                    for c in range(NQ):
                        product3(pe, bank[:, 0:QW], cq["hi"][:, c, rows], cq["lo"][:, c, rows],
                                 wq["hi"][:, c, :], wq["lo"][:, c, :], c == 0, c == NQ - 1)
                    for c in range(NK):
                        last = product3(pe, bank[:, QW:QW + KW], ckv["hi"][:, c, rows], ckv["lo"][:, c, rows],
                                        wk["hi"][:, c, :], wk["lo"][:, c, :], c == 0, c == NK - 1)
                    last.then_inc(made, 1)
                elif what == "turn":
                    a, h, half = turns[n]
                    if n == 0:
                        pe.wait_ge(evicted, 1 + NS * (g + 1))
                    else:
                        pe.wait_ge(t_split, 1 + 8 * g + n)
                    if n in (0, 2):
                        e = 2 * g + n // 2
                        pe.wait_ge(q_rot, 2 * e + 2)
                        pe.wait_ge(k_norm, e + 1)
                        pe.wait_ge(k_rope_done, e + 1)
                    src = (q32, k32)[a]
                    for i in range(4):
                        last = pe.transpose(bank[0:QK, i * P:(i + 1) * P], src[:, 2 * (4 * half + i) + h, :], k["ident"][:])
                    last.then_inc(turned, 1)

            def own(pe, step, g):
                if step == "used 1":
                    pe.wait_ge(v_split, 1 + 2 * g + 2)

            def extra(pe, step, g):
                if step in OWN:
                    own(pe, step, g)
                else:
                    prepare(pe, step, g + 1)

            for step in PREPARE:
                prepare(pe, step, 0)
            pe.wait_ge(t_split, 1 + 4)
            at_.pe(pe, at_.opening)
            with pe.Fori(0, PAIRS - 1) as g:
                pe.wait_ge(t_split, 1 + 8 * g + 8)
                pe.wait_ge(v_split, 1 + 2 * g + 1)
                at_.pe(pe, at_.steps, g, extra)
            pe.wait_ge(t_split, 1 + 8 * PAIRS)
            pe.wait_ge(v_split, 1 + 2 * (PAIRS - 1) + 1)
            at_.pe(pe, at_.closing, PAIRS - 1, own)


def build(nc, a, out):
    with ExitStack() as ctx:
        banks = ctx.enter_context(nc.psum_tensor("banks", [P, 8, HALF], F32))
        psum = {b: banks[:, b, :] for b in range(8)}
        psum["pair"] = [banks[:, 2 * i:2 * i + 2, :].rearrange("p a b -> p (a b)") for i in range(2)]
        x_mid = nc.dram_tensor("x_mid", (S, D), F32, kind="Internal").ap()
        ot_dram = nc.dram_tensor("attention_out_t", (D, S), F32, kind="Internal").ap()

        k, mem = {}, Memory(nc, CONST_AT, WORK_AT)
        for n, dt in (("ident", F32), ("ident_r", F32R), ("strict", F32R), ("causal", F32R), ("upper", F32R), ("lower", F32R)):
            k[n] = mem(n, [P, P], dt)
        k["eps"] = mem("eps", [P, 1])
        mem = Memory(nc, WORK_AT, X_AT)
        for n in ("strict", "causal", "upper", "lower"):
            k["tmp_" + n] = mem("tmp_" + n, [P, P])
        make_constants(nc, k)
        mem = Memory(nc, HT_AT, CONST_AT)
        ht = {h: mem(f"ht_{h}", [P, ND, S], F32R) for h in ("hi", "lo")}
        x = Memory(nc, X_AT, 229344)("x", [P, NS, D])

        for layer in range(DEPTH):
            tag = f"l{layer}"
            x_dram = a["x"].rearrange("b s d -> (b s) d") if layer == 0 else x_mid
            norm_transposed(nc, f"{tag}n", k, x, x_dram if layer == 0 else None, a["ln_attn"][layer], ht, psum)
            w_in = (a["sb_w_in"] if layer == 0 else a["mla_w_in"])[0]
            q_mem_at = w_in.shape[1] - MEM_Q
            memory_heads(nc, f"{tag}m", k, a["mem"][0], a["ln_mem"][layer], a["w_mem_kv"][layer], a["g_qn_mem"][layer],
                         a["g_kn_mem"][layer], w_in[:, q_mem_at:], ht, psum, ot_dram)
            if layer == 0:
                stick_breaking(nc, f"{tag}s", k, w_in, ht, psum, ot_dram)
            else:
                mem = Memory(nc, WORK_AT, 229344)
                cq = {h: mem(f"cq_{h}", [P, Q_RANK // P, S], F32R) for h in ("hi", "lo")}
                ckv = {h: mem(f"ckv_{h}", [P, KV_RANK // P, S], F32R) for h in ("hi", "lo")}
                k_rope, k_rot = mem("k_rope", [P, NS, ROPE]), mem("k_rot", [P, NS, ROPE])
                tab = [mem(f"rope_tab{n}", [P, NS, ROPE // 2]) for n in range(4)]
                k_ss = mem("k_ss", [P, NS])
                down_project(nc, f"{tag}q", k, w_in[:, 0:Q_RANK], Q_RANK, Q_RANK, a["mla_q_norm"][0], ht, cq, None,
                             mem.at, psum)
                down_project(nc, f"{tag}c", k, w_in[:, Q_RANK:q_mem_at], KV_RANK + ROPE, KV_RANK, a["mla_kv_norm"][0],
                             ht, ckv, k_rope, mem.at, psum)
                rotary_tables(nc, f"{tag}r", k, a["positions"], a["mla_g_qn"][0], a["mla_g_kn"][0], k_rope, tab, k_rot,
                              k_ss, mem.at)
                latent_heads(nc, f"{tag}a", k, a["mla_w_q_up"][0], a["mla_w_kv_up"][0], a["mla_g_qn"][0],
                             a["mla_g_kn"][0], cq, ckv, tab, k_rot, k_ss, mem.at, psum, ot_dram)
            project_and_swiglu(nc, f"{tag}f", k, x, x_dram, ot_dram, a["w_out"][layer], a["ln_ffn"][layer],
                               a["w_ffn_gu"][layer], a["w_ffn_down"][layer], ht, psum,
                               x_mid if layer == 0 else out.rearrange("b s d -> (b s) d"))


_INS = ["x", "mem", "positions", "ln_attn", "w_out", "ln_mem", "w_mem_kv", "g_qn_mem", "g_kn_mem", "ln_ffn", "w_ffn_gu",
        "w_ffn_down", "sb_w_in", "mla_w_in", "mla_q_norm", "mla_w_q_up", "mla_kv_norm", "mla_w_kv_up", "mla_g_qn",
        "mla_g_kn"]


def kernel(**inputs):
    import numpy as _np
    import concourse.bacc as _bacc
    from concourse import mybir as _mybir
    from concourse.bass_utils import run_bass_kernel_spmd as _run

    nc = _bacc.Bacc("TRN2", target_bir_lowering=False, num_devices=1)
    arrays, args = {}, {}
    for name in _INS:
        v = _np.ascontiguousarray(inputs[name])
        arrays[f"in_{name}_dram"] = v
        args[name] = nc.dram_tensor(f"in_{name}_dram", v.shape, _mybir.dt.from_np(v.dtype), kind="ExternalInput").ap()
    out = nc.dram_tensor("out_0_dram", (1, S, D), F32, kind="ExternalOutput").ap()
    build(nc, args, out)
    r = _run(nc, [arrays], core_ids=[0])
    return r.results[0]["out_0_dram"]
```

```python
from contextlib import ExitStack

import concourse.bass as bass
import numpy as np
from concourse import mybir

P = 128
F32 = mybir.dt.float32
F32R = mybir.dt.float32r
I32 = mybir.dt.int32
ALU = mybir.AluOpType
ACT = mybir.ActivationFunctionType
AX = mybir.AxisListType.X

D = 1024
S = 1024
ND, NS = D // P, S // P
HALF = 512
DEPTH = 2
HD = 64
HEADS = 12
PAIRS = HEADS // 2
NOPE, ROPE = 64, 32
QK = NOPE + ROPE
Q_RANK, KV_RANK = 768, 256
MEM, MEM_HEADS = 256, 4
MEM_Q = MEM_HEADS * HD
FF = 2816
NF = FF // P
SB_Q = HEADS * HD
EPS = 1e-6
THETA = 10000.0
MASKED = -1e30

BASE = 16512
HT_AT = BASE
CONST_AT = HT_AT + 2 * ND * S * 4
WORK_AT = CONST_AT + 5 * 1024
X_AT = 229344 - NS * D * 4


class Memory:

    def __init__(self, nc, at, end):
        self.nc, self.at, self.end = nc, at, end

    def __call__(self, name, shape, dtype=F32):
        size = int(np.prod(shape[1:])) * 4
        t = self.nc.alloc_sbuf_tensor_at(name, shape, dtype, offset=self.at)
        self.at += (size + 31) // 32 * 32
        assert self.at <= self.end, (name, self.at, self.end)
        return t


class Phase(ExitStack):

    def __init__(self, nc):
        super().__init__()
        self.nc, self.semaphores = nc, []

    def semaphore(self, name):
        self.semaphores.append(self.nc.alloc_semaphore(name))
        return self.semaphores[-1]

    def __exit__(self, *exc):
        super().__exit__(*exc)
        if exc[0] is None:
            self.nc.clear_and_free_semaphores(self.semaphores)
            self.nc.all_engine_barrier()


def as_f32(ap):
    return ap.bitcast(F32)


def product3(pe, out, l_hi, l_lo, r_hi, r_lo, first, last):
    pe.matmul(out, l_hi, r_hi, start=first, stop=False, skip_group_check=True)
    pe.matmul(out, l_hi, r_lo, start=False, stop=False, skip_group_check=True)
    return pe.matmul(out, l_lo, r_hi, start=False, stop=last, skip_group_check=True)


def make_constants(nc, k):
    with Phase(nc) as ctx:
        made = ctx.semaphore("const_made")
        filled = ctx.semaphore("const_filled")
        t = [k["ident"], k["tmp_strict"], k["tmp_causal"], k["tmp_upper"], k["tmp_lower"]]
        block = ctx.enter_context(nc.Block())

        @block.gpsimd
        def _(pool):
            for m, v in zip(t, (0.0, 0.0, 0.0, -1.0, -1.0)):
                pool.memset(m[:], v).then_inc(filled, 1)
            pool.wait_ge(filled, 5)
            pool.affine_select(out=t[0][:], in_=t[0][:], compare_op=ALU.not_equal, fill=1.0, base=0,
                               pattern=[[-1, P]], channel_multiplier=1).then_inc(made, 1)
            pool.affine_select(out=t[1][:], in_=t[1][:], compare_op=ALU.is_gt, fill=MASKED, base=0,
                               pattern=[[1, P]], channel_multiplier=-1).then_inc(made, 1)
            pool.affine_select(out=t[2][:], in_=t[2][:], compare_op=ALU.is_ge, fill=MASKED, base=0,
                               pattern=[[-1, P]], channel_multiplier=1).then_inc(made, 1)
            pool.affine_select(out=t[3][:], in_=t[3][:], compare_op=ALU.is_ge, fill=0.0, base=0,
                               pattern=[[-1, P]], channel_multiplier=1).then_inc(made, 1)
            pool.affine_select(out=t[4][:], in_=t[4][:], compare_op=ALU.is_gt, fill=0.0, base=0,
                               pattern=[[1, P]], channel_multiplier=-1).then_inc(made, 1)

        @block.vector
        def _(dve):
            dve.wait_ge(made, 5)
            dve.memset(k["eps"][:], EPS)
            for name, src in (("ident_r", t[0]), ("strict", t[1]), ("causal", t[2]),
                              ("upper", t[3]), ("lower", t[4])):
                dve.tensor_copy(k[name][:], src[:])


def gain_columns(gain):
    return gain.rearrange("(c p) -> p c", p=P)


def project_and_swiglu(nc, tag, k, x, x_dram, ot_dram, w_out, gain, w_gu, w_down, ht, psum, store_to):
    KB = 1024
    def place(name, at, shape, dtype=F32):
        return Memory(nc, WORK_AT + at * KB, X_AT)(f"{tag}_{name}", shape, dtype)

    gu_raw = [place(f"gu_raw{s}", 8 * s, [P, ND, 2, P]) for s in range(2)]
    gu_hi = [place(f"gu_hi{s}", 16 + 16 * s, [P, ND, 2, P], F32R) for s in range(2)]
    gu_lo = [place(f"gu_lo{s}", 24 + 16 * s, [P, ND, 2, P], F32R) for s in range(2)]
    dn_raw = [place(f"dn_raw{s}", 48 + 4 * s, [P, D]) for s in range(2)]
    dn_hi = [place(f"dn_hi{s}", 56 + 8 * s, [P, D], F32R) for s in range(2)]
    dn_lo = [place(f"dn_lo{s}", 60 + 8 * s, [P, D], F32R) for s in range(2)]
    a_hi = [place(f"a_hi{s}", 72 + 8 * s, [P, S], F32R) for s in range(2)]
    a_lo = [place(f"a_lo{s}", 76 + 8 * s, [P, S], F32R) for s in range(2)]
    hidden = place("hidden", 92, [P, 2, HALF])
    gate = place("gate", 100, [P, 2, HALF])
    w_raw = [place(f"w_raw{s}", 4 * s, [P, D]) for s in range(2)]
    o_raw = [place(f"o_raw{s}", 8 + 4 * s, [P, S]) for s in range(3)]
    w_hi = [place(f"w_hi{c}", 20 + 8 * c, [P, D], F32R) for c in range(ND)]
    w_lo = [place(f"w_lo{c}", 24 + 8 * c, [P, D], F32R) for c in range(ND)]
    xn = place("xn", 84, [P, 4, D])
    junk = place("junk", 100, [P, D])
    small = Memory(nc, WORK_AT + 104 * KB, X_AT)
    ss, std, rstd = (small(f"{tag}_{n}", [P, NS]) for n in ("ss", "std", "rstd"))
    gcol = small(f"{tag}_gcol", [P, ND])
    ot = ht
    gu_rows = w_gu.rearrange("(c p) f -> p c f", p=P)
    outs = [(t, n) for t in range(NS) for n in range(D // HALF)]
    NOUT = len(outs)
    four = lambda g: slice(4 * g, 4 * g + 4)
    group = lambda g: slice(g * HALF, (g + 1) * HALF)
    mix_bank = lambda n: n if n < 8 else n - 8
    norm_bank = lambda g, c: 4 * g + c % 4
    with Phase(nc) as ctx:
        sem = lambda n: ctx.semaphore(f"{tag}_{n}")
        x_in = [sem(f"x_in{t}") for t in range(NS)]
        w_in, o_in = [sem(f"w_in{s}") for s in range(2)], [sem(f"o_in{s}") for s in range(3)]
        (g_in, w_hi_done, w_lo_done, o_hi_done, o_lo_done, w_used, made, mixed, squared, root, inverse, normed, turned,
         hi_done, lo_done) = (
            sem(n) for n in ("g_in", "w_hi_done", "w_lo_done", "o_hi_done", "o_lo_done", "w_used", "made", "mixed",
                             "squared", "root", "inverse", "normed", "turned", "hi_done", "lo_done"))
        gu_in = [sem(f"gu_in{s}") for s in range(2)]
        dn_in = [sem(f"dn_in{s}") for s in range(2)]
        gu_hi_done, gu_lo_done, dn_hi_done, dn_lo_done = (
            sem("gu_hi_done"), sem("gu_lo_done"), sem("dn_hi_done"), sem("dn_lo_done"))
        gu_made, silu_done, hid_done, a_hi_done, a_lo_done, dn_made, added, stored = (
            sem("gu_made"), sem("silu_done"), sem("hid_done"), sem("a_hi_done"), sem("a_lo_done"),
            sem("dn_made"), sem("added"), sem("stored"))
        block = ctx.enter_context(nc.Block())

        def chunks(eng, step):
            for s in range(2):
                step(0, s, True, False)
            with eng.Fori(1, NF // 2 - 1) as i:
                for s in range(2):
                    step(i, s, False, False)
            for s in range(2):
                step(NF // 2 - 1, s, False, s == 1)

        def following(i, s):
            return (i, 1) if s == 0 else (i + 1, 0)

        @block.sync
        def _(sp):
            def load_gu(i, s):
                for half in range(2):
                    sp.dma_start(gu_raw[s][:, :, half, :],
                                 gu_rows[:, :, bass.ds((2 * i + s) * P + half * FF, P)]).then_inc(gu_in[s], 16)

            def load_dn(i, s):
                sp.dma_start(dn_raw[s][:], w_down[bass.ds((2 * i + s) * P, P), :]).then_inc(dn_in[s], 16)

            for c in range(ND):
                if c >= 2:
                    sp.wait_ge(w_lo_done, c - 1)
                sp.dma_start(w_raw[c % 2][:], w_out[c * P:(c + 1) * P, :]).then_inc(w_in[c % 2], 16)
                if c >= 3:
                    sp.wait_ge(o_lo_done, c - 2)
                sp.dma_start(o_raw[c % 3][:], ot_dram[c * P:(c + 1) * P, :]).then_inc(o_in[c % 3], 16)
            for t in range(NS):
                sp.dma_start(x[:, t, :], x_dram[t * P:(t + 1) * P, :]).then_inc(x_in[t], 16)
            with nc.allow_non_contiguous_dma("gain"):
                sp.dma_start(gcol[:], gain_columns(gain)).then_inc(g_in, 16)
            sp.wait_ge(w_lo_done, ND)
            sp.wait_ge(o_lo_done, ND)
            for s in range(2):
                load_gu(0, s)
            for s in range(2):
                sp.wait_ge(w_used, 4 + s)
                load_dn(0, s)
            with sp.Fori(1, NF // 2) as i:
                for s in range(2):
                    sp.wait_ge(gu_lo_done, 2 * i + s - 1)
                    sp.wait_ge(dn_lo_done, 2 * i + s - 1)
                    load_gu(i, s)
                    load_dn(i, s)
            for t in range(NS):
                sp.wait_ge(added, (NF - 1) * NOUT + 2 * (t + 1))
                sp.dma_start(store_to[t * P:(t + 1) * P, :], x[:, t, :]).then_inc(stored, 16)
            sp.wait_ge(stored, 16 * NS)

        @block.gpsimd
        def _(pool):
            def lower_gu(i, s):
                pool.wait_ge(gu_hi_done, 2 * i + s + 1)
                pool.tensor_tensor(gu_lo[s][:], gu_raw[s][:], as_f32(gu_hi[s][:]),
                                   ALU.subtract).then_inc(gu_lo_done, 1)

            def step(i, s, first, last):
                pool.wait_ge(dn_hi_done, 2 * i + s + 1)
                pool.tensor_tensor(dn_lo[s][:], dn_raw[s][:], as_f32(dn_hi[s][:]),
                                   ALU.subtract).then_inc(dn_lo_done, 1)
                if not last:
                    lower_gu(*following(i, s))

            for c in range(ND):
                pool.wait_ge(w_hi_done, c + 1)
                pool.tensor_tensor(w_lo[c][:], w_raw[c % 2][:], as_f32(w_hi[c][:]), ALU.subtract).then_inc(w_lo_done, 1)
            lower_gu(0, 0)
            chunks(pool, step)

        @block.scalar
        def _(act):
            def upper_gu(i, s, first):
                act.wait_ge(gu_in[s], 32 * (i + 1))
                if not first:
                    act.wait_ge(gu_made, 4 * (2 * i + s - 1))
                act.activation(gu_hi[s][:], gu_raw[s][:], ACT.Copy).then_inc(gu_hi_done, 1)

            def step(i, s, first, last):
                f = 2 * i + s
                act.wait_ge(dn_in[s], 16 * (i + 1))
                if not first:
                    act.wait_ge(dn_made, NOUT * (f - 1))
                act.activation(dn_hi[s][:], dn_raw[s][:], ACT.Copy).then_inc(dn_hi_done, 1)
                if not last:
                    upper_gu(*following(i, s), first and s == 0)
                for h in range(2):
                    act.wait_ge(gu_made, 4 * f + 2 * h + 1)
                    if not first or s:
                        act.wait_ge(hid_done, 2 * f + h - 1)
                    act.activation(gate[:, h, :], psum[2 * h][:], ACT.Silu).then_inc(silu_done, 1)
                    act.wait_ge(hid_done, 2 * f + h + 1)
                    act.activation(a_hi[s][:, h * HALF:(h + 1) * HALF], hidden[:, h, :],
                                   ACT.Copy).then_inc(a_hi_done, 1)

            def squares(t):
                act.wait_ge(mixed, 2 * (t + 1))
                if t:
                    act.wait_ge(squared, t)
                act.activation(junk[:], x[:, t, :], ACT.Square, accum_out=ss[:, t:t + 1]).then_inc(squared, 1)

            def deviations(g):
                act.wait_ge(squared, 4 * (g + 1))
                act.activation(std[:, four(g)], ss[:, four(g)], ACT.Sqrt, bias=k["eps"][:, 0:1],
                               scale=1.0 / D).then_inc(root, 1)

            def upper_normed(g, c):
                act.wait_ge(turned, ND * g + c + 1)
                act.activation(ht["hi"][:, c, group(g)], psum[norm_bank(g, c)][:], ACT.Copy,
                               scale=gcol[:, c:c + 1]).then_inc(hi_done, 1)

            for c in range(ND):
                act.wait_ge(w_in[c % 2], 16 * (c // 2 + 1))
                act.activation(w_hi[c][:], w_raw[c % 2][:], ACT.Copy).then_inc(w_hi_done, 1)
                act.wait_ge(o_in[c % 3], 16 * (c // 3 + 1))
                act.activation(ot["hi"][:, c, :], o_raw[c % 3][:], ACT.Copy).then_inc(o_hi_done, 1)
            for t in range(4):
                squares(t)
            deviations(0)
            for t in (4, 5):
                squares(t)
            act.wait_ge(g_in, 16)
            for c in range(ND):
                upper_normed(0, c)
                if c == 2:
                    act.wait_ge(w_used, 2)
                    upper_gu(0, 0, True)
            for t in (6, 7):
                squares(t)
            deviations(1)
            for c in range(ND):
                upper_normed(1, c)
            chunks(act, step)

        @block.vector
        def _(dve):
            def add(f):
                for n, (t, half) in enumerate(outs):
                    dve.wait_ge(dn_made, NOUT * f + n + 1)
                    cols = slice(half * HALF, (half + 1) * HALF)
                    dve.tensor_tensor(x[:, t, cols], psum[4 + n % 4][:], x[:, t, cols], ALU.add).then_inc(added, 1)

            def step(i, s, first, last):
                f = 2 * i + s
                for h in range(2):
                    dve.wait_ge(silu_done, 2 * f + h + 1)
                    dve.wait_ge(gu_made, 4 * f + 2 * h + 2)
                    if not first or s:
                        dve.wait_ge(a_lo_done, 2 * f + h - 1)
                    dve.tensor_tensor(hidden[:, h, :], psum[2 * h + 1][:], gate[:, h, :],
                                      ALU.mult).then_inc(hid_done, 1)
                    dve.wait_ge(a_hi_done, 2 * f + h + 1)
                    cols = slice(h * HALF, (h + 1) * HALF)
                    if not first:
                        dve.wait_ge(dn_made, NOUT * (f - 1))
                    dve.tensor_tensor(a_lo[s][:, cols], hidden[:, h, :], as_f32(a_hi[s][:, cols]),
                                      ALU.subtract).then_inc(a_lo_done, 1)
                if not first or s:
                    add(f - 1)

            def mix(tiles):
                for t in tiles:
                    dve.wait_ge(x_in[t], 16)
                    for half in range(2):
                        n, cols = 2 * t + half, slice(half * HALF, (half + 1) * HALF)
                        dve.wait_ge(made, n + 1)
                        dve.tensor_tensor(x[:, t, cols], psum[mix_bank(n)][:], x[:, t, cols], ALU.add).then_inc(mixed, 1)

            def normalise(g):
                dve.wait_ge(root, g + 1)
                dve.reciprocal(rstd[:, four(g)], std[:, four(g)]).then_inc(inverse, 1)
                dve.wait_ge(inverse, g + 1)
                for t in range(4 * g, 4 * g + 4):
                    dve.tensor_scalar(xn[:, t % 4, :], x[:, t, :], rstd[:, t:t + 1], None, ALU.mult).then_inc(normed, 1)

            def lower_normed(g):
                for c in range(ND):
                    dve.wait_ge(hi_done, ND * g + c + 1)
                    dve.scalar_tensor_tensor(ht["lo"][:, c, group(g)], psum[norm_bank(g, c)][:], gcol[:, c:c + 1],
                                             as_f32(ht["hi"][:, c, group(g)]), ALU.mult, ALU.subtract).then_inc(lo_done, 1)

            for c in range(ND):
                dve.wait_ge(o_hi_done, c + 1)
                dve.tensor_tensor(ot["lo"][:, c, :], o_raw[c % 3][:], as_f32(ot["hi"][:, c, :]),
                                  ALU.subtract).then_inc(o_lo_done, 1)
            mix((0, 1, 2, 3))
            normalise(0)
            mix((4, 5))
            lower_normed(0)
            mix((6, 7))
            normalise(1)
            lower_normed(1)
            chunks(dve, step)
            add(NF - 1)

        @block.tensor
        def _(pe):
            def gate_up(i, s, first, halves=(0, 1)):
                f = 2 * i + s
                pe.wait_ge(gu_lo_done, f + 1)
                for h in halves:
                    if not first:
                        pe.wait_ge(hid_done, 2 * f + h - 1)
                    for b in range(2):
                        for c in range(ND):
                            cols = slice(h * HALF, (h + 1) * HALF)
                            last = product3(pe, psum[2 * h + b][:], gu_hi[s][:, c, b, :], gu_lo[s][:, c, b, :],
                                            ht["hi"][:, c, cols], ht["lo"][:, c, cols], c == 0, c == ND - 1)
                        last.then_inc(gu_made, 1)

            def step(i, s, first, last_chunk):
                f = 2 * i + s
                if not last_chunk:
                    gate_up(*following(i, s), False)
                pe.wait_ge(dn_lo_done, f + 1)
                pe.wait_ge(a_lo_done, 2 * f + 2)
                for n, (t, half) in enumerate(outs):
                    if not (first and s == 0 and n < 4):
                        pe.wait_ge(added, NOUT * f + n - 3)
                    cols = slice(half * HALF, (half + 1) * HALF)
                    rows = slice(t * P, (t + 1) * P)
                    product3(pe, psum[4 + n % 4][:], a_hi[s][:, rows], a_lo[s][:, rows], dn_hi[s][:, cols],
                             dn_lo[s][:, cols], True, True).then_inc(dn_made, 1)

            def turn(g, c):
                n = ND * g + c
                pe.wait_ge(normed, 4 * (g + 1))
                if c < 4:
                    pe.wait_ge(mixed, 9 + c if g == 0 else 13 + c)
                else:
                    pe.wait_ge(lo_done, n - 3)
                for i in range(4):
                    last = pe.transpose(psum[norm_bank(g, c)][:, i * P:(i + 1) * P], xn[:, i, c * P:(c + 1) * P],
                                        k["ident"][:])
                last.then_inc(turned, 1)

            for wave, ns in enumerate((range(8), range(8, 12), range(12, 16))):
                for c in range(ND):
                    pe.wait_ge(w_lo_done, c + 1)
                    pe.wait_ge(o_lo_done, c + 1)
                    for n in ns:
                        t, half = n // 2, n % 2
                        if wave and c == 0:
                            pe.wait_ge(mixed, n - 7)
                        cols, rows = slice(half * HALF, (half + 1) * HALF), slice(t * P, (t + 1) * P)
                        last = product3(pe, psum[mix_bank(n)][:], ot["hi"][:, c, rows], ot["lo"][:, c, rows],
                                        w_hi[c][:, cols], w_lo[c][:, cols], c == 0, c == ND - 1)
                        if c == ND - 1:
                            last.then_inc(made, 1)
                    if wave == 2:
                        if c < ND - 1:
                            last.then_inc(w_used, 1)
                        turn(0, c)
            pe.wait_ge(lo_done, ND)
            gate_up(0, 0, True, (0,))
            for c in range(ND):
                turn(1, c)
            pe.wait_ge(lo_done, 2 * ND)
            gate_up(0, 0, True, (1,))
            chunks(pe, step)


class Attend:

    def __init__(self, nc, ctx, tag, mem, psum, k, jobs, keys_of, blocks_of, causal, scores, values, store,
                 rows_mem, ring, score_banks, out_banks=(6, 7), plan=None, extras={}):
        self.nc, self.k, self.jobs, self.causal, self.ring = nc, k, jobs, causal, ring
        self.keys_of, self.blocks_of, self.scores, self.values, self.store = keys_of, blocks_of, scores, values, store
        self.p = [[rows_mem(f"{tag}_p{n}_{i}", [P, keys_of(4 * jobs[n][1] + i)]) for i in range(4)] for n in range(ring)]
        self.pt_hi = [mem(f"{tag}_pt_hi{s}", [P, HALF], F32R) for s in range(2)]
        self.pt_lo = [mem(f"{tag}_pt_lo{s}", [P, HALF], F32R) for s in range(2)]
        self.nmx, self.rsum, self.rinv = (mem(f"{tag}_{n}", [P, 4]) for n in ("nmx", "rsum", "rinv"))
        self.o_tmp = mem(f"{tag}_o_tmp", [HD, HALF])
        self.o_out = [mem(f"{tag}_o_out{s}", [HD, HALF]) for s in range(2)]
        self.s_ps = score_banks
        self.t_ps = [psum[4], psum[5]]
        self.o_ps = [psum[b] for b in out_banks]
        (self.scores_made, self.nmax_done, self.exp_done, self.inv_done, self.rows_done,
         self.turned, self.hi_done, self.split_done, self.pv_made, self.tmp_done, self.out_done) = (
            ctx.semaphore(f"{tag}_{n}") for n in (
                "scores_made", "nmax_done", "exp_done", "inv_done", "rows_done", "turned",
                "hi_done", "split_done", "pv_made", "tmp_done", "out_done"))
        self.stored = [ctx.semaphore(f"{tag}_stored{s}") for s in range(2)]
        self.ns, self.nj = 4 * len(jobs), len(jobs)
        self.first = [sum(blocks_of(half) for _, half in jobs[:n]) for n in range(len(jobs) + 1)]
        self.nt = self.first[-1]

        if plan is None:
            plan = [6] + [min(self.ns, 4 * n + 6 + 4 * (j + 1) // blocks_of(half)) for n, (h, half) in enumerate(jobs)
                          for j in range(blocks_of(half))]
        steps, made, exps, inverses, rows = [], 0, 0, 0, 0

        def score_up_to(count):
            nonlocal made
            while made < count:
                exp_up_to(made)
                row_up_to(made - 1)
                steps.append(("S", made // 4, made % 4))
                made += 1

        def exp_up_to(count):
            nonlocal exps
            while exps < count:
                steps.append(("P", exps // 4, exps % 4))
                exps += 1

        def inverse_up_to(count):
            nonlocal inverses
            exp_up_to(count)
            while inverses < count:
                steps.append(("I", inverses // 4, inverses % 4))
                inverses += 1

        def row_up_to(count):
            nonlocal rows
            inverse_up_to(count)
            while rows < count:
                steps.append(("R", rows // 4, rows % 4))
                rows += 1

        score_up_to(plan[0])
        row_up_to(plan[0])
        self.opening, steps = steps, []
        for n in range(self.nj):
            blocks = blocks_of(jobs[n][1])
            for j in range(blocks):
                tau = self.first[n] + j
                row_up_to(max(rows, 4 * n + 4))
                inverse_up_to(exps - 1)
                steps.append(("T", n, j, tau))
                if tau:
                    steps.append(("V",) + self.of(tau - 1))
                    if j == 0:
                        steps.append(("E", n - 1))
                exp_up_to(made)
                score_up_to(plan[tau + 1])
                steps += [("X", x) for x in extras.get(tau, ())]
        steps += [("V",) + self.of(self.nt - 1), ("E", self.nj - 1)]
        row_up_to(plan[-1])
        self.steps = steps
        self.closing = [s for s in steps if s[0] not in "SPIR" or s[1] < self.nj]

    def of(self, tau):
        n = max(m for m in range(self.nj) if self.first[m] <= tau)
        return n, tau - self.first[n], tau

    def columns(self, n, j):
        return max(0, j - 4 * self.jobs[n][1]) * P if self.causal else 0

    def pe(self, pe, steps, turn=0, extra=None):
        for kind, *step in steps:
            if kind == "S":
                n, i = step
                s, (h, half) = 4 * n + i, self.jobs[n % self.nj]
                if s >= len(self.s_ps):
                    pe.wait_ge(self.exp_done, turn * self.ns + s - len(self.s_ps) + 1)
                self.scores(pe, h, 4 * half + i, self.s_ps[s % len(self.s_ps)]).then_inc(self.scores_made, 1)
            elif kind == "T":
                n, j, tau = step
                pe.wait_ge(self.rows_done, turn * self.ns + 4 * n + 4)
                if tau >= 2:
                    pe.wait_ge(self.split_done, turn * self.nt + tau - 1)
                for i in range(self.columns(n, j) // P, 4):
                    last = pe.transpose(self.t_ps[tau % 2][:, i * P:(i + 1) * P],
                                        self.p[n % self.ring][i][:, j * P:(j + 1) * P], self.k["ident"][:])
                last.then_inc(self.turned, 1)
            elif kind == "V":
                n, j, tau = step
                c0, h, o = self.columns(n, j), self.jobs[n][0], self.o_ps[n % len(self.o_ps)]
                pe.wait_ge(self.split_done, turn * self.nt + tau + 1)
                if j == 0:
                    pe.wait_ge(self.out_done, 1 + turn * self.nj + max(n + 1 - len(self.o_ps), 0))
                pe.matmul(o[:, c0:HALF], self.values(h, j), self.pt_hi[tau % 2][:, c0:HALF],
                          start=j == 0, stop=False, skip_group_check=True)
                pe.matmul(o[:, c0:HALF], self.values(h, j), self.pt_lo[tau % 2][:, c0:HALF], start=False,
                          stop=tau + 1 == self.first[n + 1], skip_group_check=True).then_inc(self.pv_made, 1)
            elif kind == "X" and extra:
                extra(pe, step[0], turn)

    def act(self, act, steps, turn=0, extra=None):
        for kind, *step in steps:
            if kind == "P":
                n, i = step
                s, keys = 4 * n + i, self.keys_of(4 * self.jobs[n % self.nj][1] + i)
                act.wait_ge(self.nmax_done, turn * self.ns + s + 1)
                if n >= self.ring:
                    act.wait_ge(self.turned, turn * self.nt + self.first[n - self.ring + 1])
                act.activation(self.p[n % self.ring][i][:, 0:keys], self.s_ps[s % len(self.s_ps)][:, 0:keys], ACT.Exp,
                               bias=self.nmx[:, s % 4:s % 4 + 1],
                               accum_out=self.rsum[:, s % 4:s % 4 + 1]).then_inc(self.exp_done, 1)
            elif kind == "T":
                n, j, tau = step
                c0 = self.columns(n, j)
                act.wait_ge(self.turned, turn * self.nt + tau + 1)
                act.wait_ge(self.pv_made, 1 + turn * self.nt + max(tau - 1, 0))
                act.activation(self.pt_hi[tau % 2][:, c0:HALF], self.t_ps[tau % 2][:, c0:HALF],
                               ACT.Copy).then_inc(self.hi_done, 1)
            elif kind == "E":
                n = step[0]
                act.wait_ge(self.pv_made, 1 + turn * self.nt + self.first[n + 1])
                act.wait_ge(self.out_done, 1 + turn * self.nj + n)
                act.activation(self.o_tmp[:], self.o_ps[n % len(self.o_ps)][HD:2 * HD, :], ACT.Copy).then_inc(self.tmp_done, 1)
            elif kind == "X" and extra:
                extra(act, step[0], turn)

    def dve(self, dve, steps, turn=0, extra=None):
        for kind, *step in steps:
            if kind == "S":
                n, i = step
                s, keys = 4 * n + i, self.keys_of(4 * self.jobs[n % self.nj][1] + i)
                one = slice(s % 4, s % 4 + 1)
                dve.wait_ge(self.scores_made, turn * self.ns + s + 1)
                dve.tensor_reduce(self.nmx[:, one], self.s_ps[s % len(self.s_ps)][:, 0:keys], AX, ALU.max,
                                  negate=True).then_inc(self.nmax_done, 1)
            elif kind == "I":
                s = 4 * step[0] + step[1]
                one = slice(s % 4, s % 4 + 1)
                dve.wait_ge(self.exp_done, turn * self.ns + s + 1)
                dve.reciprocal(self.rinv[:, one], self.rsum[:, one]).then_inc(self.inv_done, 1)
            elif kind == "R":
                n, i = step
                s = 4 * n + i
                one, row = slice(s % 4, s % 4 + 1), self.p[n % self.ring][i]
                dve.wait_ge(self.inv_done, turn * self.ns + s + 1)
                dve.tensor_scalar(row[:], row[:], self.rinv[:, one], None, ALU.mult).then_inc(self.rows_done, 1)
            elif kind == "T":
                n, j, tau = step
                c0 = self.columns(n, j)
                dve.wait_ge(self.hi_done, turn * self.nt + tau + 1)
                dve.tensor_tensor(self.pt_lo[tau % 2][:, c0:HALF], self.t_ps[tau % 2][:, c0:HALF],
                                  as_f32(self.pt_hi[tau % 2][:, c0:HALF]), ALU.subtract).then_inc(self.split_done, 1)
            elif kind == "E":
                n = step[0]
                dve.wait_ge(self.tmp_done, turn * self.nj + n + 1)
                dve.wait_ge(self.stored[n % 2], 16 + 16 * (turn * (self.nj // 2) + n // 2))
                dve.tensor_tensor(self.o_out[n % 2][:], self.o_ps[n % len(self.o_ps)][0:HD, :], self.o_tmp[:],
                                  ALU.add).then_inc(self.out_done, 1)
            elif kind == "X" and extra:
                extra(dve, step[0], turn)

    def begin(self, sp):
        for s in (self.pv_made, self.out_done):
            sp.sem_inc(s, 1)
        for s in self.stored:
            sp.sem_inc(s, 16)

    def sync(self, sp, turn=0):
        for n, (h, half) in enumerate(self.jobs):
            sp.wait_ge(self.out_done, 1 + turn * self.nj + n + 1)
            sp.dma_start(self.store(h, half, turn), self.o_out[n % 2][:]).then_inc(self.stored[n % 2], 16)

    def finish(self, sp, turns=1):
        for s in range(2):
            sp.wait_ge(self.stored[s], 16 + 16 * turns * (self.nj // 2))


def wide(ap, n, w):
    return ap.unsqueeze(2).broadcast_to([P, n, w])


def rows_of(ap, n, w):
    return ap.unsqueeze(1).broadcast_to([P, n, w])


def memory_heads(nc, tag, k, x, x_dram, ln, mem_dram, ln_mem, w_kv, g_q, g_k, w_q, ht, psum, ot_dram):
    KB = 1024
    def place(name, at, shape, dtype=F32):
        return Memory(nc, WORK_AT + at * KB, X_AT)(f"{tag}_{name}", shape, dtype)

    NM = MEM // P
    NKH, NQH = NM * MEM_HEADS, NS * MEM_HEADS
    QG = NQH // 2
    xn, junk = place("xn", 0, [P, 4, D]), place("junk", 16, [P, D])
    mem_x = place("mem_x", 20, [P, NM, D])
    mt = {h: place(f"mt_{h}", at, [P, ND, MEM], F32R) for h, at in (("hi", 28), ("lo", 36))}
    raw = [place(f"raw{s}", 44 + 8 * s, [P, ND // 2, 2 * MEM_Q]) for s in range(2)]
    w_hi = [place(f"wkv_hi{s}", 60 + 16 * s, [P, ND // 2, 2 * MEM_Q], F32R) for s in range(2)]
    w_lo = [place(f"wkv_lo{s}", 68 + 16 * s, [P, ND // 2, 2 * MEM_Q], F32R) for s in range(2)]
    w_hi.append(place("wq_hi", 60, [P, ND, MEM_Q], F32R))
    w_lo.append(place("wq_lo", 68, [P, ND, MEM_Q], F32R))
    q32, k32 = place("q32", 92, [P, NQH, HD]), place("k32", 100, [P, NKH, 2, HD])
    q_sq = place("q_sq", 16, [P, QG, HD])
    k_hl = place("k_hl", 20, [P, 2, NKH, 2, HD], F32R)
    k_hh = place("k_hh", 28, [P, MEM_HEADS, MEM], F32R)
    k_ll = place("k_ll", 32, [P, MEM_HEADS, MEM], F32R)
    v = place("v", 36, [P, NM, MEM_HEADS, 2 * HD], F32R)
    k_sq = place("k_sq", 40, [P, NKH, HD])
    q_hl = place("q_hl", 52, [P, QG, 2, HD], F32R)
    q_st = place("q_st", 76, [P, MEM_HEADS, S], F32R)
    small = Memory(nc, WORK_AT + 104 * KB, X_AT)
    ss, std, rstd = (small(f"{tag}_{n}", [P, NS]) for n in ("ss", "std", "rstd"))
    mss, mstd, mrstd = (small(f"{tag}_{n}", [P, NM]) for n in ("mss", "mstd", "mrstd"))
    hss, hstd, hrstd = (small(f"{tag}_{n}", [P, NKH + NQH]) for n in ("hss", "hstd", "hrstd"))
    gcol, mcol = small(f"{tag}_gcol", [P, ND]), small(f"{tag}_mcol", [P, ND])
    gq, gk = small(f"{tag}_gq", [P, HD]), small(f"{tag}_gk", [P, HD])
    four = lambda g: slice(4 * g, 4 * g + 4)
    group = lambda g: slice(g * HALF, (g + 1) * HALF)
    keys, queries = slice(0, NKH), lambda g: slice(NKH + g * QG, NKH + (g + 1) * QG)
    with Phase(nc) as ctx:
        sem = lambda n: ctx.semaphore(f"{tag}_{n}")
        x_in = [sem(f"x_in{t}") for t in range(NS)] if x_dram is not None else None
        m_in, w_in = [sem(f"m_in{t}") for t in range(NM)], [sem(f"w_in{n}") for n in range(3)]
        g_in, m_squared, m_root, m_inverse, m_normed, m_turned, m_hi, m_lo, w_hi_done, w_lo_done, kv_made = (
            sem(n) for n in ("g_in", "m_squared", "m_root", "m_inverse", "m_normed", "m_turned", "m_hi", "m_lo",
                             "w_hi_done", "w_lo_done", "kv_made"))
        squared, root, inverse, normed, turned, hi_done, lo_done, q_made, q_out = (
            sem(n) for n in ("squared", "root", "inverse", "normed", "turned", "hi_done", "lo_done", "q_made", "q_out"))
        k_chain, k_sums, k_root, k_normed, k_hi, k_lo, q_squared, q_sums, q_root, q_chain, q_normed, q_hi, q_lo, h_turned = (
            sem(n) for n in ("k_chain", "k_sums", "k_root", "k_normed", "k_hi", "k_lo", "q_squared", "q_sums", "q_root",
                             "q_chain", "q_normed", "q_hi", "q_lo", "h_turned"))
        stacked = [sem(f"stacked{s}") for s in range(2)]
        block = ctx.enter_context(nc.Block())
        kk = k32[:, :, 0, :]
        v_flat = v[:].rearrange("p t h (a d) -> p (t h) a d", a=2)
        turns = [("k", a, t) for a in range(2) for t in range(NM)] + [("q", 0, t) for t in range(NS)]
        kv_rows, q_rows = w_kv.rearrange("(c p) n -> p c n", p=P), w_q.rearrange("(c p) n -> p c n", p=P)
        raws = [raw[0][:], raw[1][:], raw[0][:].rearrange("p c (a n) -> p (c a) n", a=2)]

        def stack_to(n):
            what, a, t = turns[n]
            dst = q_st if what == "q" else (k_hh, k_ll)[a]
            return dst[:, :, t * P:(t + 1) * P], psum[4 + n % 2][:].rearrange("p (h q) -> p h q", h=MEM_HEADS)

        @block.sync
        def _(sp):
            for t in range(NM):
                sp.dma_start(mem_x[:, t, :], mem_dram[t * P:(t + 1) * P, :]).then_inc(m_in[t], 16)
            sp.dma_start(raws[0], kv_rows[:, 0:ND // 2, :]).then_inc(w_in[0], 16)
            with nc.allow_non_contiguous_dma("gains"):
                sp.dma_start(mcol[:], gain_columns(ln_mem)).then_inc(g_in, 16)
                sp.dma_start(gcol[:], gain_columns(ln)).then_inc(g_in, 16)
            sp.dma_start(gq[:], g_q.partition_broadcast(P)).then_inc(g_in, 16)
            sp.dma_start(gk[:], g_k.partition_broadcast(P)).then_inc(g_in, 16)
            if x_dram is not None:
                for t in range(4):
                    sp.dma_start(x[:, t, :], x_dram[t * P:(t + 1) * P, :]).then_inc(x_in[t], 16)
            sp.dma_start(raws[1], kv_rows[:, ND // 2:ND, :]).then_inc(w_in[1], 16)
            if x_dram is not None:
                for t in range(4, NS):
                    sp.dma_start(x[:, t, :], x_dram[t * P:(t + 1) * P, :]).then_inc(x_in[t], 16)
            sp.wait_ge(w_lo_done, 1)
            sp.dma_start(raws[2], q_rows).then_inc(w_in[2], 16)

        @block.gpsimd
        def _(pool):
            for n in range(3):
                pool.wait_ge(w_hi_done, n + 1)
                pool.tensor_tensor(w_lo[n][:], raws[n], as_f32(w_hi[n][:]), ALU.subtract).then_inc(w_lo_done, 1)

        @block.scalar
        def _(act):
            def upper_weights(n):
                act.wait_ge(w_in[n], 16)
                act.activation(w_hi[n][:], raws[n], ACT.Copy).then_inc(w_hi_done, 1)

            def squares(g):
                for t in range(4 * g, 4 * g + 4):
                    if x_in:
                        act.wait_ge(x_in[t], 16)
                    if t:
                        act.wait_ge(squared, t)
                    act.activation(junk[:], x[:, t, :], ACT.Square, accum_out=ss[:, t:t + 1]).then_inc(squared, 1)
                act.wait_ge(squared, 4 * (g + 1))
                act.activation(std[:, four(g)], ss[:, four(g)], ACT.Sqrt, bias=k["eps"][:, 0:1],
                               scale=1.0 / D).then_inc(root, 1)

            def upper_normed(g):
                for c in range(ND):
                    n = ND * g + c
                    act.wait_ge(turned, n + 1)
                    act.activation(ht["hi"][:, c, group(g)], psum[n % 4][:], ACT.Copy,
                                   scale=gcol[:, c:c + 1]).then_inc(hi_done, 1)

            def queries_out(tiles):
                for t in tiles:
                    act.wait_ge(q_made, t + 1)
                    act.activation(q32[:, t * MEM_HEADS:(t + 1) * MEM_HEADS, :],
                                   psum[6 + t % 2][:, 0:MEM_Q].rearrange("p (h d) -> p h d", h=MEM_HEADS),
                                   ACT.Copy).then_inc(q_out, 1)

            def squares_of_queries(g):
                act.wait_ge(q_out, 4 * (g + 1))
                if g:
                    act.wait_ge(q_sums, g)
                act.activation(q_sq[:], q32[:, g * QG:(g + 1) * QG, :], ACT.Square).then_inc(q_squared, 1)

            def deviations_of_queries(g):
                act.wait_ge(q_sums, g + 1)
                act.activation(hstd[:, queries(g)], hss[:, queries(g)], ACT.Sqrt, bias=k["eps"][:, 0:1],
                               scale=1.0 / HD).then_inc(q_root, 1)

            def upper_queries(g):
                act.wait_ge(q_normed, g + 1)
                if g:
                    act.wait_ge(h_turned, 8)
                act.activation(q_hl[:, :, 0, :], q32[:, g * QG:(g + 1) * QG, :], ACT.Copy).then_inc(q_hi, 1)

            def stack(ns):
                for n in ns:
                    act.wait_ge(h_turned, n + 1)
                    dst, src = stack_to(n)
                    act.activation(dst, src, ACT.Copy).then_inc(stacked[n % 2], 1)

            for t in range(NM):
                act.wait_ge(m_in[t], 16)
                if t:
                    act.wait_ge(m_squared, t)
                act.activation(junk[:], mem_x[:, t, :], ACT.Square, accum_out=mss[:, t:t + 1]).then_inc(m_squared, 1)
            act.wait_ge(m_squared, NM)
            act.activation(mstd[:], mss[:], ACT.Sqrt, bias=k["eps"][:, 0:1], scale=1.0 / D).then_inc(m_root, 1)
            upper_weights(0)
            act.wait_ge(g_in, 64)
            for c in range(ND):
                act.wait_ge(m_turned, c + 1)
                act.activation(mt["hi"][:, c, :], psum[c % 4][:, 0:MEM], ACT.Copy, scale=mcol[:, c:c + 1]).then_inc(m_hi, 1)
            squares(0)
            upper_weights(1)
            upper_normed(0)
            squares(1)
            act.wait_ge(kv_made, 1)
            upper_weights(2)
            act.wait_ge(k_sums, 1)
            act.activation(hstd[:, keys], hss[:, keys], ACT.Sqrt, bias=k["eps"][:, 0:1], scale=1.0 / HD).then_inc(k_root, 1)
            act.wait_ge(k_normed, 1)
            for a in range(2):
                act.activation(k_hl[:, 0, :, a, :], kk, ACT.Copy).then_inc(k_hi, 1)
            act.activation(v_flat[:, :, 0, :], k32[:, :, 1, :], ACT.Copy).then_inc(k_hi, 1)
            queries_out(range(0, 4))
            squares_of_queries(0)
            upper_normed(1)
            deviations_of_queries(0)
            queries_out((4, 5))
            upper_queries(0)
            stack((0, 2))
            queries_out((6, 7))
            squares_of_queries(1)
            stack((4, 6))
            deviations_of_queries(1)
            upper_queries(1)
            stack((8, 10))

        @block.vector
        def _(dve):
            def normalise(g):
                dve.wait_ge(root, g + 1)
                dve.reciprocal(rstd[:, four(g)], std[:, four(g)]).then_inc(inverse, 1)
                dve.wait_ge(inverse, g + 1)
                for t in range(4 * g, 4 * g + 4):
                    dve.tensor_scalar(xn[:, t % 4, :], x[:, t, :], rstd[:, t:t + 1], None, ALU.mult).then_inc(normed, 1)

            def lower_normed(g):
                for c in range(ND):
                    n = ND * g + c
                    dve.wait_ge(hi_done, n + 1)
                    dve.scalar_tensor_tensor(ht["lo"][:, c, group(g)], psum[n % 4][:], gcol[:, c:c + 1],
                                             as_f32(ht["hi"][:, c, group(g)]), ALU.mult, ALU.subtract).then_inc(lo_done, 1)

            def sums_of_queries(g):
                dve.wait_ge(q_squared, g + 1)
                dve.tensor_reduce(hss[:, queries(g)], q_sq[:], AX, ALU.add).then_inc(q_sums, 1)

            def normalise_queries(g):
                part = q32[:, g * QG:(g + 1) * QG, :]
                dve.wait_ge(q_root, g + 1)
                dve.reciprocal(hrstd[:, queries(g)], hstd[:, queries(g)]).then_inc(q_chain, 1)
                dve.wait_ge(q_chain, 2 * g + 1)
                dve.tensor_tensor(part, part, wide(hrstd[:, queries(g)], QG, HD), ALU.mult).then_inc(q_chain, 1)
                dve.wait_ge(q_chain, 2 * g + 2)
                dve.tensor_tensor(part, part, rows_of(gq[:], QG, HD), ALU.mult).then_inc(q_normed, 1)

            def lower_queries(g):
                dve.wait_ge(q_hi, g + 1)
                dve.tensor_tensor(q_hl[:, :, 1, :], q32[:, g * QG:(g + 1) * QG, :], as_f32(q_hl[:, :, 0, :]),
                                  ALU.subtract).then_inc(q_lo, 1)

            def stack(ns):
                for n in ns:
                    dve.wait_ge(h_turned, n + 1)
                    dst, src = stack_to(n)
                    dve.tensor_copy(dst, src).then_inc(stacked[n % 2], 1)

            dve.wait_ge(m_root, 1)
            dve.reciprocal(mrstd[:], mstd[:]).then_inc(m_inverse, 1)
            dve.wait_ge(m_inverse, 1)
            for t in range(NM):
                dve.tensor_scalar(mem_x[:, t, :], mem_x[:, t, :], mrstd[:, t:t + 1], None, ALU.mult).then_inc(m_normed, 1)
            dve.wait_ge(g_in, 64)
            dve.tensor_scalar(gq[:], gq[:], float(HD) ** -0.5, None, ALU.mult).then_inc(k_chain, 1)
            for c in range(ND):
                dve.wait_ge(m_hi, c + 1)
                dve.scalar_tensor_tensor(mt["lo"][:, c, :], psum[c % 4][:, 0:MEM], mcol[:, c:c + 1],
                                         as_f32(mt["hi"][:, c, :]), ALU.mult, ALU.subtract).then_inc(m_lo, 1)
            normalise(0)
            lower_normed(0)
            normalise(1)
            dve.wait_ge(kv_made, 2)
            for t in range(NM):
                last = dve.tensor_copy(k32[:, t * MEM_HEADS:(t + 1) * MEM_HEADS, :, :],
                                       psum[4 + t][:].rearrange("p (h a d) -> p h a d", h=MEM_HEADS, a=2))
            last.then_inc(k_chain, 1)
            dve.wait_ge(k_chain, 2)
            dve.tensor_tensor(k_sq[:], kk, kk, ALU.mult).then_inc(k_chain, 1)
            dve.wait_ge(k_chain, 3)
            dve.tensor_reduce(hss[:, keys], k_sq[:], AX, ALU.add).then_inc(k_sums, 1)
            dve.wait_ge(k_root, 1)
            dve.reciprocal(hrstd[:, keys], hstd[:, keys]).then_inc(k_chain, 1)
            dve.wait_ge(k_chain, 4)
            dve.tensor_tensor(kk, kk, wide(hrstd[:, keys], NKH, HD), ALU.mult).then_inc(k_chain, 1)
            dve.wait_ge(k_chain, 5)
            dve.tensor_tensor(kk, kk, rows_of(gk[:], NKH, HD), ALU.mult).then_inc(k_normed, 1)
            dve.wait_ge(k_hi, 3)
            for a in range(2):
                dve.tensor_tensor(k_hl[:, 1, :, a, :], kk, as_f32(k_hl[:, 0, :, a, :]), ALU.subtract).then_inc(k_lo, 1)
            dve.tensor_tensor(v_flat[:, :, 1, :], k32[:, :, 1, :], as_f32(v_flat[:, :, 0, :]), ALU.subtract)
            sums_of_queries(0)
            lower_normed(1)
            normalise_queries(0)
            lower_queries(0)
            stack((1, 3))
            sums_of_queries(1)
            stack((5, 7))
            normalise_queries(1)
            lower_queries(1)
            stack((9, 11))

        @block.tensor
        def _(pe):
            def keys_and_values(part):
                pe.wait_ge(w_lo_done, part + 1)
                for t in range(NM):
                    for c in range(ND // 2):
                        cc, rows = part * (ND // 2) + c, slice(t * P, (t + 1) * P)
                        last = product3(pe, psum[4 + t][:], mt["hi"][:, cc, rows], mt["lo"][:, cc, rows],
                                        w_hi[part][:, c, :], w_lo[part][:, c, :], cc == 0, cc == ND - 1)
                last.then_inc(kv_made, 1)

            def turn(g):
                pe.wait_ge(normed, 4 * (g + 1))
                for c in range(ND):
                    n = ND * g + c
                    if n >= 4:
                        pe.wait_ge(lo_done, n - 3)
                    for i in range(4):
                        last = pe.transpose(psum[n % 4][:, i * P:(i + 1) * P], xn[:, i, c * P:(c + 1) * P], k["ident"][:])
                    last.then_inc(turned, 1)

            def project(tiles):
                for t in tiles:
                    if t >= 2:
                        pe.wait_ge(q_out, t - 1)
                    rows = slice(t * P, (t + 1) * P)
                    for c in range(ND):
                        last = product3(pe, psum[6 + t % 2][:, 0:MEM_Q], ht["hi"][:, c, rows], ht["lo"][:, c, rows],
                                        w_hi[2][:, c, :], w_lo[2][:, c, :], c == 0, c == ND - 1)
                    last.then_inc(q_made, 1)

            def turn_heads(ns):
                for n in ns:
                    what, a, t = turns[n]
                    if n >= 2:
                        pe.wait_ge(stacked[n % 2], n // 2)
                    for h in range(MEM_HEADS):
                        g = t * MEM_HEADS + h
                        src = q_hl[:, g % QG, :, :] if what == "q" else k_hl[:, a, g, :, :]
                        last = pe.transpose(psum[4 + n % 2][:, h * P:(h + 1) * P],
                                            as_f32(src.rearrange("p a d -> p (a d)")), k["ident"][:])
                    last.then_inc(h_turned, 1)

            pe.wait_ge(m_normed, NM)
            for c in range(ND):
                if c >= 4:
                    pe.wait_ge(m_lo, c - 3)
                for i in range(NM):
                    last = pe.transpose(psum[c % 4][:, i * P:(i + 1) * P], mem_x[:, i, c * P:(c + 1) * P], k["ident"][:])
                last.then_inc(m_turned, 1)
            pe.wait_ge(m_lo, ND)
            keys_and_values(0)
            turn(0)
            keys_and_values(1)
            pe.wait_ge(w_lo_done, 3)
            pe.wait_ge(lo_done, ND)
            project(range(0, 4))
            turn(1)
            pe.wait_ge(lo_done, 2 * ND)
            project((4, 5))
            pe.wait_ge(k_lo, 2)
            turn_heads(range(0, 4))
            project((6, 7))
            pe.wait_ge(q_lo, 1)
            turn_heads(range(4, 8))
            pe.wait_ge(q_lo, 2)
            turn_heads(range(8, 12))

    mem = Memory(nc, WORK_AT + 40 * KB, WORK_AT + 76 * KB)
    with Phase(nc) as ctx:
        def scores(pe, h, tile, out):
            rows = slice(tile * P, (tile + 1) * P)
            pe.matmul(out[:, 0:MEM], q_st[:, h, rows], k_hh[:, h, :], start=True, stop=False, skip_group_check=True)
            return pe.matmul(out[:, 0:MEM], q_st[:, h, rows], k_ll[:, h, :], start=False, stop=True, skip_group_check=True)

        jobs = [(h, half) for h in range(MEM_HEADS) for half in range(2)]
        at = Attend(nc, ctx, f"{tag}a", mem, psum, k, jobs, lambda tile: MEM, lambda half: MEM // P, False, scores,
                    lambda h, j: v[:, j, h, :],
                    lambda h, half, turn: ot_dram[SB_Q + h * HD:SB_Q + (h + 1) * HD, half * HALF:(half + 1) * HALF],
                    mem, 4, psum["pair"], plan=[8]+[min(32,8+2*(t+1)) for t in range(16)])
        block = ctx.enter_context(nc.Block())

        @block.sync
        def _(sp):
            at.begin(sp)
            at.sync(sp)
            at.finish(sp)

        @block.tensor
        def _(pe):
            at.pe(pe, at.opening + at.steps)

        @block.scalar
        def _(act):
            at.act(act, at.opening + at.steps)

        @block.vector
        def _(dve):
            at.dve(dve, at.opening + at.steps)



def stick_breaking(nc, tag, k, w_in_dram, ht, psum, ot_dram):
    mem = Memory(nc, WORK_AT, 229344)
    q_st = mem(f"{tag}_q_st", [P, 2, S], F32R)
    k_hh = mem(f"{tag}_k_hh", [P, 2, S], F32R)
    k_ll = mem(f"{tag}_k_ll", [P, 2, S], F32R)
    v = mem(f"{tag}_v", [P, NS, 2, 2 * HD])
    stage = [mem(f"{tag}_{n}32", [P, S]) for n in "qkv"]
    raw = [mem(f"{tag}_raw{i}", [P, ND, P]) for i in range(3)]
    w_hi = [mem(f"{tag}_w_hi{i}", [P, ND, P], F32R) for i in range(3)]
    w_lo = [mem(f"{tag}_w_lo{i}", [P, ND, P], F32R) for i in range(3)]
    NA, NR, NW = 3, 6, 3
    soft = [mem(f"{tag}_soft{s}", [P, HALF]) for s in range(NA)]
    run = [mem(f"{tag}_run{s}", [P, HALF]) for s in range(NR)]
    run_hi = [mem(f"{tag}_run_hi{s}", [P, HALF], F32R) for s in range(NR)]
    run_lo = [mem(f"{tag}_run_lo{s}", [P, HALF], F32R) for s in range(NR)]
    wt = [mem(f"{tag}_wt{s}", [P, HALF]) for s in range(NW)]
    o_out = [mem(f"{tag}_o_out{s}", [P, HALF]) for s in range(2)]
    rows = w_in_dram.rearrange("(c p) n -> p c n", p=P)

    blocks = [(c, j, h) for c in (1, 0) for j in reversed(range(4 * c + 4)) for h in range(2)]
    NB = len(blocks)
    NZ = 6
    out_bank, bank = psum[6], psum[7]
    first_col = [max(0, j - 4 * c) * P for c, j, h in blocks]
    chained = [b for b, (c, j, h) in enumerate(blocks) if j < 4 * c + 3]
    n_chained = [sum(1 for x in chained if x <= b) for b in range(NB)]
    NC = len(chained)
    START = {b: n for n, b in enumerate(b for b, (c, j, h) in enumerate(blocks) if j == 4 * c + 3 and h == 0)}
    END = {b: n for n, b in enumerate(b for b, (c, j, h) in enumerate(blocks) if j == 0 and h == 1)}
    LOW = next(b for b, (c, j, h) in enumerate(blocks) if j == 3)
    LAG_U, LAG_PV = 3, 4
    FIRST_USES = [("q", 1), ("k", 1), ("v", 1), ("turn", 1), ("q", 0), ("k", 0), ("v", 0)]
    USES = {("q", 1): 2, ("turn", 0): 4, ("k", 1): 7, ("v", 1): 10, ("turn", 1): 12, ("q", 0): 15, ("k", 0): 18, ("v", 0): 21}
    order = list(USES)
    F0, UN = len(FIRST_USES), len(USES)
    UPPER = (16, 19, 22)
    LOWER = {17: [(0, 0)], 18: [(0, 2)], 19: [(0, 4)], 20: [(0, 6), (1, 0)], 21: [(1, 2)], 22: [(1, 4), (1, 6)],
             23: [(2, c) for c in range(0, ND, 2)]}
    PARTS = [(0, 3), (3, 6), (6, ND)]
    with Phase(nc) as ctx:
        sem = lambda n: ctx.semaphore(f"{tag}_{n}")
        w_in = [sem(f"w_in{i}") for i in range(3)]
        w_hi_done = [sem(f"w_hi_done{i}") for i in range(3)]
        w_lo_done = [sem(f"w_lo_done{i}") for i in range(3)]
        (filled, emptied, split_hi, split_done, scores_made, abs_done, exp_done, soft_done, sp_done, run_added,
         run_hi_done, run_split, sums_made, weight_done, pv_made, out_done, cleared, lowered) = (
            sem(n) for n in ("filled", "emptied", "split_hi", "split_done", "scores_made", "abs_done", "exp_done",
                             "soft_done", "sp_done", "run_added", "run_hi_done", "run_split", "sums_made",
                             "weight_done", "pv_made", "out_done", "cleared",
                             "lowered"))
        stored = [sem(f"stored{s}") for s in range(2)]
        block = ctx.enter_context(nc.Block())

        def wait(eng, sem, g, per, n):
            if not isinstance(g, int) or per * g + n > 0:
                eng.wait_ge(sem, per * g + n)

        def pairs(eng, step):
            for t in range(NB):
                step(t, 0, False)
            with eng.Fori(1, PAIRS - 1) as g:
                for t in range(NB):
                    step(t, g, False)
            for t in range(NB + LAG_PV + 1):
                step(t, PAIRS - 1, True)

        def exists(b, g, last):
            return not (b < 0 and isinstance(g, int) and g == 0) and not (b >= NB and last)

        def uses(use, last):
            return 0 if last else order.index(use)

        @block.sync
        def _(sp):
            def load(i, g):
                sp.dma_start(raw[i][:], rows[:, :, bass.ds(g * P + i * SB_Q, P)]).then_inc(w_in[i], 16)

            def store(g):
                for n, c in enumerate((1, 0)):
                    sp.wait_ge(out_done, 2 * g + n + 1)
                    row = g * P if c else (g + 1) * P - P
                    sp.dma_start(ot_dram[bass.ds(row, P), c * HALF:(c + 1) * HALF], o_out[n][:]).then_inc(stored[n], 16)

            for i in range(3):
                load(i, 0)
            for i in range(3):
                sp.wait_ge(w_lo_done[i], 1)
                load(i, 1)
            with sp.Fori(0, PAIRS - 1) as g:
                for i in range(3):
                    sp.wait_ge(w_lo_done[i], g + 2)
                    load(i, g + 2)
                store(g)
            store(PAIRS - 1)
            for s in range(2):
                sp.wait_ge(stored[s], 16 * PAIRS)

        @block.gpsimd
        def _(pool):
            def lower(i, c, g):
                pool.wait_ge(w_hi_done[i], g + 1)
                ins = pool.tensor_tensor(w_lo[i][:, c:c + 2, :], raw[i][:, c:c + 2, :], as_f32(w_hi[i][:, c:c + 2, :]),
                                         ALU.subtract)
                if c == ND - 2:
                    ins.then_inc(w_lo_done[i], 1)

            def step(t, g, last):
                if t < NB:
                    f = first_col[t]
                    pool.wait_ge(run_hi_done, NB * g + t + 1)
                    wait(pool, sums_made, g, NB, t - NR + 3)
                    pool.tensor_tensor(run_lo[t % NR][:, f:HALF], run[t % NR][:, f:HALF],
                                       as_f32(run_hi[t % NR][:, f:HALF]), ALU.subtract).then_inc(run_split, 1)
                if not last:
                    for i, c in LOWER.get(t, ()):
                        lower(i, c, g + 2)

            for g in range(2):
                for i in range(3):
                    for c in range(0, ND, 2):
                        lower(i, c, g)
            pairs(pool, step)

        @block.scalar
        def _(act):
            def upper(i, g):
                act.wait_ge(w_in[i], 16 * (g + 1))
                act.activation(w_hi[i][:], raw[i][:], ACT.Copy).then_inc(w_hi_done[i], 1)

            def values(half, bank=bank):
                z = bank[:].rearrange("p (t h d) -> p t h d", h=2, d=HD)
                for h in range(2):
                    last = act.activation(v[:, 4 * half:4 * half + 4, h, h * HD:(h + 1) * HD], z[:, :, h, :], ACT.Copy)
                last.then_inc(emptied, 1)

            def magnitude(b, g):
                f, s = first_col[b % NB], soft[b % NA]
                act.wait_ge(scores_made, NB * g + b + 1)
                wait(act, sp_done, g, NB, b - NA + 1)
                act.activation(s[:, f:HALF], psum[b % NZ][:, f:HALF], ACT.Abs).then_inc(abs_done, 1)

            def beside(t, g, last):
                if t == USES["turn", 0]:
                    act.wait_ge(filled, UN * g + F0 + uses(("turn", 0), last) + 1)
                    wait(act, pv_made, g, NB, 0)
                    values(0)
                elif last:
                    return
                elif t == USES["turn", 1]:
                    act.wait_ge(filled, UN * g + F0 + uses(("turn", 1), last) + 1)
                    act.wait_ge(pv_made, NB * g + LOW)
                    values(1)
                if t in UPPER:
                    i = UPPER.index(t)
                    act.wait_ge(filled, UN * g + F0 + uses(("qkv"[i], 0), last) + 1)
                    upper(i, g + 2)

            def step(t, g, last):
                if t < NB:
                    f, s = first_col[t], soft[t % NA]
                    act.wait_ge(abs_done, NB * g + t + 1)
                    act.activation(s[:, f:HALF], s[:, f:HALF], ACT.Exp, scale=-1.0).then_inc(exp_done, 1)
                if exists(t + 1, g, last):
                    magnitude(t + 1, g)
                if t < NB:
                    act.wait_ge(exp_done, NB * g + t + 1)
                    act.activation(s[:, f:HALF], s[:, f:HALF], ACT.Ln, bias=1.0).then_inc(soft_done, 1)
                b = t - LAG_U
                if exists(b, g, last):
                    f = first_col[b % NB]
                    act.wait_ge(sums_made, NB * g + b + 1)
                    wait(act, pv_made, g, NB, b - NW + 1)
                    act.activation(wt[b % NW][:, f:HALF], psum[b % NZ][:, f:HALF], ACT.Exp).then_inc(weight_done, 1)
                beside(t, g, last)

            for i in range(3):
                upper(i, 0)
            act.wait_ge(filled, 4)
            act.wait_ge(cleared, 1)
            values(1, psum[3])
            for i in range(3):
                act.wait_ge(filled, 5 + i)
                upper(i, 1)
            act.preload_act_table_set("natural_log_exp_and_others")
            magnitude(0, 0)
            pairs(act, step)

        @block.vector
        def _(dve):
            def stage_out(what, half, bank=bank):
                dst, cols = stage["qkv".index(what)], slice(half * HALF, (half + 1) * HALF)
                if what == "q":
                    dve.tensor_scalar(dst[:, cols], bank[:], float(HD) ** -0.5, None, ALU.mult).then_inc(emptied, 1)
                else:
                    dve.tensor_copy(dst[:, cols], bank[:]).then_inc(emptied, 1)

            def upper_half(half, part):
                cols = slice(half * HALF, (half + 1) * HALF)
                if part == 0:
                    for h in range(2):
                        r = slice(h * HD, (h + 1) * HD)
                        last = dve.tensor_copy(q_st[r, h, cols], stage[0][r, cols])
                else:
                    r = slice((part - 1) * HD, part * HD)
                    for a in range(2):
                        last = dve.tensor_copy(k_hh[a * HD:(a + 1) * HD, part - 1, cols], stage[1][r, cols])
                last.then_inc(split_hi, 1)

            def lower_half(half, n, part):
                cols = slice(half * HALF, (half + 1) * HALF)
                dve.wait_ge(split_hi, 3 * n + part + 1)
                if part == 0:
                    for h in range(2):
                        r, o = slice(h * HD, (h + 1) * HD), slice((1 - h) * HD, (2 - h) * HD)
                        last = dve.tensor_tensor(q_st[o, h, cols], stage[0][r, cols], as_f32(q_st[r, h, cols]), ALU.subtract)
                else:
                    r = slice((part - 1) * HD, part * HD)
                    last = dve.tensor_tensor(k_ll[0:HD, part - 1, cols], stage[1][r, cols], as_f32(k_hh[r, part - 1, cols]),
                                             ALU.subtract)
                last.then_inc(lowered, 1)

            def repeat_lower(half, n, h):
                cols = slice(half * HALF, (half + 1) * HALF)
                dve.wait_ge(lowered, 3 * n + h + 2)
                ins = dve.tensor_copy(k_ll[HD:2 * HD, h, cols], as_f32(k_ll[0:HD, h, cols]))
                if h == 1:
                    ins.then_inc(split_done, 1)

            def halves(half, n, s):
                if s < 3:
                    upper_half(half, s)
                if 0 < s:
                    lower_half(half, n, s - 1)
                if s == 3:
                    for h in range(2):
                        repeat_lower(half, n, h)

            def beside(t, g, last):
                if t == 0:
                    dve.wait_ge(emptied, UN * g + F0)
                    wait(dve, scores_made, g, NB, 0)
                if t < 4:
                    halves(0, 2 * g + 1, t)
                if last:
                    return
                for use, at in USES.items():
                    if use[0] != "turn" and t == at:
                        dve.wait_ge(filled, UN * g + F0 + uses(use, last) + 1)
                        stage_out(*use)
                if t == 15:
                    dve.wait_ge(scores_made, NB * g + 16)
                if 15 <= t < 19:
                    halves(1, 2 * g + 2, t - 15)

            def step(t, g, last):
                if t < NB:
                    f, r = first_col[t], run[t % NR]
                    dve.wait_ge(soft_done, NB * g + t + 1)
                    wait(dve, run_split, g, NB, t - NR + 1)
                    dve.scalar_tensor_tensor(r[:, f:HALF], psum[t % NZ][:, f:HALF], 0.0,
                                             soft[t % NA][:, f:HALF], ALU.max, ALU.add).then_inc(sp_done, 1)
                b = t - 1
                if exists(b, g, last):
                    f, r = first_col[b % NB], run[b % NR]
                    if b % NB in chained:
                        dve.wait_ge(run_added, NC * g + n_chained[b % NB] - (NC if b < 0 else 0))
                    else:
                        dve.wait_ge(sp_done, NB * g + b + 1)
                    wait(dve, sums_made, g, NB, b - NR + 3)
                    dve.tensor_copy(run_hi[b % NR][:, f:HALF], r[:, f:HALF]).then_inc(run_hi_done, 1)
                if t in chained:
                    fn, r = first_col[t - 2], run[t % NR]
                    dve.wait_ge(sp_done, NB * g + t + 1)
                    dve.tensor_tensor(r[:, fn:HALF], r[:, fn:HALF], run[(t - 2) % NR][:, fn:HALF],
                                      ALU.add).then_inc(run_added, 1)
                b = t - LAG_PV + 0
                if b % NB in END and exists(b, g, last):
                    n = END[b % NB]
                    dve.wait_ge(pv_made, NB * g + b + 1)
                    wait(dve, stored[n], g, 16, -16 if b < 0 else 0)
                    dve.tensor_copy(o_out[n][:], out_bank[:]).then_inc(out_done, 1)
                beside(t, g, last)

            dve.memset(v[:], 0.0).then_inc(cleared, 1)
            for n, use in enumerate(FIRST_USES):
                if use[0] != "turn":
                    dve.wait_ge(filled, n + 1)
                    stage_out(*use, psum[n])
                if n == 2:
                    dve.wait_ge(emptied, 3)
                    for s in range(4):
                        halves(1, 0, s)
            pairs(dve, step)

        @block.tensor
        def _(pe):
            def project(what, half, chunks, g, bank=bank):
                i, cols = "qkv".index(what), slice(half * HALF, (half + 1) * HALF)
                if chunks[0] == 0:
                    pe.wait_ge(w_lo_done[i], g + 1)
                for c in range(*chunks):
                    last = product3(pe, bank[:], w_hi[i][:, c, :], w_lo[i][:, c, :],
                                    ht["hi"][:, c, cols], ht["lo"][:, c, cols], c == 0, c == ND - 1)
                if chunks[1] == ND:
                    last.then_inc(filled, 1)

            def turn(half, bank=bank):
                for i in range(4):
                    tt = 4 * half + i
                    last = pe.transpose(bank[:, i * P:(i + 1) * P], stage[2][:, tt * P:(tt + 1) * P], k["ident"][:])
                last.then_inc(filled, 1)

            def scores(b, g):
                c, j, h = blocks[b % NB]
                f, z = first_col[b % NB], psum[b % NZ]
                wait(pe, weight_done, g, NB, b - NZ + 1)
                if b % NB == 0:
                    pe.wait_ge(split_done, 2 * (g + b // NB) + 1)
                elif b == LOW:
                    pe.wait_ge(split_done, 2 * g + 2)
                q = q_st[:, h, c * HALF + f:(c + 1) * HALF]
                diagonal = j >= 4 * c
                pe.matmul(z[:, f:HALF], k_hh[:, h, j * P:(j + 1) * P], q, start=True, stop=False, skip_group_check=True)
                last = pe.matmul(z[:, f:HALF], k_ll[:, h, j * P:(j + 1) * P], q, start=False,
                                 stop=not diagonal, skip_group_check=True)
                if diagonal:
                    last = pe.matmul(z[:, f:f + P], k["ident_r"][:], k["strict"][:], start=False, stop=True,
                                     skip_group_check=True)
                last.then_inc(scores_made, 1)

            def beside(t, g, last):
                for use, at in USES.items():
                    if last and use != ("turn", 0):
                        continue
                    if use[0] == "turn":
                        if t == at:
                            pe.wait_ge(emptied, UN * g + F0 + uses(use, last))
                            turn(use[1])
                    elif at - 2 <= t <= at:
                        if t == at - 2:
                            pe.wait_ge(emptied, UN * g + F0 + uses(use, last))
                        project(*use, PARTS[t - at + 2], g + 1)

            def step(t, g, last):
                if exists(t + 1, g, last):
                    scores(t + 1, g)
                b = t - LAG_U
                if exists(b, g, last):
                    bb = b % NB
                    f, z, s = first_col[bb], psum[b % NZ], b % NR
                    pe.wait_ge(run_split, NB * g + b + 1)
                    pe.wait_ge(sp_done, NB * g + b + 1)
                    pe.matmul(z[:, f:HALF], k["upper"][:], run_hi[s][:, f:HALF], start=False, stop=False, skip_group_check=True)
                    ins = pe.matmul(z[:, f:HALF], k["upper"][:], run_lo[s][:, f:HALF], start=False,
                                    stop=bb not in chained, skip_group_check=True)
                    if bb in chained:
                        fn, s = first_col[bb - 2], (b - 2) % NR
                        pe.matmul(z[:, fn:HALF], k["lower"][:], run_hi[s][:, fn:HALF], start=False, stop=False, skip_group_check=True)
                        ins = pe.matmul(z[:, fn:HALF], k["lower"][:], run_lo[s][:, fn:HALF], start=False,
                                        stop=True, skip_group_check=True)
                    ins.then_inc(sums_made, 1)
                b = t - LAG_PV
                if exists(b, g, last):
                    bb = b % NB
                    c, j, h = blocks[bb]
                    f = first_col[bb]
                    pe.wait_ge(weight_done, NB * g + b + 1)
                    if bb in START:
                        wait(pe, out_done, g, 2, START[bb])
                    if b == 0:
                        pe.wait_ge(emptied, UN * g + 4)
                    elif b == LOW:
                        pe.wait_ge(emptied, UN * g + F0 + uses(("turn", 0), last) + 1)
                    pe.matmul(out_bank[:, f:HALF], v[:, j, h, :], wt[b % NW][:, f:HALF], start=bb in START,
                              stop=bb in END, skip_group_check=True).then_inc(pv_made, 1)
                beside(t, g, last)

            for n, (what, half) in enumerate(FIRST_USES):
                if what == "turn":
                    pe.wait_ge(emptied, n)
                    turn(half, psum[n])
                else:
                    project(what, half, (0, ND), 0, psum[n])
            pe.wait_ge(emptied, F0)
            scores(0, 0)
            pairs(pe, step)


TWO_PI = 6.283185307179586
TURN = (6.28125, float(np.float32(np.int64(0.0019353071795864769 * 2**22) / 2.0**22)))
TURN += (float(np.float32(TWO_PI - TURN[0] - TURN[1])),)
ROUND = 1.5 * 2.0**23
PI_IN = 3.1415925


def latent_inputs(nc, tag, k, w_dram, q_gain, kv_gain, positions, g_q, g_k, ht, cq, ckv, k_rope, tab, k_rot, k_ss, at, psum):
    H = ROPE // 2
    NQ, NK, KVW = Q_RANK // P, KV_RANK // P, KV_RANK + ROPE
    PW = Q_RANK // 2
    mem = Memory(nc, at, 229344)
    wq_raw = [mem(f"{tag}_wq_raw{s}", [P, Q_RANK]) for s in range(2)]
    wq_hi, wq_lo = (mem(f"{tag}_wq_{h}", [P, ND, Q_RANK], F32R) for h in ("hi", "lo"))
    q32 = mem(f"{tag}_q32", [P, 4, Q_RANK])
    junk = mem(f"{tag}_junk", [P, Q_RANK])
    ss, std, rstd = (mem(f"{tag}_{n}", [P, 2, NS]) for n in ("ss", "std", "rstd"))
    gcol = mem(f"{tag}_gcol", [P, NQ + NK])
    over = Memory(nc, WORK_AT, WORK_AT + 2 * NQ * S * 4)
    wk_raw = [over(f"{tag}_wk_raw{s}", [P, KVW]) for s in range(2)]
    wk_hi, wk_lo = (over(f"{tag}_wk_{h}", [P, ND, KVW], F32R) for h in ("hi", "lo"))
    k32 = over(f"{tag}_k32", [P, NS, KV_RANK])
    pos_i, pos = over(f"{tag}_pos_i", [P, NS], I32), over(f"{tag}_pos", [P, NS])
    freq, gq, gk = over(f"{tag}_freq", [P, H]), over(f"{tag}_gq", [P, ROPE]), over(f"{tag}_gk", [P, ROPE])
    ang, full, a, b, c, cos, sin = (over(f"{tag}_{n}", [P, NS, H]) for n in ("ang", "full", "a", "b", "c", "cos", "sin"))
    sq, kg = over(f"{tag}_sq", [P, NS, ROPE]), over(f"{tag}_kg", [P, NS, ROPE])
    rows = w_dram.rearrange("(c p) n -> c p n", p=P)
    turns = [("k", g, c) for g in range(2) for c in range(NK)] + [("q", g, c) for g in range(2) for c in range(NQ)]
    four = lambda g: slice(4 * g, 4 * g + 4)
    with Phase(nc) as ctx:
        sem = lambda n: ctx.semaphore(f"{tag}_{n}")
        wq_in, wk_in = [sem(f"wq_in{s}") for s in range(2)], [sem(f"wk_in{s}") for s in range(2)]
        (g_in, rope_in, wk_hi_done, wk_lo_done, wq_hi_done, wq_lo_done, k_made, k_copied, q_made, q_copied, k_squared,
         q_squared, root, inverse, k_normed, q_normed, turned, hi_done, lo_done, rope_done, sines) = (
            sem(n) for n in ("g_in", "rope_in", "wk_hi_done", "wk_lo_done", "wq_hi_done", "wq_lo_done", "k_made",
                             "k_copied", "q_made", "q_copied", "k_squared", "q_squared", "root", "inverse", "k_normed",
                             "q_normed", "turned", "hi_done", "lo_done", "rope_done", "sines"))
        block = ctx.enter_context(nc.Block())
        count, angles_ready = [0], []

        @block.sync
        def _(sp):
            for s in range(2):
                sp.dma_start(wk_raw[s][:], rows[s][:, Q_RANK:]).then_inc(wk_in[s], 16)
            with nc.allow_non_contiguous_dma("gains and positions"):
                sp.dma_start(gcol[:, 0:NQ], gain_columns(q_gain)).then_inc(g_in, 16)
                sp.dma_start(gcol[:, NQ:], gain_columns(kv_gain)).then_inc(g_in, 16)
                sp.dma_start(pos_i[:], positions.rearrange("b (t p) -> p (b t)", p=P)).then_inc(rope_in, 16)
            sp.dma_start(gq[:], g_q[NOPE:QK].partition_broadcast(P)).then_inc(rope_in, 16)
            sp.dma_start(gk[:], g_k[NOPE:QK].partition_broadcast(P)).then_inc(rope_in, 16)
            for c in range(2, ND):
                sp.wait_ge(wk_lo_done, c - 1)
                sp.dma_start(wk_raw[c % 2][:], rows[c][:, Q_RANK:]).then_inc(wk_in[c % 2], 16)
            for c in range(ND):
                if c >= 2:
                    sp.wait_ge(wq_lo_done, c - 1)
                sp.dma_start(wq_raw[c % 2][:], rows[c][:, 0:Q_RANK]).then_inc(wq_in[c % 2], 16)

        @block.gpsimd
        def _(pool):
            for raw, hi, lo, hi_sem, lo_sem in ((wk_raw, wk_hi, wk_lo, wk_hi_done, wk_lo_done),
                                                (wq_raw, wq_hi, wq_lo, wq_hi_done, wq_lo_done)):
                for c in range(ND):
                    pool.wait_ge(hi_sem, c + 1)
                    pool.tensor_tensor(lo[:, c, :], raw[c % 2][:], as_f32(hi[:, c, :]), ALU.subtract).then_inc(lo_sem, 1)

        @block.vector
        def _(dve):
            def then(ins):
                count[0] += 1
                ins.then_inc(rope_done, 1)
                dve.wait_ge(rope_done, count[0])

            def copy_keys(tiles):
                for t in tiles:
                    dve.wait_ge(k_made, t + 1)
                    dve.tensor_copy(k32[:, t, :], psum[4 + t % 2][:, 0:KV_RANK])
                    dve.tensor_copy(k_rope[:, t, :], psum[4 + t % 2][:, KV_RANK:KVW]).then_inc(k_copied, 1)

            def copy_queries(tiles):
                for t in tiles:
                    dve.wait_ge(q_made, t + 1)
                    if t == 4:
                        dve.wait_ge(turned, 10)
                    for h in range(2):
                        last = dve.tensor_copy(q32[:, t % 4, h * PW:(h + 1) * PW], psum[2 * (t % 2) + h][:, 0:PW])
                    last.then_inc(q_copied, 1)

            def normalise(which, tiles, n):
                dve.wait_ge(root, n)
                dve.reciprocal(rstd[:, which, tiles], std[:, which, tiles]).then_inc(inverse, 1)
                dve.wait_ge(inverse, n)
                for t in range(tiles.start, tiles.stop):
                    src = k32[:, t, :] if which else q32[:, t % 4, :]
                    dve.tensor_scalar(src, src, rstd[:, which, t:t + 1], None,
                                      ALU.mult).then_inc((q_normed, k_normed)[which], 1)

            def lower(ns):
                for n in ns:
                    what, g, c = turns[n]
                    dst, col = (cq, c) if what == "q" else (ckv, NQ + c)
                    cols = slice(g * HALF, (g + 1) * HALF)
                    dve.wait_ge(hi_done, n + 1)
                    dve.scalar_tensor_tensor(dst["lo"][:, c, cols], psum[6 + n % 2][:], gcol[:, col:col + 1],
                                             as_f32(dst["hi"][:, c, cols]), ALU.mult, ALU.subtract).then_inc(lo_done, 1)

            for i in range(H):
                last = dve.memset(freq[:, i:i + 1], float(np.float32(THETA) ** np.float32(-i / H)))
            then(last)
            dve.wait_ge(rope_in, 48)
            then(dve.tensor_copy(pos[:], pos_i[:]))
            then(dve.tensor_tensor(ang[:], wide(pos[:], NS, H), rows_of(freq[:], NS, H), ALU.mult))
            then(dve.tensor_scalar(full[:], ang[:], 1.0 / TWO_PI, ROUND, ALU.mult, ALU.add))
            then(dve.tensor_scalar(full[:], full[:], ROUND, None, ALU.subtract))
            for part in TURN:
                then(dve.scalar_tensor_tensor(ang[:], full[:], -part, ang[:], ALU.mult, ALU.add))
            then(dve.tensor_scalar(a[:], ang[:], PI_IN, -PI_IN, ALU.min, ALU.max))
            then(dve.tensor_scalar(b[:], ang[:], TWO_PI / 4, None, ALU.add))
            then(dve.tensor_scalar(c[:], b[:], TWO_PI / 2, -TWO_PI, ALU.is_gt, ALU.mult))
            then(dve.tensor_tensor(b[:], b[:], c[:], ALU.add))
            then(dve.tensor_scalar(b[:], b[:], PI_IN, -PI_IN, ALU.min, ALU.max))
            angles_ready.append(count[0])
            copy_keys(range(NS))
            dve.wait_ge(sines, 2)
            for n, (g, f) in enumerate(((0, cos), (1, sin), (1, cos), (0, sin))):
                dve.tensor_tensor(tab[n][:], f[:], rows_of(gq[:, g * H:(g + 1) * H], NS, H), ALU.mult)
            dve.wait_ge(k_copied, NS)
            then(dve.tensor_tensor(sq[:], k_rope[:], k_rope[:], ALU.mult))
            dve.tensor_reduce(k_ss[:], sq[:], AX, ALU.add)
            then(dve.tensor_tensor(kg[:], k_rope[:], rows_of(gk[:], NS, ROPE), ALU.mult))
            for first, second, op, out in ((cos, sin, ALU.subtract, 0), (sin, cos, ALU.add, H)):
                then(dve.tensor_tensor(a[:], kg[:, :, 0:H], first[:], ALU.mult))
                then(dve.tensor_tensor(b[:], kg[:, :, H:ROPE], second[:], ALU.mult))
                then(dve.tensor_tensor(k_rot[:, :, out:out + H], a[:], b[:], op))
            normalise(1, slice(0, NS), 1)
            copy_queries(range(4))
            lower(range(0, 4))
            normalise(0, four(0), 2)
            lower(range(4, 10))
            copy_queries(range(4, NS))
            normalise(0, four(1), 3)
            lower(range(10, 16))

        @block.scalar
        def _(act):
            def upper_weights(raw, hi, loaded, done):
                for c in range(ND):
                    act.wait_ge(loaded[c % 2], 16 * (c // 2 + 1))
                    act.activation(hi[:, c, :], raw[c % 2][:], ACT.Copy).then_inc(done, 1)

            def squares(which, tiles):
                copied, squared = ((q_copied, q_squared), (k_copied, k_squared))[which]
                for t in tiles:
                    act.wait_ge(copied, t + 1)
                    if t:
                        act.wait_ge(squared, t)
                    elif which == 0:
                        act.wait_ge(k_squared, NS)
                    src = k32[:, t, :] if which else q32[:, t % 4, :]
                    act.activation(junk[:, 0:src.shape[-1]], src, ACT.Square,
                                   accum_out=ss[:, which, t:t + 1]).then_inc(squared, 1)

            def deviations(which, tiles, rank):
                squared = (q_squared, k_squared)[which]
                act.wait_ge(squared, tiles.stop)
                act.activation(std[:, which, tiles], ss[:, which, tiles], ACT.Sqrt, bias=k["eps"][:, 0:1],
                               scale=1.0 / rank).then_inc(root, 1)

            def upper(ns):
                for n in ns:
                    what, g, c = turns[n]
                    dst, col = (cq, c) if what == "q" else (ckv, NQ + c)
                    act.wait_ge(turned, n + 1)
                    act.activation(dst["hi"][:, c, g * HALF:(g + 1) * HALF], psum[6 + n % 2][:], ACT.Copy,
                                   scale=gcol[:, col:col + 1]).then_inc(hi_done, 1)

            upper_weights(wk_raw, wk_hi, wk_in, wk_hi_done)
            act.wait_ge(rope_done, angles_ready[0])
            act.activation(sin[:], a[:], ACT.Sin).then_inc(sines, 1)
            act.activation(cos[:], b[:], ACT.Sin).then_inc(sines, 1)
            upper_weights(wq_raw, wq_hi, wq_in, wq_hi_done)
            squares(1, range(NS))
            deviations(1, slice(0, NS), KV_RANK)
            squares(0, range(4))
            deviations(0, four(0), Q_RANK)
            act.wait_ge(g_in, 32)
            upper(range(0, 4))
            upper(range(4, 10))
            squares(0, range(4, NS))
            deviations(0, four(1), Q_RANK)
            upper(range(10, 16))

        @block.tensor
        def _(pe):
            def project_queries(tiles):
                for t in tiles:
                    if t >= 2:
                        pe.wait_ge(q_copied, t - 1)
                    r = slice(t * P, (t + 1) * P)
                    for h in range(2):
                        cols = slice(h * PW, (h + 1) * PW)
                        for c in range(ND):
                            last = product3(pe, psum[2 * (t % 2) + h][:, 0:PW], ht["hi"][:, c, r], ht["lo"][:, c, r],
                                            wq_hi[:, c, cols], wq_lo[:, c, cols], c == 0, c == ND - 1)
                    last.then_inc(q_made, 1)

            def turn(ns):
                for n in ns:
                    what, g, c = turns[n]
                    if what == "q":
                        pe.wait_ge(q_normed, 4 * (g + 1))
                    else:
                        pe.wait_ge(k_normed, 4 * (g + 1))
                    if n >= 2:
                        pe.wait_ge(lo_done, n - 1)
                    for i in range(4):
                        src = (q32[:, i, :] if what == "q" else k32[:, 4 * g + i, :])[:, c * P:(c + 1) * P]
                        last = pe.transpose(psum[6 + n % 2][:, i * P:(i + 1) * P], src, k["ident"][:])
                    last.then_inc(turned, 1)

            pe.wait_ge(wk_lo_done, ND)
            for t in range(NS):
                if t >= 2:
                    pe.wait_ge(k_copied, t - 1)
                r = slice(t * P, (t + 1) * P)
                for c in range(ND):
                    last = product3(pe, psum[4 + t % 2][:, 0:KVW], ht["hi"][:, c, r], ht["lo"][:, c, r],
                                    wk_hi[:, c, :], wk_lo[:, c, :], c == 0, c == ND - 1)
                last.then_inc(k_made, 1)
            pe.wait_ge(wq_lo_done, ND)
            project_queries(range(0, 4))
            turn(range(0, 4))
            project_queries((4,))
            turn(range(4, 10))
            project_queries(range(5, NS))
            turn(range(10, 16))


def latent_heads(nc, tag, k, w_q_up, w_kv_up, g_q, g_k, cq, ckv, tab, k_rot, k_ss, at, psum, ot_dram):
    mem = Memory(nc, at, 229344)
    low = Memory(nc, HT_AT, CONST_AT)
    NQ, NK = Q_RANK // P, KV_RANK // P
    QW, KW = 2 * QK, 2 * (NOPE + HD)
    G = NS * 2
    H = ROPE // 2
    wq = {n: mem(f"{tag}_wq_{n}", [P, NQ, QW], F32 if n == "raw" else F32R) for n in ("raw", "hi", "lo")}
    wk = {n: mem(f"{tag}_wk_{n}", [P, NK, KW], F32 if n == "raw" else F32R) for n in ("raw", "hi", "lo")}
    q32, k32 = mem(f"{tag}_q32", [P, G, QK]), mem(f"{tag}_k32", [P, G, QK])
    junk = mem(f"{tag}_junk", [P, 2, QK + NOPE])
    ra, rb, rc, rd = (mem(f"{tag}_{n}", [P, G, H]) for n in ("ra", "rb", "rc", "rd"))
    qt = {n: mem(f"{tag}_qt_{n}", [QK, 2, S], F32R) for n in ("hi", "lo")}
    kt = {n: mem(f"{tag}_kt_{n}", [QK, 2, S], F32R) for n in ("hi", "lo")}
    ss, std, rstd = (mem(f"{tag}_{n}", [P, 2, G]) for n in ("ss", "std", "rstd"))
    gcol = mem(f"{tag}_gcol", [QK, 2])
    v32 = low(f"{tag}_v32", [P, G, HD])
    v = low(f"{tag}_v", [P, 2, NS, 2 * HD], F32R)
    q_rows, k_rows = w_q_up.rearrange("(c p) n -> p c n", p=P), w_kv_up.rearrange("(c p) n -> p c n", p=P)
    turns = [(a, h, half) for h in range(2) for half in range(2) for a in range(2)]
    PREPARE = (["project 0", "project 1", "project 2", "project 3", "sum 0", "root 0", "normalise 0", "rotate 0",
                "project 4", "project 5", "project 6", "project 7", "next weights", "sum 1", "root 1", "normalise 1",
                "rotate 1", "values 0"] + [f"turn {n}" for n in range(8)])
    extras = {0: ["values 1", "project 0"], 1: ["project 1"], 2: ["project 2"], 3: ["project 3"],
              4: ["project 4", "sum 0", "root 0"], 5: ["project 5", "normalise 0"], 6: ["project 6", "rotate 0"],
              7: ["project 7"], 8: ["next weights", "sum 1", "root 1"], 9: ["normalise 1"],
              10: ["rotate 1", "turn 0"], 11: ["used 1", "turn 1"], 12: ["turn 2"], 13: ["values 0", "turn 3"],
              14: ["turn 4"], 16: ["turn 5"], 18: ["turn 6"], 21: ["turn 7"]}
    plan = [8, 9, 10, 11, 12, 13, 13, 14, 14, 15, 15, 16, 16, 16, 17, 18, 19, 20, 20, 21, 21, 22, 22, 23, 24]
    OWN = ("values 1", "used 1")
    group = lambda n: slice(G // 2 * n, G // 2 * (n + 1))
    tiles = lambda n: slice(NS // 2 * n, NS // 2 * (n + 1))
    with Phase(nc) as ctx:
        def scores(pe, h, tile, out):
            rows, keys = slice(tile * P, (tile + 1) * P), (tile + 1) * P
            for at_key in range(0, keys, HALF):
                cols = slice(at_key, min(at_key + HALF, keys))
                product3(pe, out[:, cols], qt["hi"][:, h, rows], qt["lo"][:, h, rows],
                         kt["hi"][:, h, cols], kt["lo"][:, h, cols], True, cols.stop < keys)
            return pe.matmul(out[:, rows], k["ident_r"][:], k["causal"][:], start=False, stop=True, skip_group_check=True)

        at_ = Attend(nc, ctx, f"{tag}a", low, psum, k, [(h, half) for h in range(2) for half in range(2)],
                     lambda tile: (tile + 1) * P, lambda half: 4 * half + 4, True, scores,
                     lambda h, j: v[:, h, j, :],
                     lambda h, half, g: ot_dram[bass.ds(g * P + h * HD, HD), half * HALF:(half + 1) * HALF],
                     low, 4, psum["pair"], (6,), plan, extras)
        sem = lambda n: ctx.semaphore(f"{tag}_{n}")
        (g_in, wq_in, wk_in, wq_hi, wk_hi, wq_lo, wk_lo, made, evicted, squared, v_hi, v_split, sums, root, inverse,
         q_norm, k_norm, k_rope_done, rot_dve, rot_pool, q_rot, turned, t_hi, t_split, ones, scaled) = (
            sem(n) for n in ("g_in", "wq_in", "wk_in", "wq_hi", "wk_hi", "wq_lo", "wk_lo", "made", "evicted", "squared", "v_hi",
                             "v_split", "sums", "root", "inverse", "q_norm", "k_norm", "k_rope_done",
                             "rot_dve", "rot_pool", "q_rot", "turned", "t_hi", "t_split", "ones", "scaled"))
        block = ctx.enter_context(nc.Block())
        bank = psum[7]
        q4 = q32[:].rearrange("p (t h) d -> p t h d", h=2)
        x1, x2 = q4[:, :, :, NOPE:NOPE + H], q4[:, :, :, NOPE + H:QK]
        four = lambda tile, n: tile[:, group(n), :].rearrange("p (t h) d -> p t h d", h=2)
        table = lambda m, n: tab[m][:, tiles(n), :].unsqueeze(2).broadcast_to([P, NS // 2, 2, H])
        v_head = lambda h: v32[:].rearrange("p (t h) d -> p t h d", h=2)[:, :, h, :]

        @block.sync
        def _(sp):
            def load(g):
                sp.dma_start(wq["raw"][:], q_rows[:, :, bass.ds(g * QW, QW)]).then_inc(wq_in, 16)
                sp.dma_start(wk["raw"][:], k_rows[:, :, bass.ds(g * KW, KW)]).then_inc(wk_in, 16)

            at_.begin(sp)
            for s in (made, evicted, squared, v_split, turned, t_split):
                sp.sem_inc(s, 1)
            load(0)
            sp.wait_ge(ones, 1)
            with nc.allow_non_contiguous_dma("gains"):
                sp.dma_start(gcol[0:NOPE, 0:1], g_q[0:NOPE].unsqueeze(1)).then_inc(g_in, 16)
                sp.dma_start(gcol[0:NOPE, 1:2], g_k[0:NOPE].unsqueeze(1)).then_inc(g_in, 16)
            sp.wait_ge(wq_lo, 1)
            sp.wait_ge(wk_lo, 1)
            load(1)
            with sp.Fori(0, PAIRS - 2) as g:
                sp.wait_ge(wq_lo, g + 2)
                sp.wait_ge(wk_lo, g + 2)
                load(g + 2)
                at_.sync(sp, g)
            sp.wait_ge(wq_lo, PAIRS)
            sp.wait_ge(wk_lo, PAIRS)
            load(PAIRS - 1)
            for g in range(PAIRS - 2, PAIRS):
                at_.sync(sp, g)
            at_.finish(sp, PAIRS)

        @block.gpsimd
        def _(pool):
            def lower_values(h, n):
                pool.wait_ge(v_hi, n + 1)
                pool.tensor_tensor(v[:, h, :, HD:], v_head(h), as_f32(v[:, h, :, 0:HD]), ALU.subtract).then_inc(v_split, 1)

            def lower_weights(g):
                for w, hi, lo in ((wq, wq_hi, wq_lo), (wk, wk_hi, wk_lo)):
                    pool.wait_ge(hi, g + 1)
                    pool.tensor_tensor(w["lo"][:], w["raw"][:], as_f32(w["hi"][:]), ALU.subtract).then_inc(lo, 1)

            def rotate(n, g):
                e, x1n, x2n = 2 * g + n, x1[:, tiles(n)], x2[:, tiles(n)]
                pool.wait_ge(inverse, e + 1)
                pool.tensor_tensor(k32[:, group(n), NOPE:QK].rearrange("p (t h) d -> p t h d", h=2),
                                   k_rot[:, tiles(n), :].unsqueeze(2).broadcast_to([P, NS // 2, 2, ROPE]),
                                   rstd[:, 1, group(n)].rearrange("p (t h) -> p t h", h=2).unsqueeze(3).broadcast_to([P, NS // 2, 2, ROPE]),
                                   ALU.mult).then_inc(k_rope_done, 1)
                pool.wait_ge(q_norm, e + 1)
                pool.tensor_tensor(four(rc, n), x2n, table(2, n), ALU.mult).then_inc(rot_pool, 1)
                pool.tensor_tensor(four(rd, n), x1n, table(3, n), ALU.mult).then_inc(rot_pool, 1)
                pool.wait_ge(rot_pool, 2 * e + 2)
                pool.wait_ge(rot_dve, 2 * e + 2)
                pool.tensor_tensor(x2n, four(rc, n), four(rd, n), ALU.add).then_inc(q_rot, 1)

            def prepare(g):
                rotate(0, g)
                lower_weights(g + 1)
                rotate(1, g)
                lower_values(0, 2 * g)

            lower_weights(0)
            prepare(0)
            with pool.Fori(0, PAIRS - 1) as g:
                lower_values(1, 2 * g + 1)
                prepare(g + 1)
            lower_values(1, 2 * PAIRS - 1)

        @block.scalar
        def _(act):
            def upper_weights(g):
                act.wait_ge(made, 1 + NS * g)
                act.wait_ge(wq_in, 16 * (g + 1))
                act.activation(wq["hi"][:], wq["raw"][:], ACT.Copy).then_inc(wq_hi, 1)
                act.wait_ge(wk_in, 16 * (g + 1))
                act.activation(wk["hi"][:], wk["raw"][:], ACT.Copy).then_inc(wk_hi, 1)

            def prepare(act, step, g):
                what, n = step.split()[0], int(step[-1]) if step[-1].isdigit() else 0
                if what == "next":
                    upper_weights(g + 1)
                elif what == "project":
                    act.wait_ge(made, 1 + NS * g + n + 1)
                    if n == 0:
                        act.wait_ge(turned, 1 + 8 * g)
                        act.wait_ge(v_split, 1 + 2 * g)
                    kv = bank[:, QW:QW + KW].rearrange("p (g d) -> p g d", d=NOPE + HD)
                    two = slice(2 * n, 2 * n + 2)
                    act.activation(q32[:, two, :], bank[:, 0:QW].rearrange("p (g d) -> p g d", d=QK), ACT.Copy)
                    act.activation(k32[:, two, 0:NOPE], kv[:, :, 0:NOPE], ACT.Copy)
                    act.activation(v32[:, two, :], kv[:, :, NOPE:], ACT.Copy).then_inc(evicted, 1)
                    act.wait_ge(evicted, 1 + NS * g + n + 1)
                    act.wait_ge(squared, 1 + NS * g + n)
                    for h in range(2):
                        one = slice(2 * n + h, 2 * n + h + 1)
                        act.activation(junk[:, h, 0:QK], q32[:, 2 * n + h, :], ACT.Square, accum_out=ss[:, 0, one])
                        last = act.activation(junk[:, h, QK:], k32[:, 2 * n + h, 0:NOPE], ACT.Square, accum_out=ss[:, 1, one])
                    last.then_inc(squared, 1)
                elif what == "root":
                    act.wait_ge(sums, 2 * g + n + 1)
                    act.activation(std[:, :, group(n)], ss[:, :, group(n)], ACT.Sqrt, bias=k["eps"][:, 0:1],
                                   scale=1.0 / QK).then_inc(root, 1)
                elif what == "values":
                    act.activation(v[:, 0, :, 0:HD], v_head(0), ACT.Copy).then_inc(v_hi, 1)
                elif what == "turn":
                    a, h, half = turns[n]
                    act.wait_ge(turned, 1 + 8 * g + n + 1)
                    act.activation((qt, kt)[a]["hi"][:, h, half * HALF:(half + 1) * HALF], bank[0:QK, :], ACT.Copy,
                                   scale=gcol[:, a:a + 1]).then_inc(t_hi, 1)

            def own(act, step, g):
                if step == "values 1":
                    act.wait_ge(at_.pv_made, 1 + g * at_.nt)
                    act.activation(v[:, 1, :, 0:HD], v_head(1), ACT.Copy).then_inc(v_hi, 1)

            def extra(act, step, g):
                if step in OWN:
                    own(act, step, g)
                else:
                    prepare(act, step, g + 1)

            act.wait_ge(g_in, 32)
            act.activation(gcol[:, 0:1], gcol[:, 0:1], ACT.Copy, scale=float(QK) ** -0.5).then_inc(scaled, 1)
            act.wait_ge(scaled, 1)
            upper_weights(0)
            for step in PREPARE:
                prepare(act, step, 0)
            at_.act(act, at_.opening)
            with act.Fori(0, PAIRS - 1) as g:
                at_.act(act, at_.steps, g, extra)
            at_.act(act, at_.closing, PAIRS - 1, own)

        @block.vector
        def _(dve):
            def prepare(dve, step, g):
                what, n = step.split()[0], int(step[-1]) if step[-1].isdigit() else 0
                e = 2 * g + n
                if what == "sum":
                    dve.wait_ge(squared, 1 + NS * g + NS // 2 * (n + 1))
                    ks = ss[:, 1, group(n)].rearrange("p (t h) -> p t h", h=2)
                    dve.tensor_tensor(ks, ks, k_ss[:, tiles(n)].unsqueeze(2).broadcast_to([P, NS // 2, 2]),
                                      ALU.add).then_inc(sums, 1)
                elif what == "normalise":
                    dve.wait_ge(root, e + 1)
                    dve.reciprocal(rstd[:, :, group(n)], std[:, :, group(n)]).then_inc(inverse, 1)
                    dve.wait_ge(inverse, e + 1)
                    dve.tensor_tensor(q32[:, group(n), :], q32[:, group(n), :], wide(rstd[:, 0, group(n)], G // 2, QK),
                                      ALU.mult).then_inc(q_norm, 1)
                    dve.tensor_tensor(k32[:, group(n), 0:NOPE], k32[:, group(n), 0:NOPE],
                                      wide(rstd[:, 1, group(n)], G // 2, NOPE), ALU.mult).then_inc(k_norm, 1)
                elif what == "rotate":
                    x1n, x2n = x1[:, tiles(n)], x2[:, tiles(n)]
                    dve.wait_ge(q_norm, e + 1)
                    dve.tensor_tensor(four(ra, n), x1n, table(0, n), ALU.mult).then_inc(rot_dve, 1)
                    dve.tensor_tensor(four(rb, n), x2n, table(1, n), ALU.mult).then_inc(rot_dve, 1)
                    dve.wait_ge(rot_dve, 2 * e + 2)
                    dve.wait_ge(rot_pool, 2 * e + 2)
                    dve.tensor_tensor(x1n, four(ra, n), four(rb, n), ALU.subtract).then_inc(q_rot, 1)
                elif what == "turn":
                    a, h, half = turns[n]
                    dve.wait_ge(t_hi, 8 * g + n + 1)
                    cols, t = slice(half * HALF, (half + 1) * HALF), (qt, kt)[a]
                    dve.scalar_tensor_tensor(t["lo"][:, h, cols], bank[0:QK, :], gcol[:, a:a + 1],
                                             as_f32(t["hi"][:, h, cols]), ALU.mult, ALU.subtract).then_inc(t_split, 1)

            dve.memset(gcol[:], 1.0).then_inc(ones, 1)
            for step in PREPARE:
                prepare(dve, step, 0)
            at_.dve(dve, at_.opening)
            with dve.Fori(0, PAIRS - 1) as g:
                at_.dve(dve, at_.steps, g, lambda dve, step, g: step not in OWN and prepare(dve, step, g + 1))
            at_.dve(dve, at_.closing, PAIRS - 1)

        @block.tensor
        def _(pe):
            def prepare(pe, step, g):
                what, n = step.split()[0], int(step[-1]) if step[-1].isdigit() else 0
                if what == "project":
                    if n == 0:
                        pe.wait_ge(wq_lo, g + 1)
                        pe.wait_ge(wk_lo, g + 1)
                        pe.wait_ge(t_split, 1 + 8 * g)
                    pe.wait_ge(evicted, 1 + NS * g + n)
                    rows = slice(n * P, (n + 1) * P)
                    for c in range(NQ):
                        product3(pe, bank[:, 0:QW], cq["hi"][:, c, rows], cq["lo"][:, c, rows],
                                 wq["hi"][:, c, :], wq["lo"][:, c, :], c == 0, c == NQ - 1)
                    for c in range(NK):
                        last = product3(pe, bank[:, QW:QW + KW], ckv["hi"][:, c, rows], ckv["lo"][:, c, rows],
                                        wk["hi"][:, c, :], wk["lo"][:, c, :], c == 0, c == NK - 1)
                    last.then_inc(made, 1)
                elif what == "turn":
                    a, h, half = turns[n]
                    if n == 0:
                        pe.wait_ge(evicted, 1 + NS * (g + 1))
                    else:
                        pe.wait_ge(t_split, 1 + 8 * g + n)
                    if n in (0, 2):
                        e = 2 * g + n // 2
                        pe.wait_ge(q_rot, 2 * e + 2)
                        pe.wait_ge(k_norm, e + 1)
                        pe.wait_ge(k_rope_done, e + 1)
                    src = (q32, k32)[a]
                    for i in range(4):
                        last = pe.transpose(bank[0:QK, i * P:(i + 1) * P], src[:, 2 * (4 * half + i) + h, :], k["ident"][:])
                    last.then_inc(turned, 1)

            def own(pe, step, g):
                if step == "used 1":
                    pe.wait_ge(v_split, 1 + 2 * g + 2)

            def extra(pe, step, g):
                if step in OWN:
                    own(pe, step, g)
                else:
                    prepare(pe, step, g + 1)

            for step in PREPARE:
                prepare(pe, step, 0)
            pe.wait_ge(t_split, 1 + 4)
            at_.pe(pe, at_.opening)
            with pe.Fori(0, PAIRS - 1) as g:
                pe.wait_ge(t_split, 1 + 8 * g + 8)
                pe.wait_ge(v_split, 1 + 2 * g + 1)
                at_.pe(pe, at_.steps, g, extra)
            pe.wait_ge(t_split, 1 + 8 * PAIRS)
            pe.wait_ge(v_split, 1 + 2 * (PAIRS - 1) + 1)
            at_.pe(pe, at_.closing, PAIRS - 1, own)


def build(nc, a, out):
    with ExitStack() as ctx:
        banks = ctx.enter_context(nc.psum_tensor("banks", [P, 8, HALF], F32))
        psum = {b: banks[:, b, :] for b in range(8)}
        psum["pair"] = [banks[:, 2 * i:2 * i + 2, :].rearrange("p a b -> p (a b)") for i in range(2)]
        x_mid = nc.dram_tensor("x_mid", (S, D), F32, kind="Internal").ap()
        ot_dram = nc.dram_tensor("attention_out_t", (D, S), F32, kind="Internal").ap()

        k, mem = {}, Memory(nc, CONST_AT, WORK_AT)
        for n, dt in (("ident", F32), ("ident_r", F32R), ("strict", F32R), ("causal", F32R), ("upper", F32R), ("lower", F32R)):
            k[n] = mem(n, [P, P], dt)
        k["eps"] = mem("eps", [P, 1])
        mem = Memory(nc, WORK_AT, X_AT)
        for n in ("strict", "causal", "upper", "lower"):
            k["tmp_" + n] = mem("tmp_" + n, [P, P])
        make_constants(nc, k)
        mem = Memory(nc, HT_AT, CONST_AT)
        ht = {h: mem(f"ht_{h}", [P, ND, S], F32R) for h in ("hi", "lo")}
        x = Memory(nc, X_AT, 229344)("x", [P, NS, D])

        for layer in range(DEPTH):
            tag = f"l{layer}"
            x_dram = a["x"].rearrange("b s d -> (b s) d") if layer == 0 else x_mid
            w_in = (a["sb_w_in"] if layer == 0 else a["mla_w_in"])[0]
            q_mem_at = w_in.shape[1] - MEM_Q
            memory_heads(nc, f"{tag}m", k, x, x_dram if layer == 0 else None, a["ln_attn"][layer], a["mem"][0], a["ln_mem"][layer], a["w_mem_kv"][layer], a["g_qn_mem"][layer],
                         a["g_kn_mem"][layer], w_in[:, q_mem_at:], ht, psum, ot_dram)
            if layer == 0:
                stick_breaking(nc, f"{tag}s", k, w_in, ht, psum, ot_dram)
            else:
                mem = Memory(nc, WORK_AT, 229344)
                cq = {h: mem(f"cq_{h}", [P, Q_RANK // P, S], F32R) for h in ("hi", "lo")}
                ckv = {h: mem(f"ckv_{h}", [P, KV_RANK // P, S], F32R) for h in ("hi", "lo")}
                k_rope, k_rot = mem("k_rope", [P, NS, ROPE]), mem("k_rot", [P, NS, ROPE])
                tab = [mem(f"rope_tab{n}", [P, NS, ROPE // 2]) for n in range(4)]
                k_ss = mem("k_ss", [P, NS])
                latent_inputs(nc, f"{tag}i", k, w_in[:, 0:q_mem_at], a["mla_q_norm"][0], a["mla_kv_norm"][0],
                              a["positions"], a["mla_g_qn"][0], a["mla_g_kn"][0], ht, cq, ckv, k_rope, tab, k_rot,
                              k_ss, mem.at, psum)
                latent_heads(nc, f"{tag}a", k, a["mla_w_q_up"][0], a["mla_w_kv_up"][0], a["mla_g_qn"][0],
                             a["mla_g_kn"][0], cq, ckv, tab, k_rot, k_ss, mem.at, psum, ot_dram)
            project_and_swiglu(nc, f"{tag}f", k, x, x_dram, ot_dram, a["w_out"][layer], a["ln_ffn"][layer],
                               a["w_ffn_gu"][layer], a["w_ffn_down"][layer], ht, psum,
                               x_mid if layer == 0 else out.rearrange("b s d -> (b s) d"))


_INS = ["x", "mem", "positions", "ln_attn", "w_out", "ln_mem", "w_mem_kv", "g_qn_mem", "g_kn_mem", "ln_ffn", "w_ffn_gu",
        "w_ffn_down", "sb_w_in", "mla_w_in", "mla_q_norm", "mla_w_q_up", "mla_kv_norm", "mla_w_kv_up", "mla_g_qn",
        "mla_g_kn"]


def kernel(**inputs):
    import numpy as _np
    import concourse.bacc as _bacc
    from concourse import mybir as _mybir
    from concourse.bass_utils import run_bass_kernel_spmd as _run

    nc = _bacc.Bacc("TRN2", target_bir_lowering=False, num_devices=1)
    arrays, args = {}, {}
    for name in _INS:
        v = _np.ascontiguousarray(inputs[name])
        arrays[f"in_{name}_dram"] = v
        args[name] = nc.dram_tensor(f"in_{name}_dram", v.shape, _mybir.dt.from_np(v.dtype), kind="ExternalInput").ap()
    out = nc.dram_tensor("out_0_dram", (1, S, D), F32, kind="ExternalOutput").ap()
    build(nc, args, out)
    r = _run(nc, [arrays], core_ids=[0])
    return r.results[0]["out_0_dram"]
```
